# Optimizing a Trainium2 kernel written in Bass

```python
import jax
import jax.numpy as jnp
from jax import lax
import numpy as np

D_MODEL = 2048
BATCH = 1
SEQ = 128
DEPTH = 1
DEC_BATCH = 1
DEC_SEQ = 256
PAST_LEN = 128

GRID_W = 64
D_MIX = D_MODEL
D_A = D_MIX // 2
D_B = D_MIX - D_A
HEAD_A = 64
H_A = D_A // HEAD_A
CHUNK = 128
H_B = 8
HEAD_B = D_B // H_B
LORA_W = 64
LORA_A = 64
N_SHIFT = 4 * D_A + 2 * LORA_W + 2 * LORA_A
P_IN = N_SHIFT + 2 * D_B
PK_HEADS = 8
D_KEY = 256
HALF_KEY = D_KEY // 2
N_KEYS = 128
N_EXPERTS = N_KEYS * N_KEYS
TOPK = 16
TOKEN_BLOCK = 128
EPS = 1e-6
GN_EPS = 64e-5

kernel_name = "hybrid_rwkv7_chunkgmlp_peer_diffusion_step"

F32 = jnp.float32

def rmsnorm(x, g):
    xf = x.astype(F32)
    y = xf * lax.rsqrt(jnp.mean(xf * xf, axis=-1, keepdims=True) + EPS)
    return (y * g.astype(F32)).astype(x.dtype)

def layernorm(x, w, b):
    xf = x.astype(F32)
    mu = jnp.mean(xf, axis=-1, keepdims=True)
    var = jnp.mean(jnp.square(xf - mu), axis=-1, keepdims=True)
    y = (xf - mu) * lax.rsqrt(var + EPS)
    return (y * w.astype(F32) + b.astype(F32)).astype(x.dtype)

def seq_shift(z):
    zp = jnp.pad(z, ((0, 0), (1, 1), (0, 0)))
    return 0.5 * (zp[:, :-2] + zp[:, 2:])

def grid_shift(z):
    b, t, ch = z.shape
    rows = t // GRID_W
    g = z.reshape(b, rows, GRID_W, ch)
    gp = jnp.pad(g, ((0, 0), (1, 1), (1, 1), (0, 0)))
    nb = 0.25 * (gp[:, :-2, 1:-1] + gp[:, 2:, 1:-1] + gp[:, 1:-1, :-2] + gp[:, 1:-1, 2:])
    return nb.reshape(b, t, ch)

def rwkv7_scan(r, w, k, v, kk, a, s0, reverse):
    def step(s, xs):
        r_t, w_t, k_t, v_t, kk_t, a_t = xs
        sa = jnp.einsum('bhvk,bhk->bhv', s, -kk_t)
        s = (s * w_t[:, :, None, :]
             + sa[..., None] * (kk_t * a_t)[:, :, None, :]
             + v_t[..., None] * k_t[:, :, None, :])
        y = jnp.einsum('bhvk,bhk->bhv', s, r_t)
        return s, y
    xs = tuple(jnp.moveaxis(u, 1, 0) for u in (r, w, k, v, kk, a))
    s_final, ys = lax.scan(step, s0.astype(F32), xs, reverse=reverse)
    return jnp.moveaxis(ys, 0, 1), s_final

def token_mix(h, shift_fn, s0_f, s0_b, p):
    b, t, _ = h.shape
    z = jnp.einsum('btd,dp->btp', h, p['w_in'])
    za, zb = z[..., :N_SHIFT], z[..., N_SHIFT:]
    za = za + p['mu_shift'] * (shift_fn(za) - za)
    r, k, v, g = (za[..., i * D_A:(i + 1) * D_A] for i in range(4))
    lw = za[..., 4 * D_A:4 * D_A + 2 * LORA_W].reshape(b, t, 2, LORA_W)
    la = za[..., 4 * D_A + 2 * LORA_W:].reshape(b, t, 2, LORA_A)
    wl = (p['w0'] + jnp.einsum('btdr,drc->btdc', jnp.tanh(lw), p['w2'])).astype(F32)
    decay = jnp.exp(-jnp.exp(-jax.nn.softplus(-wl) - 0.5))
    a = jax.nn.sigmoid((p['a0'] + jnp.einsum('btdr,drc->btdc', la, p['a2'])).astype(F32))
    kk = (k * p['k_k']).astype(F32).reshape(b, t, H_A, HEAD_A)
    kk = kk / jnp.maximum(jnp.linalg.norm(kk, axis=-1, keepdims=True), 1e-12)
    kd = k.astype(F32)[:, :, None] * (1.0 + (a - 1.0) * p['k_a'].astype(F32))
    hs = lambda u: u.reshape(u.shape[:-1] + (H_A, HEAD_A))
    rh, vh, kdh, dh, ah = hs(r.astype(F32)), hs(v.astype(F32)), hs(kd), hs(decay), hs(a)
    y_fwd, s_f = rwkv7_scan(rh, dh[:, :, 0], kdh[:, :, 0], vh, kk, ah[:, :, 0], s0_f, False)
    y_bwd, s_b = rwkv7_scan(rh, dh[:, :, 1], kdh[:, :, 1], vh, kk, ah[:, :, 1], s0_b, True)
    y = y_fwd + y_bwd
    mu = jnp.mean(y, axis=-1, keepdims=True)
    var = jnp.mean(jnp.square(y - mu), axis=-1, keepdims=True)
    yn = (y - mu) * lax.rsqrt(var + GN_EPS)
    yn = yn * hs(p['ln_x_w'].astype(F32)) + hs(p['ln_x_b'].astype(F32))
    r_k = p['r_k'].astype(F32)
    bonus = jnp.sum(jnp.sum(rh[:, :, None] * kdh * r_k, axis=-1, keepdims=True) * vh[:, :, None], axis=2)
    y_a = ((yn + bonus).reshape(b, t, D_A) * jax.nn.sigmoid(g.astype(F32))).astype(h.dtype)
    u = jax.nn.gelu(zb[..., :D_B])
    vg = layernorm(jax.nn.gelu(zb[..., D_B:]), p['ln_v_w'], p['ln_v_b'])
    vc = vg.reshape(b, t // CHUNK, CHUNK, H_B, HEAD_B)
    sp = jnp.einsum('hpq,bnqhc->bnphc', p['w_s'], vc) + p['b_s'].T[:, :, None]
    y_g = u * sp.reshape(b, t, D_B)
    o = jnp.einsum('btc,cd->btd', jnp.concatenate([y_a, y_g], axis=-1), p['w_out'])
    return o, s_f.astype(h.dtype), s_b.astype(h.dtype)

def peer(h, p):
    b, t, d = h.shape
    n = b * t
    x = h.reshape(n, d)
    q = jnp.einsum('nd,dq->nq', x, p['w_query']).reshape(n, PK_HEADS, 2, HALF_KEY)
    s1 = jnp.einsum('nhc,hkc->nhk', q[:, :, 0], p['sub_keys'][0])
    s2 = jnp.einsum('nhc,hkc->nhk', q[:, :, 1], p['sub_keys'][1])
    v1, i1 = lax.top_k(s1, TOPK)
    v2, i2 = lax.top_k(s2, TOPK)
    cand = (v1[..., :, None] + v2[..., None, :]).reshape(n, PK_HEADS, TOPK * TOPK)
    cidx = (i1[..., :, None] * N_KEYS + i2[..., None, :]).reshape(n, PK_HEADS, TOPK * TOPK)
    top_s, pos = lax.top_k(cand, TOPK)
    idx = jnp.take_along_axis(cidx, pos, axis=-1)
    gates = jax.nn.softmax(top_s.astype(F32), axis=-1).astype(h.dtype)
    eu, ev = p['expert_u'], p['expert_v']

    def block(args):
        xb, ib, gb = args
        act = jax.nn.gelu(jnp.einsum('nd,nhkd->nhk', xb, eu[ib]))
        return jnp.einsum('nhk,nhkd->nd', act * gb, ev[ib])

    nb = n // TOKEN_BLOCK
    out = lax.map(block, (x.reshape(nb, TOKEN_BLOCK, d),
                          idx.reshape(nb, TOKEN_BLOCK, PK_HEADS, TOPK),
                          gates.reshape(nb, TOKEN_BLOCK, PK_HEADS, TOPK)))
    return out.reshape(b, t, d)

def layer(x, mod, shift_fn, s0_f, s0_b, p):
    sh1, sc1, gt1, sh2, sc2, gt2 = (m[:, None, :] for m in jnp.split(mod, 6, axis=-1))
    h = rmsnorm(x, p['g_pre1']) * (1.0 + sc1) + sh1
    o, s_f, s_b = token_mix(h, shift_fn, s0_f, s0_b, p)
    x = x + gt1 * rmsnorm(o, p['g_post1'])
    h = rmsnorm(x, p['g_pre2']) * (1.0 + sc2) + sh2
    x = x + gt2 * rmsnorm(peer(h, p), p['g_post2'])
    return x, s_f, s_b

def setup_inputs(seed: int = 0) -> dict:
    key = jax.random.key(seed)
    ks = jax.random.split(key, 40)
    nrm = lambda i, shape, s: jax.random.normal(ks[i], shape, F32) * s
    D = D_MODEL
    return {
        'x_prompt': nrm(0, (BATCH, SEQ, D), 1.0),
        'x_sample': nrm(1, (DEC_BATCH, DEC_SEQ, D), 1.0),
        'c': nrm(2, (DEC_BATCH, D), 1.0),
        'state_fwd': nrm(3, (DEC_BATCH, DEPTH, H_A, HEAD_A, HEAD_A), 0.5),
        'state_bwd': nrm(4, (DEC_BATCH, DEPTH, H_A, HEAD_A, HEAD_A), 0.5),
        'c_ctx': nrm(5, (D,), 1.0),
        'w_ada': nrm(6, (DEPTH, D, 6 * D), 0.5 * D ** -0.5),
        'b_ada': nrm(7, (DEPTH, 6 * D), 0.02),
        'g_pre1': 1.0 + nrm(8, (DEPTH, D), 0.02),
        'g_post1': 1.0 + nrm(9, (DEPTH, D), 0.02),
        'g_pre2': 1.0 + nrm(10, (DEPTH, D), 0.02),
        'g_post2': 1.0 + nrm(11, (DEPTH, D), 0.02),
        'w_in': nrm(12, (DEPTH, D, P_IN), D ** -0.5),
        'mu_shift': jax.random.uniform(ks[13], (DEPTH, N_SHIFT), F32),
        'w0': nrm(14, (DEPTH, 2, D_A), 0.5),
        'w2': nrm(15, (DEPTH, 2, LORA_W, D_A), 0.1),
        'a0': nrm(16, (DEPTH, 2, D_A), 0.3),
        'a2': nrm(17, (DEPTH, 2, LORA_A, D_A), 0.5 * LORA_A ** -0.5),
        'k_k': 0.85 + nrm(18, (DEPTH, D_A), 0.05),
        'k_a': 1.0 + nrm(19, (DEPTH, D_A), 0.05),
        'r_k': nrm(20, (DEPTH, H_A, HEAD_A), 0.1),
        'ln_x_w': 1.0 + nrm(21, (DEPTH, D_A), 0.02),
        'ln_x_b': nrm(22, (DEPTH, D_A), 0.02),
        'ln_v_w': 1.0 + nrm(23, (DEPTH, D_B), 0.02),
        'ln_v_b': nrm(24, (DEPTH, D_B), 0.02),
        'w_s': nrm(25, (DEPTH, H_B, CHUNK, CHUNK), CHUNK ** -0.5),
        'b_s': 1.0 + nrm(26, (DEPTH, H_B, CHUNK), 0.02),
        'w_out': nrm(27, (DEPTH, D_MIX, D), D_MIX ** -0.5),
        'w_query': nrm(28, (DEPTH, D, PK_HEADS * D_KEY), D ** -0.5),
        'sub_keys': nrm(29, (DEPTH, 2, PK_HEADS, N_KEYS, HALF_KEY), HALF_KEY ** -0.5),
        'expert_u': nrm(30, (DEPTH, N_EXPERTS, D), D ** -0.5),
        'expert_v': nrm(31, (DEPTH, N_EXPERTS, D), D ** -0.5),
    }

def reference(x_prompt, x_sample, c, state_fwd, state_bwd, c_ctx, w_ada, b_ada, g_pre1, g_post1,
              g_pre2, g_post2, w_in, mu_shift, w0, w2, a0, a2, k_k, k_a, r_k, ln_x_w, ln_x_b,
              ln_v_w, ln_v_b, w_s, b_s, w_out, w_query, sub_keys, expert_u, expert_v):
    xp, xs = x_prompt, x_sample
    new_f, new_b = [], []
    for l in range(DEPTH):
        p = {'g_pre1': g_pre1[l], 'g_post1': g_post1[l], 'g_pre2': g_pre2[l], 'g_post2': g_post2[l],
             'w_in': w_in[l], 'mu_shift': mu_shift[l], 'w0': w0[l], 'w2': w2[l], 'a0': a0[l],
             'a2': a2[l], 'k_k': k_k[l], 'k_a': k_a[l], 'r_k': r_k[l], 'ln_x_w': ln_x_w[l],
             'ln_x_b': ln_x_b[l], 'ln_v_w': ln_v_w[l], 'ln_v_b': ln_v_b[l], 'w_s': w_s[l],
             'b_s': b_s[l], 'w_out': w_out[l], 'w_query': w_query[l], 'sub_keys': sub_keys[l],
             'expert_u': expert_u[l], 'expert_v': expert_v[l]}
        mod_ctx = (jax.nn.silu(c_ctx) @ w_ada[l] + b_ada[l])[None]
        mod_lat = jax.nn.silu(c) @ w_ada[l] + b_ada[l]
        zeros = jnp.zeros((xp.shape[0], H_A, HEAD_A, HEAD_A), xp.dtype)
        xp, s_f, s_b = layer(xp, mod_ctx, seq_shift, zeros, zeros, p)
        new_f.append(s_f)
        new_b.append(s_b)
        xs, _, _ = layer(xs, mod_lat, grid_shift, state_fwd[:, l], state_bwd[:, l], p)
    new_state_fwd = jnp.stack(new_f, axis=1)
    new_state_bwd = jnp.stack(new_b, axis=1)
    return (xp, xs, new_state_fwd, new_state_bwd)


_drawn_inputs = setup_inputs


def setup_inputs(seed=0):
    import zlib

    import numpy as np

    out = dict(_drawn_inputs(seed))
    spreads = {}
    factors = {'state_fwd': 4.32,
     'state_bwd': 3.625,
     'g_post2': 8.0,
     'ln_x_w': 3.137,
     'ln_x_b': 3.403,
     'ln_v_w': 3.161,
     'ln_v_b': 3.412,
     'b_s': 3.206}
    for name, (base, spread) in spreads.items():
        noise = np.random.default_rng([zlib.crc32(name.encode()), seed]).standard_normal(out[name].shape)
        drawn = base * np.exp(spread * noise) if base else spread * noise
        out[name] = jnp.asarray(drawn.astype(out[name].dtype))
    for name, factor in factors.items():
        out[name] = (out[name] * factor).astype(out[name].dtype)
    return out
```

```python
from contextlib import ExitStack

import numpy as np

import concourse.bass as bass
from concourse import mybir

F32 = mybir.dt.float32
F32R = mybir.dt.float32r
U32 = mybir.dt.uint32
I32 = mybir.dt.int32
ALU = mybir.AluOpType
ACT = mybir.ActivationFunctionType
AX = mybir.AxisListType

P = 128
D = 2048
KD = D // P
CTX, LAT = 128, 256
T = CTX + LAT
TILES = T // P
GRID_W = 64
GRID_H = LAT // GRID_W
DA = 1024
DB = D - DA
HEAD = 64
PAIRS = DA // P
NSHIFT = (4 * DA + 256) // P
NIN = NSHIFT + 2 * DB // P
HB = DB // P
PKH = 8
TOPK = 16
NK = 128
SLOTS = PKH * TOPK
EXP_HALF = float(np.exp(-0.5))
EPS = 1e-6
GN_EPS = 64e-5
RING = 2
CREDIT = 8
NEG = -3.0e38

Z_R, Z_K, Z_V, Z_G, Z_LW, Z_LA, Z_U, Z_VG = 0, 8, 16, 24, 32, 33, 34, 42


def _mask(f):
    p, q = np.meshgrid(np.arange(P), np.arange(P), indexing="ij")
    return f(p, q).astype(np.float32)


def constant_tables():
    t = {"ident": _mask(lambda p, q: p == q),
         "mean_d": np.full((P, P), 1.0 / D, np.float32),
         "mean_db": np.full((P, P), 1.0 / DB, np.float32),
         "head_sum": _mask(lambda p, q: p // HEAD == q // HEAD),
         "head_mean": _mask(lambda p, q: p // HEAD == q // HEAD) / HEAD,
         "iota": _mask(lambda p, q: q),
         "ones": np.ones((P, P), np.float32),
         "pick": _mask(lambda p, q: (p < 4) & (p % 2 == q))}
    for d, (lt, le) in enumerate(((lambda i, t: i < t, lambda i, t: i <= t),
                                  (lambda i, t: i > t, lambda i, t: i >= t))):
        t[f"ab{d}"] = _mask(lt)
        t[f"rb{d}"] = _mask(le)
        t[f"ak{d}"] = _mask(lt)
        t[f"rk{d}"] = _mask(le)
    for d, sign in ((0, 1), (1, -1)):
        t[f"two{d}"] = _mask(lambda i, t: (t - i == sign) & (i // 2 == t // 2))
        for b in (2, 4, 8, 16):
            t[f"half{d}_{b}"] = _mask(lambda t, i: (t // b - i // b == sign) & (i // (2 * b) == t // (2 * b)))
        t[f"off{d}"] = _mask(lambda i, t: (sign * (t - i) > 0) & (i // 32 != t // 32))
    return t


TABLE_NAMES = list(constant_tables())
NTAB = TABLE_NAMES.index("ab0")
COLS = {}
_n = 0
for _name, _w in (("b_ada", 96), ("g_pre1", 16), ("g_post1", 16), ("g_pre2", 16), ("g_post2", 16),
                  ("mu", NSHIFT), ("w0", 16), ("a0", 16), ("k_k", 8), ("k_a", 8), ("r_k", 8),
                  ("ln_x_w", 8), ("ln_x_b", 8), ("ln_v_w", 8), ("ln_v_b", 8)):
    COLS[_name] = (_n, _w)
    _n += _w
NCOLS = _n


class Tally:

    def __init__(self, sem, start=0):
        self.sem, self.v = sem, start


class Chain:

    def __init__(self, eng, tally, it=None, per=0):
        self.eng, self.t, self.it, self.per, self.n = eng, tally, it, per, 0

    def at(self, n):
        v = self.t.v + n
        return v if self.it is None else self.it * self.per + v

    def done(self, ins):
        ins.then_inc(self.t.sem, 1)
        self.n += 1
        return self.n

    def wait(self, n=None):
        self.eng.wait_ge(self.t.sem, self.at(self.n if n is None else n))

    def link(self, ins):
        self.done(ins)
        self.wait()

    def close(self, passes=1):
        assert self.it is None or self.n == self.per, (self.n, self.per)
        self.t.v += self.n * passes
        self.n = 0


class Signal:

    def __init__(self, tally, per):
        self.t, self.per, self.n = tally, per, 0

    def inc(self, ins):
        ins.then_inc(self.t.sem, 1)
        self.n += 1
        return self.n

    def wait(self, eng, it, n):
        assert 1 <= n <= self.per, (n, self.per)
        eng.wait_ge(self.t.sem, it * self.per + self.t.v + n)

    def close(self, passes):
        assert self.n == self.per, (self.n, self.per)
        self.t.v += self.per * passes
        self.n = 0


def build_program(nc, x_t, c_t, cols_in, tables_in, w_ada, w_in, w2a2, w_s, b_s, state_t, w_out, w_query,
                  keys_t, expert_u, expert_v, y_out, state_out, debug=None):
    ctx = ExitStack()

    def sem(name, start=0):
        return Tally(ctx.enter_context(nc.semaphore(name)), start)

    def sb(stack, name, shape, dt=F32):
        return stack.enter_context(nc.sbuf_tensor(name, shape, dt))

    with ctx:
        ps = ctx.enter_context(nc.psum_tensor("ps", [P, 8, 512], F32))
        x = sb(ctx, "x", [P, KD, T])
        cols = sb(ctx, "cols", [P, NCOLS])
        tab = sb(ctx, "tab", [P, NTAB, P])
        mod = sb(ctx, "mod", [P, 96, 2])
        rstd = sb(ctx, "rstd", [P, T])
        eps = sb(ctx, "eps", [P, 2])

        def table(name):
            n = TABLE_NAMES.index(name)
            return tab[:, n, :] if n < NTAB else scan_tab[:, n - NTAB, :]

        def scan_tables(name, n=1):
            a = TABLE_NAMES.index(name) - NTAB
            return scan_tab[:, a:a + n, :]

        def col(name, i=0, n=1):
            a, w = COLS[name]
            return cols[:, a + i:a + i + n]

        loads = sem("loads")
        raw_landed = [sem(f"raw_landed{i}") for i in range(8)]
        hi_ready = sem("hi_ready")
        lo_ready = sem("lo_ready", CREDIT)
        product_ready = sem("product_ready", CREDIT)
        bank_free = sem("bank_free", RING)
        act_chain = sem("act_chain")
        dve_chain = sem("dve_chain")
        pool_chain = sem("pool_chain")
        act_to_pe = sem("act_to_pe")
        dve_to_pe = sem("dve_to_pe")
        pe_to_act = sem("pe_to_act")
        pe_to_dve = sem("pe_to_dve")
        act_to_dve = sem("act_to_dve")
        dve_to_act = sem("dve_to_act")
        stores = sem("stores")

        z_scope = ExitStack()
        scan_tab = sb(z_scope, "scan_tab", [P, len(TABLE_NAMES) - NTAB, P])

        with nc.Block() as block:
            @block.sync
            def _(sp):
                for dst, src in ((x[:, :, :], x_t), (cols[:, :], cols_in), (tab[:, :, :], tables_in[:, 0:NTAB]),
                                 (scan_tab[:, :, :], tables_in[:, NTAB:])):
                    sp.dma_start(dst, src).then_inc(loads.sem, 16)
                sp.wait_ge(loads.sem, 64)

            @block.tensor
            def _(pe):
                pe.sem_inc(product_ready.sem, CREDIT)

            @block.vector
            def _(dve):
                dve.sem_inc(lo_ready.sem, CREDIT)
                nc.vector.memset(eps[:, 0:1], EPS)
                nc.vector.memset(eps[:, 1:2], GN_EPS)
                dve.sem_inc(bank_free.sem, RING)
        loads.v = 64

        class Stream:
            def __init__(self, per, raw, parts):
                assert per % len(raw) == 0 and per % len(parts) == 0
                self.per, self.raw, self.parts = per, raw, parts

            def load(self, sp, blocks, weights):
                with sp.Fori(0, blocks // self.per) as it:
                    for n in range(self.per):
                        u = n % len(self.raw)
                        sp.wait_ge(lo_ready.sem, it * self.per + lo_ready.v + n + 1 - len(self.raw))
                        sp.dma_start(self.raw[u], weights[bass.ds(it * self.per + n, 1)].rearrange("o p k c -> (o p) k c")
                                     ).then_inc(raw_landed[u].sem, 16)

            def high(self, act, it, n):
                u, turn = n % len(self.raw), n // len(self.raw)
                turns = self.per // len(self.raw)
                act.wait_ge(raw_landed[u].sem, it * (16 * turns) + raw_landed[u].v + 16 * (turn + 1))
                act.wait_ge(product_ready.sem,
                            it * self.per + product_ready.v + n + 1 - len(self.parts))
                nc.scalar.activation(self.parts[n % len(self.parts)][0], self.raw[u], ACT.Copy).then_inc(hi_ready.sem, 1)

            def low(self, dve, it, n):
                hi, lo = self.parts[n % len(self.parts)]
                dve.wait_ge(hi_ready.sem, it * self.per + hi_ready.v + n + 1)
                nc.vector.tensor_tensor(lo, self.raw[n % len(self.raw)], hi.bitcast(F32), ALU.subtract
                                        ).then_inc(lo_ready.sem, 1)

            def product(self, pe, it, n, bank):
                hi, lo = self.parts[n % len(self.parts)]
                pe.wait_ge(lo_ready.sem, it * self.per + lo_ready.v + n + 1)
                pe.wait_ge(bank_free.sem, it * self.per + bank_free.v + n + 1 - RING)
                for k in range(KD):
                    pe.matmul(bank, hi[:, k, :], hhi[:, k, :], start=(k == 0), stop=False)
                    pe.matmul(bank, hi[:, k, :], hlo[:, k, :], start=False, stop=False)
                    last = pe.matmul(bank, lo[:, k, :], hhi[:, k, :], start=False, stop=(k == KD - 1))
                last.then_inc(product_ready.sem, 1)

            def ahead(self, eng, blocks, split, drain):
                for n in range(RING):
                    split(0, n)
                eng_loop = eng.Fori(0, blocks // RING - 1)
                with eng_loop as it:
                    for n in range(RING):
                        drain(it, n)
                        split(it, n + RING)
                for n in range(RING):
                    drain(blocks // RING - 1, n)

            def close(self, blocks, banks=True):
                for u in range(len(self.raw)):
                    raw_landed[u].v += 16 * (blocks // len(self.raw))
                for t in (hi_ready, lo_ready, product_ready) + ((bank_free,) if banks else ()):
                    t.v += blocks

        z = sb(z_scope, "z", [P, NIN, T])
        hf = z[:, Z_U:NIN, :]
        b_scope = ExitStack()
        hhi = sb(b_scope, "hhi", [P, KD, T], F32R)
        hlo = sb(b_scope, "hlo", [P, KD, T], F32R)
        raw = sb(b_scope, "raw", [P, RING, KD, P])
        whi = sb(b_scope, "whi", [P, RING, KD, P], F32R)
        wlo = sb(b_scope, "wlo", [P, RING, KD, P], F32R)
        st = Stream(RING, [raw[:, u] for u in range(RING)], [(whi[:, u], wlo[:, u]) for u in range(RING)])

        with ExitStack() as a_scope, nc.Block() as block:
            csig = sb(a_scope, "csig", [P, KD, 2])
            csil = sb(a_scope, "csil", [P, KD, 2])
            cparts = sb(a_scope, "cparts", [P, KD, 4], F32R)
            rows = sb(a_scope, "rows", [4, 2, 512])
            NCH, KQ = 24, 4
            half_used = sem("half_used")
            rows_ready = sem("rows_ready")
            turned = sem("turned", 2)
            kq = KD // KQ
            more = z[:, 0:32, :].rearrange("p b t -> p (b t)").rearrange("p (s k c) -> p s k c", s=6, k=KD)
            hs = [h[:, :, :].rearrange("p k t -> p (k t)").rearrange("p (s k c) -> p s k c", s=3, k=KD) for h in (hhi, hlo)]
            sa = Stream(2 * KQ, [raw[:, 0], raw[:, 1]] + [more[:, u] for u in range(6)],
                        [(whi[:, u], wlo[:, u]) for u in range(2)] + [(hs[0][:, u], hs[1][:, u]) for u in range(2)])

            def w4(t):
                return t.rearrange("p k c -> p (k c)").rearrange("p (k c) -> p k c", k=kq)

            @block.sync
            def _(sp):
                sp.dma_start(csig[:, :, :], c_t).then_inc(loads.sem, 16)
                sa.load(sp, NCH * KQ, w_ada)

            @block.scalar
            def _(act):
                act.wait_ge(loads.sem, loads.v + 16)
                act.sem_inc(turned.sem, 2)
                nc.scalar.activation(csil[:, :, :], csig[:, :, :], ACT.Silu).then_inc(act_chain.sem, 1)
                act.wait_ge(act_chain.sem, act_chain.v + 1)
                nc.scalar.activation(cparts[:, :, 0:2], csil[:, :, :], ACT.Copy).then_inc(act_to_dve.sem, 1)
                for k in range(KD):
                    nc.scalar.activation(hf[:, k, :], x[:, k, :], ACT.Square).then_inc(act_to_pe.sem, 1)
                act.wait_ge(pe_to_act.sem, pe_to_act.v + 1)
                nc.scalar.activation(rstd[:, :], ps[:, 7, 0:T], ACT.Sqrt, bias=eps[:, 0:1]).then_inc(act_to_dve.sem, 1)
                with act.Fori(0, NCH // 2) as it:
                    for c in range(2):
                        for q in range(KQ):
                            sa.high(act, it, c * KQ + q)
                        act.wait_ge(product_ready.sem, it * 2 * KQ + product_ready.v + (c + 1) * KQ)
                        act.wait_ge(turned.sem, it * 2 + c + 1)
                        nc.scalar.activation(rows[:, c, :], ps[0:4, c, :], ACT.Copy).then_inc(rows_ready.sem, 1)

            @block.tensor
            def _(pe):
                for k in range(KD):
                    pe.wait_ge(act_to_pe.sem, act_to_pe.v + 1 + k)
                    last = pe.matmul(ps[:, 7, 0:T], table("mean_d"), hf[:, k, :], start=(k == 0), stop=(k == KD - 1))
                last.then_inc(pe_to_act.sem, 1)
                pe.wait_ge(dve_to_pe.sem, dve_to_pe.v + 1)
                with pe.Fori(0, NCH // 2) as it:
                    for c in range(2):
                        for q in range(KQ):
                            n = c * KQ + q
                            pe.wait_ge(lo_ready.sem, it * 2 * KQ + lo_ready.v + n + 1)
                            if q == 0:
                                pe.wait_ge(rows_ready.sem, it * 2 + c) if c else pe.wait_ge(half_used.sem, it + 1)
                            for k in range(kq):
                                pe.matmul(ps[0:4, c, :], cparts[:, q * kq + k, :], w4(sa.parts[n % 4][0])[:, k, :],
                                          start=(q == 0 and k == 0), stop=False)
                                last = pe.matmul(ps[0:4, c, :], cparts[:, q * kq + k, :], w4(sa.parts[n % 4][1])[:, k, :],
                                                 start=False, stop=(q == KQ - 1 and k == kq - 1))
                            last.then_inc(product_ready.sem, 1)
                        pe.wait_ge(rows_ready.sem, it * 2 + c + 1)
                        for j in range(4):
                            last = pe.matmul(ps[:, 6, bass.ds(it * 16 + c * 8 + 2 * j, 2)], rows[:, c, j * P:(j + 1) * P],
                                             tab[0:4, TABLE_NAMES.index("pick"), 0:2], start=True, stop=True)
                        last.then_inc(turned.sem, 1)
                        if c == 1:
                            pe.sem_inc(half_used.sem, 1)

            @block.vector
            def _(dve):
                ch = Chain(dve, dve_chain)
                dve.sem_inc(half_used.sem, 1)
                dve.wait_ge(act_to_dve.sem, act_to_dve.v + 1)
                nc.vector.tensor_tensor(cparts[:, :, 2:4], csil[:, :, :], cparts[:, :, 0:2].bitcast(F32), ALU.subtract
                                        ).then_inc(dve_to_pe.sem, 1)
                dve.wait_ge(act_to_dve.sem, act_to_dve.v + 2)
                ch.done(nc.vector.reciprocal(rstd[:, :], rstd[:, :]))
                with dve.Fori(0, NCH // 2) as it:
                    for n in range(2 * KQ):
                        sa.low(dve, it, n)
                dve.wait_ge(turned.sem, 2 + NCH)
                ch.link(nc.vector.tensor_tensor(
                    mod[:, :, :], ps[:, 6, 0:2 * 96].rearrange("p (j s) -> p j s", s=2),
                    col("b_ada", 0, 96).rearrange("p (j o) -> p j o", o=1).to_broadcast([P, 96, 2]), ALU.add))
                for first, gain in ((16, "g_pre1"), (64, "g_pre2")):
                    m = mod[:, first:first + 16, :]
                    g = col(gain, 0, 16).rearrange("p (j o) -> p j o", o=1).to_broadcast([P, 16, 2])
                    ch.link(nc.vector.tensor_scalar(m, m, 1.0, None, ALU.add))
                    ch.link(nc.vector.tensor_tensor(m, m, g, ALU.mult))
                for first, gain in ((32, "g_post1"), (80, "g_post2")):
                    m = mod[:, first:first + 16, :]
                    g = col(gain, 0, 16).rearrange("p (j o) -> p j o", o=1).to_broadcast([P, 16, 2])
                    ch.link(nc.vector.tensor_tensor(m, m, g, ALU.mult))
                ch.close()
            loads.v += 16
            sa.close(NCH * KQ, banks=False)
            act_chain.v += 1
            act_to_pe.v += KD
            dve_to_pe.v += 1
            pe_to_act.v += 1
            act_to_dve.v += 2

        def modulate(src_block, dst, shift_at, scale_at):
            with nc.Block() as block:
                @block.vector
                def _(dve):
                    for k in range(KD):
                        nc.vector.tensor_tensor(dst[:, k, :], src_block[:, k, :], rstd[:, :], ALU.mult
                                                ).then_inc(dve_to_act.sem, 1)
                        if k >= 1:
                            dve.wait_ge(act_to_dve.sem, act_to_dve.v + k)
                            nc.vector.tensor_tensor(hlo[:, k - 1, :], dst[:, k - 1, :], hhi[:, k - 1, :].bitcast(F32),
                                                    ALU.subtract).then_inc(dve_chain.sem, 1)
                    dve.wait_ge(act_to_dve.sem, act_to_dve.v + KD)
                    nc.vector.tensor_tensor(hlo[:, KD - 1, :], dst[:, KD - 1, :], hhi[:, KD - 1, :].bitcast(F32),
                                            ALU.subtract).then_inc(dve_chain.sem, 1)

                @block.scalar
                def _(act):
                    ch = Chain(act, act_chain)
                    for k in range(KD):
                        act.wait_ge(dve_to_act.sem, dve_to_act.v + k + 1)
                        for s, (a, b) in enumerate(((0, CTX), (CTX, T))):
                            n = ch.done(nc.scalar.activation(dst[:, k, a:b], dst[:, k, a:b], ACT.Identity,
                                                             bias=mod[:, shift_at + k, s:s + 1],
                                                             scale=mod[:, scale_at + k, s:s + 1]))
                        ch.wait(n)
                        nc.scalar.activation(hhi[:, k, :], dst[:, k, :], ACT.Copy).then_inc(act_to_dve.sem, 1)
                    ch.close()
            dve_chain.v += KD
            dve_to_act.v += KD
            act_to_dve.v += KD

        modulate(x, hf, 0, 16)

        with ExitStack() as s_scope, nc.Block() as block:
            row = sb(s_scope, "row", [P, RING, CTX + 2])
            grid = sb(s_scope, "grid", [P, RING, GRID_H + 2, GRID_W + 2])
            near = sb(s_scope, "near", [P, T])
            near2 = sb(s_scope, "near2", [P, LAT])
            mu1 = sb(s_scope, "mu1", [P, 3, NSHIFT])
            z_padded = sem("z_padded")
            borders = sem("borders")
            shifted = sem("shifted", RING)
            g3 = near2[:, :].rearrange("p (h w) -> p h w", w=GRID_W)
            n3 = near[:, CTX:T].rearrange("p (h w) -> p h w", w=GRID_W)

            @block.sync
            def _(sp):
                st.load(sp, NSHIFT, w_in)

            @block.tensor
            def _(pe):
                with pe.Fori(0, NSHIFT // RING) as it:
                    for u in range(RING):
                        st.product(pe, it, u, ps[:, u, 0:T])

            @block.gpsimd
            def _(pool):
                nc.gpsimd.memset(row[:, :, :], 0.0).then_inc(borders.sem, 1)
                nc.gpsimd.memset(grid[:, :, :, :], 0.0).then_inc(borders.sem, 1)

            @block.scalar
            def _(act):
                act.wait_ge(borders.sem, 3)
                act.sem_inc(shifted.sem, RING)

                def drain(it, u):
                    j = it * RING + u
                    act.wait_ge(product_ready.sem, it * RING + product_ready.v + u + 1)
                    act.wait_ge(shifted.sem, it * RING + u + 1)
                    nc.scalar.activation(z[:, bass.ds(j, 1), :].rearrange("p o t -> p (o t)"), ps[:, u, 0:T],
                                         ACT.Copy, scale=mu1[:, 0, bass.ds(j, 1)])
                    nc.scalar.activation(row[:, u, 1:CTX + 1], ps[:, u, 0:CTX], ACT.Copy)
                    nc.scalar.activation(grid[:, u, 1:GRID_H + 1, 1:GRID_W + 1],
                                         ps[:, u, CTX:T].rearrange("p (h w) -> p h w", w=GRID_W),
                                         ACT.Copy).then_inc(bank_free.sem, 1)

                st.ahead(act, NSHIFT, lambda it, n: st.high(act, it, n), drain)

            @block.vector
            def _(dve):
                ch = Chain(dve, dve_chain)
                nc.vector.tensor_scalar(mu1[:, 1, :], col("mu", 0, NSHIFT), 0.5, None, ALU.mult)
                nc.vector.tensor_scalar(mu1[:, 2, :], col("mu", 0, NSHIFT), 0.25, None, ALU.mult)
                ch.link(nc.vector.tensor_scalar(mu1[:, 0, :], col("mu", 0, NSHIFT), -1.0, 1.0, ALU.mult, ALU.add))
                dve.sem_inc(borders.sem, 1)
                ch.close()
                def drain(it, u):
                    ch = Chain(dve, dve_chain, it, 4 * RING)
                    ch.n = 4 * u
                    j = it * RING + u
                    dve.wait_ge(bank_free.sem, it * RING + bank_free.v + u + 1)
                    dve.wait_ge(shifted.sem, it * RING + u + RING)
                    gr = grid[:, u]
                    ch.done(nc.vector.tensor_tensor(near[:, 0:CTX], row[:, u, 0:CTX], row[:, u, 2:CTX + 2], ALU.add))
                    ch.done(nc.vector.tensor_tensor(n3, gr[:, 0:GRID_H, 1:GRID_W + 1], gr[:, 2:GRID_H + 2, 1:GRID_W + 1], ALU.add))
                    b = ch.done(nc.vector.tensor_tensor(g3, gr[:, 1:GRID_H + 1, 0:GRID_W], gr[:, 1:GRID_H + 1, 2:GRID_W + 2], ALU.add))
                    ch.wait(b)
                    ch.done(nc.vector.tensor_tensor(near[:, CTX:T], near[:, CTX:T], near2[:, :], ALU.add))
                    zc = z[:, bass.ds(j, 1), 0:CTX].rearrange("p o t -> p (o t)")
                    zl = z[:, bass.ds(j, 1), CTX:T].rearrange("p o t -> p (o t)")
                    nc.vector.scalar_tensor_tensor(out=zc, in0=near[:, 0:CTX], scalar=mu1[:, 1, bass.ds(j, 1)], in1=zc,
                                                   op0=ALU.mult, op1=ALU.add)
                    ch.wait()
                    nc.vector.scalar_tensor_tensor(out=zl, in0=near[:, CTX:T], scalar=mu1[:, 2, bass.ds(j, 1)], in1=zl,
                                                   op0=ALU.mult, op1=ALU.add).then_inc(shifted.sem, 1)

                st.ahead(dve, NSHIFT, lambda it, n: st.low(dve, it, n), drain)
            dve_chain.v += 4 * NSHIFT
            st.close(NSHIFT)

        with nc.Block() as block:
            NB = NIN - NSHIFT

            @block.sync
            def _(sp):
                st.load(sp, NB, w_in[NSHIFT:NIN])

            @block.tensor
            def _(pe):
                with pe.Fori(0, NB // RING) as it:
                    for u in range(RING):
                        st.product(pe, it, u, ps[:, u, 0:T])

            @block.scalar
            def _(act):
                def drain(it, u):
                    act.wait_ge(product_ready.sem, it * RING + product_ready.v + u + 1)
                    nc.scalar.activation(z[:, bass.ds(it * RING + u + Z_U, 1), :].rearrange("p o t -> p (o t)"),
                                         ps[:, u, 0:T], ACT.Gelu_apprx_tanh).then_inc(bank_free.sem, 1)

                st.ahead(act, NB, lambda it, n: st.high(act, it, n), drain)

            @block.vector
            def _(dve):
                st.ahead(dve, NB, lambda it, n: st.low(dve, it, n), lambda it, n: None)
            st.close(NB)
        b_scope.close()

        g_scope = ExitStack()
        wide = sb(g_scope, "wide", [P, HB, T])
        with ExitStack() as c_scope, nc.Block() as block:
            wsp = sb(c_scope, "wsp", [P, HB, P])
            bsp = sb(c_scope, "bsp", [P, HB, P])
            mean = sb(c_scope, "mean", [P, T])
            vn = sb(c_scope, "vn", [P, RING, T])
            vt = sb(c_scope, "vt", [P, RING, T])
            spb = sb(c_scope, "spb", [P, RING, T])
            vz = z[:, Z_VG:Z_VG + HB, :]
            vn_ready, vn_turned, vt_ready = sem("vn_ready"), sem("vn_turned", RING), sem("vt_ready")
            mixed, gated = sem("mixed", RING), sem("gated", RING)

            def over_heads(t):
                return t.rearrange("p (o t) -> p o t", o=1).to_broadcast([P, HB, T])

            @block.sync
            def _(sp):
                sp.dma_start(wsp[:, :, :], w_s).then_inc(loads.sem, 16)
                sp.dma_start(bsp[:, :, :], b_s.to_broadcast([P, HB, P])).then_inc(loads.sem, 16)

            @block.tensor
            def _(pe):
                pe.sem_inc(vn_turned.sem, RING)
                pe.sem_inc(mixed.sem, RING)
                for j in range(HB):
                    last = pe.matmul(ps[:, 0, 0:T], table("mean_db"), vz[:, j, :], start=(j == 0), stop=(j == HB - 1))
                last.then_inc(pe_to_dve.sem, 1)
                pe.wait_ge(act_to_pe.sem, act_to_pe.v + 1)
                for j in range(HB):
                    last = pe.matmul(ps[:, 1, 0:T], table("mean_db"), wide[:, j, :], start=(j == 0), stop=(j == HB - 1))
                last.then_inc(pe_to_act.sem, 1)
                pe.wait_ge(loads.sem, loads.v + 32)
                with pe.Fori(0, HB // RING) as it:
                    for u in range(RING):
                        pe.wait_ge(vn_ready.sem, it * RING + u + 1)
                        pe.wait_ge(vt_ready.sem, it * RING + u + 1)
                        for c in range(TILES):
                            last = pe.transpose(ps[:, 2 + u, c * P:(c + 1) * P], vn[:, u, c * P:(c + 1) * P], table("ident"))
                        last.then_inc(vn_turned.sem, 1)
                    for u in range(RING):
                        pe.wait_ge(vt_ready.sem, it * RING + RING + u + 1)
                        pe.wait_ge(gated.sem, it * RING + u + 1)
                        for c in range(TILES):
                            last = pe.matmul(ps[:, 4 + u, c * P:(c + 1) * P], vt[:, u, c * P:(c + 1) * P],
                                             wsp[:, bass.ds(it * RING + u, 1), :].rearrange("p o q -> p (o q)"),
                                             start=True, stop=True)
                        last.then_inc(mixed.sem, 1)

            @block.scalar
            def _(act):
                act.sem_inc(vt_ready.sem, RING)
                act.wait_ge(dve_to_act.sem, dve_to_act.v + 1)
                nc.scalar.activation(wide[:, :, :], vz, ACT.Square).then_inc(act_to_pe.sem, 1)
                act.wait_ge(pe_to_act.sem, pe_to_act.v + 1)
                nc.scalar.activation(rstd[:, :], ps[:, 1, 0:T], ACT.Sqrt, bias=eps[:, 0:1]).then_inc(act_to_dve.sem, 1)
                with act.Fori(0, HB // RING) as it:
                    for u in range(RING):
                        act.wait_ge(vn_turned.sem, it * RING + RING + u + 1)
                        act.wait_ge(mixed.sem, it * RING + u + 1)
                        nc.scalar.activation(vt[:, u, :], ps[:, 2 + u, 0:T], ACT.Copy).then_inc(vt_ready.sem, 1)

            @block.vector
            def _(dve):
                ch = Chain(dve, dve_chain)
                dve.sem_inc(gated.sem, RING)
                dve.wait_ge(pe_to_dve.sem, pe_to_dve.v + 1)
                ch.link(nc.vector.tensor_copy(mean[:, :], ps[:, 0, 0:T]))
                nc.vector.tensor_tensor(vz, vz, over_heads(mean[:, :]), ALU.subtract).then_inc(dve_to_act.sem, 1)
                dve.wait_ge(act_to_dve.sem, act_to_dve.v + 1)
                ch.link(nc.vector.reciprocal(rstd[:, :], rstd[:, :]))
                ch.link(nc.vector.tensor_tensor(vz, vz, over_heads(rstd[:, :]), ALU.mult))
                ch.close()
                dve.wait_ge(loads.sem, loads.v + 32)
                with dve.Fori(0, HB // RING) as it:
                    ch = Chain(dve, dve_chain, it, RING)
                    for u in range(RING):
                        j = it * RING + u
                        dve.wait_ge(vn_turned.sem, it * RING + u + 1)
                        nc.vector.tensor_scalar(vn[:, u, :], z[:, bass.ds(j + Z_VG, 1), :].rearrange("p o t -> p (o t)"),
                                                cols[:, bass.ds(j + COLS["ln_v_w"][0], 1)],
                                                cols[:, bass.ds(j + COLS["ln_v_b"][0], 1)],
                                                ALU.mult, ALU.add).then_inc(vn_ready.sem, 1)
                    for u in range(RING):
                        j = it * RING + u
                        dve.wait_ge(mixed.sem, it * RING + RING + u + 1)
                        dve.wait_ge(gated.sem, it * RING + RING + u)
                        ch.link(nc.vector.tensor_tensor(
                            spb[:, u, :].rearrange("p (c q) -> p c q", c=TILES),
                            ps[:, 4 + u, 0:T].rearrange("p (c q) -> p c q", c=TILES),
                            bsp[:, bass.ds(j, 1), :].to_broadcast([P, TILES, P]), ALU.add))
                        uz = z[:, bass.ds(j + Z_U, 1), :].rearrange("p o t -> p (o t)")
                        nc.vector.tensor_tensor(uz, uz, spb[:, u, :], ALU.mult).then_inc(gated.sem, 1)
                ch.close(HB // RING)
            loads.v += 32
            pe_to_dve.v += 1
            act_to_pe.v += 1
            pe_to_act.v += 1
            dve_to_act.v += 1
            act_to_dve.v += 1

        kk = sb(g_scope, "kk", [P, PAIRS, T])
        ka1 = sb(g_scope, "ka1", [P, PAIRS])
        with nc.Block() as block:
            kk_raw, kk_sq, kk_norm = sem("kk_raw"), sem("kk_sq"), sem("kk_norm")

            @block.vector
            def _(dve):
                ch = Chain(dve, dve_chain)
                ch.done(nc.vector.tensor_scalar(ka1[:, :], col("k_a", 0, PAIRS), -1.0, 1.0, ALU.mult, ALU.add))
                with dve.Fori(0, PAIRS) as it:
                    nc.vector.tensor_scalar(kk[:, bass.ds(it, 1), :], z[:, bass.ds(it + Z_K, 1), :],
                                            cols[:, bass.ds(it + COLS["k_k"][0], 1)], None, ALU.mult
                                            ).then_inc(kk_raw.sem, 1)
                dve.wait_ge(act_to_dve.sem, act_to_dve.v + PAIRS)
                ch.link(nc.vector.tensor_scalar(wide[:, :, :], wide[:, :, :], 1e-12, None, ALU.max))
                ch.link(nc.vector.reciprocal(wide[:, :, :], wide[:, :, :]))
                ch.link(nc.vector.tensor_tensor(kk[:, :, :], kk[:, :, :], wide[:, :, :], ALU.mult))
                ch.close()

            @block.scalar
            def _(act):
                with act.Fori(0, PAIRS) as it:
                    act.wait_ge(kk_raw.sem, it + 1)
                    nc.scalar.activation(wide[:, bass.ds(it, 1), :], kk[:, bass.ds(it, 1), :], ACT.Square).then_inc(kk_sq.sem, 1)
                with act.Fori(0, PAIRS) as it:
                    act.wait_ge(kk_norm.sem, it + 1)
                    nc.scalar.activation(wide[:, bass.ds(it, 1), :], ps[:, bass.ds(it, 1), 0:T], ACT.Sqrt
                                         ).then_inc(act_to_dve.sem, 1)
                nc.scalar.activation(z[:, Z_LW, :], z[:, Z_LW, :], ACT.Tanh)

            @block.tensor
            def _(pe):
                with pe.Fori(0, PAIRS) as it:
                    pe.wait_ge(kk_sq.sem, it + 1)
                    pe.matmul(ps[:, bass.ds(it, 1), 0:T].rearrange("p o t -> p (o t)"), table("head_sum"),
                              wide[:, bass.ds(it, 1), :].rearrange("p o t -> p (o t)"),
                              start=True, stop=True).then_inc(kk_norm.sem, 1)
            act_to_dve.v += PAIRS

        with ExitStack() as d_scope, nc.Block() as block:
            def buf(name, shape):
                return sb(d_scope, name, shape)

            GR = 4
            lora = buf("lora", [P, 2, P])
            s_in = buf("s_in", [P, 2, HEAD])
            s_new = buf("s_new", [P, 2, HEAD])
            vs = buf("vs", [P, T])
            sg = [buf(f"sg{d}", [P, T]) for d in range(2)]
            aa = [buf(f"aa{d}", [P, T]) for d in range(2)]
            cum = buf("cum", [P, T])
            cen = [buf(f"cen{d}", [P, T]) for d in range(2)]
            cex = [buf(f"cex{d}", [P, T]) for d in range(2)]
            fac = [[sg[0], cex[0], buf("fac0", [P, T])], [sg[1], cen[1], buf("fac1", [P, T])]]
            tot = [buf(f"tot{d}", [P, TILES]) for d in range(2)]
            half = [buf(f"half{d}", [P, TILES]) for d in range(2)]
            half2 = [buf(f"halftwo{d}", [P, 1]) for d in range(2)]
            kd = [buf(f"kd{d}", [P, T]) for d in range(2)]
            bq = aa
            kq = [fac[0][2], fac[1][2]]
            kr = [buf(f"kr{d}", [P, TILES, 2, P]) for d in range(2)]
            G = buf("G", [P, GR, TILES, 4, P])
            free = wide[:, :, :].rearrange("p b t -> p (b t)").rearrange("p (n g a t) -> p n g a t", n=2, g=GR, a=TILES)
            off, tn = free[:, 0], free[:, 1]
            tt = buf("tt", [P, GR, TILES, P])
            xl = buf("xl", [P, GR, TILES, P])
            vtok = buf("vtok", [P, T])
            btok = [buf(f"btok{d}", [P, 2, 2, P]) for d in range(2)]
            rs = [buf(f"rs{d}", [P, 2, 2, HEAD]) for d in range(2)]
            wv = [buf(f"wv{d}", [P, 2, 2, HEAD]) for d in range(2)]
            sa_ = [buf(f"sa{d}", [P, TILES, 2, HEAD]) for d in range(2)]
            s0 = [buf(f"s0_{d}", [P, 2, P]) for d in range(2)]
            TURN = [(0, 1, 2), (0, 2, 1)]
            heads = [slice(0, HEAD), slice(HEAD, P)]

            def signal(name, per):
                return Signal(sem(name), per)

            pass_done = sem("pass_done", 1)
            lora_landed, state_landed = sem("lora_landed"), sem("state_landed")
            v_copied, gates_in, gates = signal("v_copied", 1), signal("gates_in", 4), signal("gates", 4)
            centred, factors = signal("centred", 2), signal("factors", 2)
            operands = signal("operands", 2)
            bonus_in, bonus_sum = signal("bonus_in", 1), signal("bonus_sum", 1)
            scores, scores_masked = signal("scores", 12), signal("scores_masked", 12)
            init_ready, off_ready = signal("init_ready", GR), signal("off_ready", GR)
            turned, tn_ready = signal("tn_turned", GR), signal("tn_ready", GR)
            LEVELS = (2, 4, 8, 16)
            xs_, xm = signal("x_products", 4 * GR), signal("x_masked", 4 * GR)
            tps, tadds = signal("t_products", 3 * GR), signal("t_added", 3 * GR)
            ttps, ttadds = signal("tt_products", 4 * GR), signal("tt_added", 4 * GR)
            toks, toks_ready = signal("tokens_turned", 3), signal("tokens_ready", 3)
            starts = signal("starts", 4)
            ROUNDS = 3
            rhs_in, rhs_ready = signal("rhs_in", 4), signal("rhs_ready", 4)
            solved, solved_ready = signal("solved", 4 * (ROUNDS + 1)), signal("solved_ready", 4 * (ROUNDS + 1))
            rest, rest_ready = signal("rest", 4 * ROUNDS), signal("rest_ready", 4 * ROUNDS)
            state_sum = signal("state_sum", 2)
            state_out_ready = signal("state_out_ready", 4)
            y_sum = signal("y_sum", 1)
            every = [v_copied, gates_in, gates, centred, factors, operands, bonus_in, bonus_sum, scores,
                     scores_masked, init_ready, off_ready, turned, tn_ready, xs_, xm, tps, tadds, ttps, ttadds, toks,
                     toks_ready, starts, rhs_in, rhs_ready, solved, solved_ready, rest, rest_ready, state_sum,
                     state_out_ready, y_sum]

            def zb(first, it):
                return z[:, bass.ds(it + first, 1), :].rearrange("p o t -> p (o t)")

            def colr(name, it, more=0):
                return cols[:, bass.ds(it + (COLS[name][0] + more), 1)]

            ENGINES = 5

            def begin(eng, it):
                eng.wait_ge(pass_done.sem, it * ENGINES + 1)

            def end(eng):
                eng.drain().then_inc(pass_done.sem, 1)

            @block.sync
            def _(sp):
                sp.sem_inc(pass_done.sem, 1)
                with sp.Fori(0, PAIRS) as it:
                    begin(sp, it)
                    sp.dma_start(lora[:, :, :], w2a2[bass.ds(it, 1)].rearrange("o p a c -> (o p) a c")
                                 ).then_inc(lora_landed.sem, 16)
                    sp.dma_start(s_in[:, :, :], state_t[bass.ds(it, 1)].rearrange("o p a c -> (o p) a c")
                                 ).then_inc(state_landed.sem, 16)
                    state_out_ready.wait(sp, it, 4)
                    sp.dma_start(state_out[bass.ds(it, 1)].rearrange("o p a c -> (o p) a c"), s_new[:, :, :]
                                 ).then_inc(stores.sem, 16)
                    sp.wait_ge(stores.sem, it * 16 + stores.v + 16)
                    sp.sem_inc(pass_done.sem, 1)

            @block.gpsimd
            def _(pool):
                with pool.Fori(0, PAIRS) as it:
                    begin(pool, it)
                    v_copied.inc(nc.gpsimd.tensor_copy(vs[:, :], zb(Z_V, it)))
                    ch = Chain(pool, pool_chain, it, GR)
                    for g in range(GR):
                        d = g // 2
                        scores_masked.wait(pool, it, TILES * (g + 1))
                        a = G[:, g, :, 0, :]
                        m = scan_tables(f"two{d}").to_broadcast([P, TILES, P])
                        e = tab[:, TABLE_NAMES.index("ident"):TABLE_NAMES.index("ident") + 1, :].to_broadcast([P, TILES, P])
                        o = scan_tables(f"off{d}").to_broadcast([P, TILES, P])
                        ch.link(nc.gpsimd.tensor_tensor(tt[:, g], a, m, ALU.mult))
                        init_ready.inc(nc.gpsimd.tensor_tensor(tt[:, g], tt[:, g], e, ALU.add))
                        off_ready.inc(nc.gpsimd.tensor_tensor(off[:, g], a, o, ALU.mult))
                    ch.close(PAIRS)
                    end(pool)

            @block.scalar
            def _(act):
                with act.Fori(0, PAIRS) as it:
                    begin(act, it)
                    for d in range(2):
                        gates_in.wait(act, it, 2 * d + 1)
                        gates.inc(nc.scalar.activation(sg[d][:, :], ps[:, 2 * d, 0:T], ACT.Sigmoid,
                                                       bias=colr("w0", it, PAIRS * d)))
                        gates_in.wait(act, it, 2 * d + 2)
                        gates.inc(nc.scalar.activation(aa[d][:, :], ps[:, 2 * d + 1, 0:T], ACT.Sigmoid,
                                                       bias=colr("a0", it, PAIRS * d)))
                    nc.scalar.activation(zb(Z_G, it), zb(Z_G, it), ACT.Sigmoid)
                    K = EXP_HALF
                    for d in range(2):
                        centred.wait(act, it, d + 1)
                        srcs = ((cen[d], -K), (cex[d], -K), (cen[d], K)) if d == 0 else ((cex[d], K), (cen[d], K), (cex[d], -K))
                        for i, (src, sc) in enumerate(srcs):
                            nc.scalar.activation(fac[d][i][:, :], src[:, :], ACT.Exp, scale=sc)
                        factors.inc(nc.scalar.activation(half[d][:, :], tot[d][:, :], ACT.Exp, scale=-K))
                    toks.wait(act, it, 1)
                    toks_ready.inc(nc.scalar.activation(vtok[:, :], ps[:, 0, 0:T], ACT.Copy))
                    for d in range(2):
                        toks.wait(act, it, 2 + d)
                        toks_ready.inc(nc.scalar.activation(btok[d][:, :, :, :].rearrange("p a b c -> p (a b c)"),
                                                            ps[:, 1 + d, :], ACT.Copy))
                    for g in range(GR):
                        turned.wait(act, it, g + 1)
                        tn_ready.inc(nc.scalar.activation(tn[:, g], ps[:, 4 + g % 2, 0:T].rearrange("p (a t) -> p a t", a=TILES), ACT.Copy))
                    for turn, w in ((0, 2), (2, 1)):
                        n = 0 if turn == 0 else 1
                        for d in range(2):
                            rhs_in.wait(act, it, 2 * n + d + 1)
                            rhs_ready.inc(nc.scalar.activation(rs[d][:, 0:w], ps[:, 0 + d, 0:P * w].rearrange("p (a h v) -> p a h v", a=w, h=2), ACT.Copy))
                        for r in range(ROUNDS + 1):
                            for d in range(2):
                                solved.wait(act, it, (2 * n) * (ROUNDS + 1) + 2 * r + d + 1)
                                solved_ready.inc(nc.scalar.activation(sa_[d][:, turn:turn + w],
                                                                      ps[:, 2 + d, 0:P * w].rearrange("p (a h v) -> p a h v", a=w, h=2), ACT.Copy))
                    y_sum.wait(act, it, 1)
                    nc.scalar.activation(zb(Z_R, it), ps[:, 7, 0:T], ACT.Copy)
                    end(act)

            @block.vector
            def _(dve):
                with dve.Fori(0, PAIRS) as it:
                    begin(dve, it)
                    ch = Chain(dve, dve_chain, it, 32)
                    for d in range(2):
                        gates.wait(dve, it, 2 * d + 1)
                        for i in range(TILES):
                            c = slice(i * P, (i + 1) * P)
                            n = ch.done(nc.vector.tensor_tensor_scan(cum[:, c], table("ones"), sg[d][:, c], 0.0, ALU.mult, ALU.add))
                        ch.wait(n)
                        ch.link(nc.vector.tensor_scalar(tot[d][:, :], cum[:, P - 1:T:P], 0.5, None, ALU.mult))
                        for i in range(TILES):
                            c = slice(i * P, (i + 1) * P)
                            n = ch.done(nc.vector.tensor_scalar(cen[d][:, c], cum[:, c], tot[d][:, i:i + 1], None, ALU.subtract))
                        ch.wait(n)
                        centred.inc(nc.vector.tensor_tensor(cex[d][:, :], cen[d][:, :], sg[d][:, :], ALU.subtract))
                    for d in range(2):
                        gates.wait(dve, it, 2 * d + 2)
                        ch.link(nc.vector.tensor_scalar(kd[d][:, :], aa[d][:, :], colr("k_a", it), ka1[:, bass.ds(it, 1)], ALU.mult, ALU.add))
                        ch.link(nc.vector.tensor_tensor(kd[d][:, :], kd[d][:, :], zb(Z_K, it), ALU.mult))
                        ch.link(nc.vector.tensor_tensor(aa[d][:, :], kk[:, bass.ds(it, 1), :].rearrange("p o t -> p (o t)"),
                                                        aa[d][:, :], ALU.mult))
                        factors.wait(dve, it, d + 1)
                        ch.link(nc.vector.tensor_tensor(bq[d][:, :], aa[d][:, :], fac[d][2][:, :], ALU.mult))
                        ch.done(nc.vector.tensor_tensor(kq[d][:, :], kd[d][:, :], fac[d][2][:, :], ALU.mult))
                        ch.done(nc.vector.scalar_tensor_tensor(
                            out=kr[d][:, :, 0, :], in0=kk[:, bass.ds(it, 1), :].rearrange("p o (a t) -> p (o a) t", a=TILES),
                            scalar=-1.0, in1=fac[d][1][:, :].rearrange("p (a t) -> p a t", a=TILES), op0=ALU.mult, op1=ALU.mult))
                        operands.inc(nc.vector.tensor_tensor(
                            kr[d][:, :, 1, :], z[:, bass.ds(it, 1), :].rearrange("p o (a t) -> p (o a) t", a=TILES),
                            fac[d][0][:, :].rearrange("p (a t) -> p a t", a=TILES), ALU.mult))
                        ch.wait()
                    for n in range(12):
                        g, tile = n // TILES, n % TILES
                        scores.wait(dve, it, n + 1)
                        first = TABLE_NAMES.index(f"ab{g // 2}")
                        scores_masked.inc(nc.vector.tensor_tensor(G[:, g, tile], ps[:, 6 + n % 2, :].rearrange("p (a t) -> p a t", a=4),
                                                                  scan_tab[:, first - NTAB:first - NTAB + 4, :], ALU.mult))
                    ch.link(nc.vector.tensor_tensor(kd[0][:, :], kd[0][:, :], kd[1][:, :], ALU.add))
                    bonus_in.inc(nc.vector.scalar_tensor_tensor(out=cum[:, :], in0=kd[0][:, :], scalar=colr("r_k", it), in1=zb(Z_R, it),
                                                                op0=ALU.mult, op1=ALU.mult))
                    dve.wait_ge(state_landed.sem, it * 16 + 16)
                    for d in range(2):
                        f, l = TURN[d][1], TURN[d][2]
                        starts.inc(nc.vector.scalar_tensor_tensor(
                            out=s0[d][:, 0, :].rearrange("p (h v) -> p h v", h=2), in0=s_in[:, d:d + 1, :].to_broadcast([P, 2, HEAD]),
                            scalar=half[d][:, f:f + 1], in1=table("head_sum").rearrange("p (h v) -> p h v", h=2),
                            op0=ALU.mult, op1=ALU.mult))
                        ch.done(nc.vector.tensor_tensor(half2[d][:, :], half[d][:, f:f + 1], half[d][:, l:l + 1], ALU.mult))
                    for lv, b in enumerate(LEVELS):
                        for g in range(GR):
                            xs_.wait(dve, it, lv * GR + g + 1)
                            i = TABLE_NAMES.index(f"half{g // 2}_{b}")
                            xm.inc(nc.vector.tensor_tensor(xl[:, g], ps[:, g % 2, 0:T].rearrange("p (a t) -> p a t", a=TILES),
                                                           scan_tab[:, i - NTAB:i - NTAB + 1, :].to_broadcast([P, TILES, P]), ALU.mult))
                        for g in range(GR):
                            if lv < 3:
                                tps.wait(dve, it, lv * GR + g + 1)
                                tadds.inc(nc.vector.tensor_tensor(tn[:, g], ps[:, 2 + g % 2, 0:T].rearrange("p (a t) -> p a t", a=TILES), tn[:, g], ALU.add))
                            ttps.wait(dve, it, lv * GR + g + 1)
                            ttadds.inc(nc.vector.tensor_tensor(tt[:, g], ps[:, 4 + g % 2, 0:T].rearrange("p (a t) -> p a t", a=TILES), tt[:, g], ALU.add))
                    bonus_sum.wait(dve, it, 1)
                    ch.done(nc.vector.tensor_tensor(zb(Z_K, it), ps[:, 6, 0:T], vs[:, :], ALU.mult))
                    for turn, w in ((0, 2), (2, 1)):
                        n = 0 if turn == 0 else 1
                        for r in range(ROUNDS):
                            for d in range(2):
                                rest.wait(dve, it, 2 * n * ROUNDS + 2 * r + d + 1)
                                if r == 0:
                                    rhs_ready.wait(dve, it, 2 * n + d + 1)
                                rest_ready.inc(nc.vector.tensor_tensor(wv[d][:, 0:w], ps[:, 4 + d, 0:P * w].rearrange("p (a h v) -> p a h v", a=w, h=2),
                                                                       rs[d][:, 0:w], ALU.add))
                        if turn == 0:
                            for d in range(2):
                                f, l = TURN[d][1], TURN[d][2]
                                state_sum.wait(dve, it, d + 1)
                                for hh in range(2):
                                    state_out_ready.inc(nc.vector.tensor_scalar(
                                        s_new[heads[hh], d, :], ps[heads[hh], 6 + d, hh * HEAD:(hh + 1) * HEAD],
                                        half[d][heads[hh], 0:1], None, ALU.mult))
                                stm = wv[d][:, 0].rearrange("p h v -> p (h v)")
                                ch.link(nc.vector.tensor_tensor(stm, ps[:, 6 + d, P:2 * P], s0[d][:, 0, :], ALU.add))
                                starts.inc(nc.vector.scalar_tensor_tensor(out=s0[d][:, 1, :], in0=stm, scalar=half2[d][:, 0:1],
                                                                          in1=table("head_sum"), op0=ALU.mult, op1=ALU.mult))
                    ch.close(PAIRS)
                    end(dve)

            @block.tensor
            def _(pe):
                with pe.Fori(0, PAIRS) as it:
                    begin(pe, it)
                    pe.wait_ge(lora_landed.sem, it * 16 + 16)
                    for d in range(2):
                        r = slice(64 * d, 64 * d + 64)
                        gates_in.inc(pe.matmul(ps[:, 2 * d, 0:T], lora[r, 0, :], z[r, Z_LW, :], start=True, stop=True))
                        gates_in.inc(pe.matmul(ps[:, 2 * d + 1, 0:T], lora[r, 1, :], z[r, Z_LA, :], start=True, stop=True))
                    v_copied.wait(pe, it, 1)
                    gates.wait(pe, it, 4)
                    for i in range(TILES):
                        last = pe.transpose(ps[:, 0, i * P:(i + 1) * P], vs[:, i * P:(i + 1) * P], table("ident"))
                    toks.inc(last)
                    for n in range(12):
                        g, tile = n // TILES, n % TILES
                        d, h = g // 2, heads[g % 2]
                        c = slice(tile * P, (tile + 1) * P)
                        if n % 6 == 0:
                            operands.wait(pe, it, d + 1)
                        if n >= 2:
                            scores_masked.wait(pe, it, n - 1)
                        m = kr[d][h, tile, :, :].rearrange("p a t -> p (a t)")
                        pe.matmul(ps[:, 6 + n % 2, 0:2 * P], bq[d][h, c], m, start=True, stop=True)
                        scores.inc(pe.matmul(ps[:, 6 + n % 2, 2 * P:4 * P], kq[d][h, c], m, start=True, stop=True))
                    for d in range(2):
                        for j in range(2):
                            c = slice(TURN[d][j] * P, (TURN[d][j] + 1) * P)
                            pe.transpose(ps[:, 1 + d, 2 * j * P:(2 * j + 1) * P], bq[d][:, c], table("ident"))
                            last = pe.transpose(ps[:, 1 + d, (2 * j + 1) * P:(2 * j + 2) * P], kq[d][:, c], table("ident"))
                        toks.inc(last)
                    for g in range(GR):
                        init_ready.wait(pe, it, g + 1)
                        if g >= 2:
                            tn_ready.wait(pe, it, g - 1)
                        for i in range(TILES):
                            last = pe.transpose(ps[:, 4 + g % 2, i * P:(i + 1) * P], tt[:, g, i], table("ident"))
                        turned.inc(last)
                    bonus_in.wait(pe, it, 1)
                    scores_masked.wait(pe, it, 12)
                    bonus_sum.inc(pe.matmul(ps[:, 6, 0:T], table("head_sum"), cum[:, :], start=True, stop=True))
                    toks_ready.wait(pe, it, 3)
                    tn_ready.wait(pe, it, GR)
                    for lv, b in enumerate(LEVELS):
                        for g in range(GR):
                            if lv > 0:
                                tadds.wait(pe, it, (lv - 1) * GR + g + 1)
                            if g >= 2:
                                xm.wait(pe, it, lv * GR + g - 1)
                            for i in range(TILES):
                                last = pe.matmul(ps[:, g % 2, i * P:(i + 1) * P], G[:, g, i, 0, :], tn[:, g, i], start=True, stop=True)
                            xs_.inc(last)
                        for g in range(GR):
                            xm.wait(pe, it, lv * GR + g + 1)
                            if g >= 2:
                                ttadds.wait(pe, it, lv * GR + g - 1)
                            elif lv > 0:
                                ttadds.wait(pe, it, (lv - 1) * GR + g + 1)
                            if lv < 3:
                                if g >= 2:
                                    tadds.wait(pe, it, lv * GR + g - 1)
                                for i in range(TILES):
                                    last = pe.matmul(ps[:, 2 + g % 2, i * P:(i + 1) * P], tt[:, g, i], xl[:, g, i], start=True, stop=True)
                                tps.inc(last)
                            for i in range(TILES):
                                last = pe.matmul(ps[:, 4 + g % 2, i * P:(i + 1) * P], xl[:, g, i], tt[:, g, i], start=True, stop=True)
                            ttps.inc(last)
                    ttadds.wait(pe, it, 4 * GR)
                    off_ready.wait(pe, it, GR)
                    for turn, w in ((0, 2), (2, 1)):
                        n = 0 if turn == 0 else 1
                        for d in range(2):
                            starts.wait(pe, it, 2 * n + d + 1)
                            for j in range(w):
                                tile = TURN[d][turn + j]
                                if tile:
                                    pe.matmul(ps[:, d, j * P:(j + 1) * P], kr[d][:, tile, 0, :], s0[d][:, turn + j - 1, :],
                                              start=True, stop=False)
                                for hh in range(2):
                                    last = pe.matmul(ps[:, d, (2 * j + hh) * HEAD:(2 * j + hh + 1) * HEAD], G[:, 2 * d + hh, tile, 2, :],
                                                     vtok[:, tile * P + hh * HEAD:tile * P + (hh + 1) * HEAD],
                                                     start=(tile == 0), stop=(tile == 0 or hh == 1))
                            rhs_in.inc(last)
                        for r in range(ROUNDS + 1):
                            for d in range(2):
                                if r == 0:
                                    rhs_ready.wait(pe, it, 2 * n + d + 1)
                                else:
                                    rest_ready.wait(pe, it, 2 * n * ROUNDS + 2 * (r - 1) + d + 1)
                                src = rs[d] if r == 0 else wv[d]
                                if n or r:
                                    solved_ready.wait(pe, it, 2 * n * (ROUNDS + 1) + 2 * r + d - 1)
                                for j in range(w):
                                    for hh in range(2):
                                        last = pe.matmul(ps[:, 2 + d, (2 * j + hh) * HEAD:(2 * j + hh + 1) * HEAD],
                                                         tt[:, 2 * d + hh, TURN[d][turn + j]], src[:, j, hh, :], start=True, stop=True)
                                solved.inc(last)
                            if r < ROUNDS:
                                for d in range(2):
                                    solved_ready.wait(pe, it, 2 * n * (ROUNDS + 1) + 2 * r + d + 1)
                                    if n or r:
                                        rest_ready.wait(pe, it, 2 * n * ROUNDS + 2 * r + d - 1)
                                    for j in range(w):
                                        for hh in range(2):
                                            last = pe.matmul(ps[:, 4 + d, (2 * j + hh) * HEAD:(2 * j + hh + 1) * HEAD],
                                                             off[:, 2 * d + hh, TURN[d][turn + j]], sa_[d][:, turn + j, hh, :], start=True, stop=True)
                                    rest.inc(last)
                        solved_ready.wait(pe, it, 2 * (n + 1) * (ROUNDS + 1))
                        if turn == 0:
                            for d in range(2):
                                for j in range(2):
                                    tile = TURN[d][j]
                                    out = ps[:, 6 + d, j * P:(j + 1) * P]
                                    pe.matmul(out, btok[d][:, j, 0, :], sa_[d][:, j, :, :].rearrange("p h v -> p (h v)"), start=True, stop=False)
                                    last = pe.matmul(out, btok[d][:, j, 1, :], vtok[:, tile * P:(tile + 1) * P], start=False, stop=True)
                                state_sum.inc(last)
                    for tile in range(TILES):
                        if tile:
                            for d in range(2):
                                pe.matmul(ps[:, 7, tile * P:(tile + 1) * P], s0[d][:, TURN[d].index(tile) - 1, :], kr[d][:, tile, 1, :],
                                          start=(d == 0), stop=False)
                        for hh in range(2):
                            out = ps[heads[hh], 7, tile * P:(tile + 1) * P]
                            for d in range(2):
                                g, turn = 2 * d + hh, TURN[d].index(tile)
                                pe.matmul(out, sa_[d][:, turn, hh, :], G[:, g, tile, 1, :], start=(d == 0 and tile == 0), stop=False)
                                last = pe.matmul(out, vtok[:, tile * P + hh * HEAD:tile * P + (hh + 1) * HEAD], G[:, g, tile, 3, :],
                                                 start=False, stop=(d == 1))
                    y_sum.inc(last)
                    end(pe)
            for sg_ in every:
                sg_.close(PAIRS)
            stores.v += 16 * PAIRS

        with nc.Block() as block:
            yz, bz, gz = z[:, Z_R:Z_R + PAIRS, :], z[:, Z_K:Z_K + PAIRS, :], z[:, Z_G:Z_G + PAIRS, :]
            gn_mean, gn_dev, gn_sq, gn_var = sem("gn_mean"), sem("gn_dev"), sem("gn_sq"), sem("gn_var")

            @block.tensor
            def _(pe):
                with pe.Fori(0, PAIRS) as it:
                    pe.matmul(ps[:, bass.ds(it, 1), 0:T].rearrange("p o t -> p (o t)"), table("head_mean"),
                              z[:, bass.ds(it, 1), :].rearrange("p o t -> p (o t)"), start=True, stop=True).then_inc(gn_mean.sem, 1)
                with pe.Fori(0, PAIRS) as it:
                    pe.wait_ge(gn_sq.sem, it + 1)
                    pe.matmul(ps[:, bass.ds(it, 1), 0:T].rearrange("p o t -> p (o t)"), table("head_mean"),
                              wide[:, bass.ds(it, 1), :].rearrange("p o t -> p (o t)"), start=True, stop=True).then_inc(gn_var.sem, 1)

            @block.scalar
            def _(act):
                with act.Fori(0, PAIRS) as it:
                    act.wait_ge(gn_dev.sem, it + 1)
                    nc.scalar.activation(wide[:, bass.ds(it, 1), :], z[:, bass.ds(it, 1), :], ACT.Square).then_inc(gn_sq.sem, 1)
                with act.Fori(0, PAIRS) as it:
                    act.wait_ge(gn_var.sem, it + 1)
                    nc.scalar.activation(wide[:, bass.ds(it, 1), :], ps[:, bass.ds(it, 1), 0:T], ACT.Sqrt, bias=eps[:, 1:2]
                                         ).then_inc(act_to_dve.sem, 1)

            @block.vector
            def _(dve):
                ch = Chain(dve, dve_chain)
                with dve.Fori(0, PAIRS) as it:
                    dve.wait_ge(gn_mean.sem, it + 1)
                    yb = z[:, bass.ds(it, 1), :]
                    nc.vector.tensor_tensor(yb, yb, ps[:, bass.ds(it, 1), 0:T], ALU.subtract).then_inc(gn_dev.sem, 1)
                dve.wait_ge(act_to_dve.sem, act_to_dve.v + PAIRS)
                ch.link(nc.vector.reciprocal(wide[:, :, :], wide[:, :, :]))
                ch.link(nc.vector.tensor_tensor(yz, yz, wide[:, :, :], ALU.mult))
                ch.close()
                with dve.Fori(0, PAIRS) as it:
                    ch = Chain(dve, dve_chain, it, 1)
                    yb = z[:, bass.ds(it, 1), :]
                    ch.done(nc.vector.tensor_scalar(yb, yb, cols[:, bass.ds(it + COLS["ln_x_w"][0], 1)],
                                                    cols[:, bass.ds(it + COLS["ln_x_b"][0], 1)], ALU.mult, ALU.add))
                ch.close(PAIRS)
                ch = Chain(dve, dve_chain)
                ch.wait()
                ch.link(nc.vector.tensor_tensor(yz, yz, bz, ALU.add))
                ch.link(nc.vector.tensor_tensor(yz, yz, gz, ALU.mult))
                ch.close()
            act_to_dve.v += PAIRS
        g_scope.close()

        def dump(name, *parts):
            with nc.Block() as block:
                @block.sync
                def _(sp):
                    for a, b, src in parts:
                        sp.dma_start(debug[name][:, a:b, :], src).then_inc(stores.sem, 16)
                        sp.wait_ge(stores.sem, stores.v + 16)
                        stores.v += 16

        if debug is not None and "z" in debug:
            dump("z", (0, NIN, z[:, :, :]))
            z_scope.close()
            return
        if debug is not None and "y" in debug:
            dump("y", (0, 8, z[:, 0:8, :]), (8, 16, z[:, Z_U:Z_U + 8, :]))

        def stack_right(stack, name, shape, dt=F32):
            return stack.enter_context(nc.sbuf_tensor(name, shape, dt, side="right"))

        def square_root_of_mean(src, sq):
            with nc.Block() as block:
                @block.scalar
                def _(act):
                    for k in range(KD):
                        nc.scalar.activation(sq[:, k, :], src[:, k, :], ACT.Square).then_inc(act_to_pe.sem, 1)
                    act.wait_ge(pe_to_act.sem, pe_to_act.v + 1)
                    nc.scalar.activation(rstd[:, :], ps[:, 7, 0:T], ACT.Sqrt, bias=eps[:, 0:1]).then_inc(act_to_dve.sem, 1)

                @block.tensor
                def _(pe):
                    for k in range(KD):
                        pe.wait_ge(act_to_pe.sem, act_to_pe.v + 1 + k)
                        last = pe.matmul(ps[:, 7, 0:T], table("mean_d"), sq[:, k, :], start=(k == 0), stop=(k == KD - 1))
                    last.then_inc(pe_to_act.sem, 1)

                @block.vector
                def _(dve):
                    dve.wait_ge(act_to_dve.sem, act_to_dve.v + 1)
                    nc.vector.reciprocal(rstd[:, :], rstd[:, :])
            act_to_pe.v += KD
            pe_to_act.v += 1
            act_to_dve.v += 1

        def add_to_residual(branch, gate_at, out=None):
            with nc.Block() as block:
                @block.vector
                def _(dve):
                    ch = Chain(dve, dve_chain)
                    for k in range(KD):
                        ch.done(nc.vector.tensor_tensor(branch[:, k, :], branch[:, k, :], rstd[:, :], ALU.mult))
                    first = ch.n - KD
                    for k in range(KD):
                        ch.wait(first + k + 1)
                        for s_, (a, b) in enumerate(((0, CTX), (CTX, T))):
                            ch.done(nc.vector.scalar_tensor_tensor(out=x[:, k, a:b], in0=branch[:, k, a:b],
                                                                   scalar=mod[:, gate_at + k, s_:s_ + 1], in1=x[:, k, a:b],
                                                                   op0=ALU.mult, op1=ALU.add))
                    ch.close()
                if out is not None:
                    base = dve_chain.v - 2 * KD
                    @block.sync
                    def _(sp):
                        for k in range(0, KD, 4):
                            sp.wait_ge(dve_chain.sem, base + 2 * (k + 4))
                            sp.dma_start(out[:, k:k + 4, :], x[:, k:k + 4, :]).then_inc(stores.sem, 16)
                        sp.wait_ge(stores.sem, stores.v + 16 * (KD // 4))
                    stores.v += 16 * (KD // 4)

        h_scope = ExitStack()
        hhi = stack_right(h_scope, "hhi2", [P, KD, T], F32R)
        hlo = stack_right(h_scope, "hlo2", [P, KD, T], F32R)
        w_scope = ExitStack()
        raw = stack_right(w_scope, "raw2", [P, RING, KD, P])
        whi = stack_right(w_scope, "whi2", [P, RING, KD, P], F32R)
        wlo = stack_right(w_scope, "wlo2", [P, RING, KD, P], F32R)
        st = Stream(RING, [raw[:, u] for u in range(RING)], [(whi[:, u], wlo[:, u]) for u in range(RING)])
        mixed_out = z[:, 8:24, :]
        with nc.Block() as block:
            parts_of_y = ((hhi[:, 0:8, :], hlo[:, 0:8, :], z[:, 0:8, :]), (hhi[:, 8:16, :], hlo[:, 8:16, :], z[:, Z_U:Z_U + 8, :]))

            @block.sync
            def _(sp):
                st.load(sp, KD, w_out)

            @block.tensor
            def _(pe):
                pe.wait_ge(dve_to_pe.sem, dve_to_pe.v + 2)
                with pe.Fori(0, KD // RING) as it:
                    for u in range(RING):
                        st.product(pe, it, u, ps[:, u, 0:T])

            @block.scalar
            def _(act):
                for hi, lo, y in parts_of_y:
                    nc.scalar.activation(hi, y, ACT.Copy).then_inc(act_to_dve.sem, 1)

                def drain(it, u):
                    act.wait_ge(product_ready.sem, it * RING + product_ready.v + u + 1)
                    nc.scalar.activation(z[:, bass.ds(it * RING + u + 8, 1), :].rearrange("p o t -> p (o t)"),
                                         ps[:, u, 0:T], ACT.Copy).then_inc(bank_free.sem, 1)

                st.ahead(act, KD, lambda it, n: st.high(act, it, n), drain)

            @block.vector
            def _(dve):
                for n, (hi, lo, y) in enumerate(parts_of_y):
                    dve.wait_ge(act_to_dve.sem, act_to_dve.v + n + 1)
                    nc.vector.tensor_tensor(lo, y, hi.bitcast(F32), ALU.subtract).then_inc(dve_to_pe.sem, 1)
                st.ahead(dve, KD, lambda it, n: st.low(dve, it, n), lambda it, n: None)
            st.close(KD)
            act_to_dve.v += 2
            dve_to_pe.v += 2
        if debug is not None and "o" in debug:
            dump("o", (0, 16, mixed_out))
        square_root_of_mean(mixed_out, hf)
        add_to_residual(mixed_out, 32)
        if debug is not None and "x2" in debug:
            dump("x2", (0, 16, x[:, :, :]))
        square_root_of_mean(x, hf)
        modulate(x, hf, 48, 64)
        if debug is not None and "h2" in debug:
            dump("h2", (0, 16, hf))
        z_scope.close()

        p_scope = ExitStack()
        gates = sb(p_scope, "gates", [P, TILES, SLOTS])
        first = sb(p_scope, "first", [P, TILES, SLOTS])
        second = sb(p_scope, "second", [P, TILES, SLOTS])
        with ExitStack() as q_scope, nc.Block() as block:
            keys = sb(q_scope, "keys", [P, 2 * PKH, NK])
            qs = sb(q_scope, "qs", [P, RING, T])
            score = sb(q_scope, "score", [P, RING, TILES, NK])
            score2 = sb(q_scope, "score2", [P, RING, TILES, NK])
            best = sb(q_scope, "best", [P, 2, TILES, TOPK])
            which = sb(q_scope, "which", [P, 2, TILES, TOPK], U32)
            whichf = sb(q_scope, "whichf", [P, 2, TILES, TOPK])
            cand = sb(q_scope, "cand", [P, TILES, TOPK, TOPK])
            cand2 = sb(q_scope, "cand2", [P, TILES, TOPK * TOPK])
            top = sb(q_scope, "top", [P, TILES, TOPK])
            pos = sb(q_scope, "pos", [P, TILES, TOPK], U32)
            half_pos = sb(q_scope, "half_pos", [P, 2, TILES, TOPK], U32)
            half_posf = sb(q_scope, "half_posf", [P, 2, TILES, TOPK])
            onehot = sb(q_scope, "onehot", [P, 2, TILES * TOPK, TOPK])
            keys_sem = sem("keys_landed")
            scored, score_ready, score_used = sem("scored"), sem("score_ready"), sem("score_used")
            settled = sem("settled")
            positions, picked = sem("positions"), sem("picked")

            @block.sync
            def _(sp):
                sp.dma_start(keys[:, :, :].rearrange("p (h s) k -> p h s k", s=2), keys_t).then_inc(keys_sem.sem, 16)
                st.load(sp, 2 * PKH, w_query)

            @block.tensor
            def _(pe):
                pe.wait_ge(keys_sem.sem, 16)
                with pe.Fori(0, PKH) as it:
                    for u in range(RING):
                        st.product(pe, it, u, ps[:, u, 0:T])
                    for u in range(RING):
                        pe.wait_ge(bank_free.sem, it * RING + bank_free.v + u + 1)
                        pe.wait_ge(score_ready.sem, it * RING + u + 1)
                        for tile in range(TILES):
                            last = pe.matmul(ps[:, 4 + u, tile * P:(tile + 1) * P], qs[:, u, tile * P:(tile + 1) * P],
                                             keys[:, bass.ds(it * 2 + u, 1), :].rearrange("p o k -> p (o k)"),
                                             start=True, stop=True)
                        last.then_inc(scored.sem, 1)

            @block.scalar
            def _(act):
                act.sem_inc(score_ready.sem, RING)
                act.sem_inc(score_used.sem, 1)

                def drain(it, u):
                    act.wait_ge(product_ready.sem, it * RING + product_ready.v + u + 1)
                    nc.scalar.activation(qs[:, u, :], ps[:, u, 0:T], ACT.Copy).then_inc(bank_free.sem, 1)

                def scores(it):
                    for u in range(RING):
                        act.wait_ge(scored.sem, it * RING + u + 1)
                        act.wait_ge(score_used.sem, it + 1)
                        nc.scalar.activation(score[:, u, :, :].rearrange("p t k -> p (t k)"), ps[:, 4 + u, 0:T], ACT.Copy
                                             ).then_inc(score_ready.sem, 1)

                for n in range(RING):
                    st.high(act, 0, n)
                with act.Fori(0, PKH - 1) as it:
                    for n in range(RING):
                        drain(it, n)
                        st.high(act, it, n + RING)
                    scores(it)
                for n in range(RING):
                    drain(PKH - 1, n)
                scores(PKH - 1)

            @block.gpsimd
            def _(pool):
                with pool.Fori(0, PKH) as it:
                    for s in range(2):
                        pool.wait_ge(positions.sem, it * 2 + s + 1)
                        for tile in range(TILES):
                            part = onehot[:, s, tile * TOPK:(tile + 1) * TOPK, :]
                            nc.gpsimd.tensor_tensor(
                                part, part, whichf[:, s, tile:tile + 1, :].to_broadcast([P, TOPK, TOPK]), ALU.mult
                                ).then_inc(picked.sem, 1)

            @block.vector
            def _(dve):
                def best16(ch, srcs, spares, values, indices):
                    def settle():
                        ch.wait()
                        dve.sem_inc(settled.sem, 1)

                    n = len(srcs)
                    settle()
                    for i in range(n):
                        ch.done(nc.vector.max(values[i][:, 0:8], srcs[i]))
                    settle()
                    for i in range(n):
                        ch.done(nc.vector.max_index(indices[i][:, 0:8], values[i][:, 0:8], srcs[i]))
                    for i in range(n):
                        ch.done(nc.vector.match_replace(spares[i], values[i][:, 0:8], srcs[i], NEG))
                    settle()
                    for i in range(n):
                        ch.done(nc.vector.max(values[i][:, 8:16], spares[i]))
                    settle()
                    for i in range(n):
                        ch.done(nc.vector.max_index(indices[i][:, 8:16], values[i][:, 8:16], spares[i]))
                    ch.wait()

                def choose(it, ch):
                    dve.wait_ge(score_ready.sem, it * RING + 2 * RING)
                    dve.sem_inc(settled.sem, 1)
                    seg = [(u, tile) for u in range(2) for tile in range(TILES)]
                    best16(ch, [score[:, u, t_, :] for u, t_ in seg], [score2[:, u, t_, :] for u, t_ in seg],
                           [best[:, u, t_, :] for u, t_ in seg], [which[:, u, t_, :] for u, t_ in seg])
                    dve.sem_inc(score_used.sem, 1)
                    ch.done(nc.vector.tensor_copy(whichf[:, :, :, :], which[:, :, :, :]))
                    for tile in range(TILES):
                        ch.done(nc.vector.tensor_tensor(
                            cand[:, tile], best[:, 0, tile, :].rearrange("p (a o) -> p a o", o=1).to_broadcast([P, TOPK, TOPK]),
                            best[:, 1, tile:tile + 1, :].to_broadcast([P, TOPK, TOPK]), ALU.add))
                    ch.wait()
                    best16(ch, [cand[:, t_].rearrange("p a b -> p (a b)") for t_ in range(TILES)],
                           [cand2[:, t_, :] for t_ in range(TILES)], [top[:, t_, :] for t_ in range(TILES)],
                           [pos[:, t_, :] for t_ in range(TILES)])
                    ch.done(nc.vector.tensor_scalar(half_pos[:, 0], pos[:, :, :], 4, None, ALU.logical_shift_right))
                    ch.link(nc.vector.tensor_scalar(half_pos[:, 1], pos[:, :, :], 15, None, ALU.bitwise_and))
                    ch.link(nc.vector.tensor_copy(half_posf[:, :, :, :], half_pos[:, :, :, :]))
                    for s in range(2):
                        nc.vector.tensor_tensor(
                            onehot[:, s], half_posf[:, s].rearrange("p t (k o) -> p (t k) o", o=1).to_broadcast([P, TILES * TOPK, TOPK]),
                            table("iota")[:, 0:TOPK].rearrange("p (o k) -> p o k", o=1).to_broadcast([P, TILES * TOPK, TOPK]),
                            ALU.is_equal).then_inc(positions.sem, 1)
                    ch.done(nc.vector.tensor_tensor(gates[:, :, bass.ds(it * TOPK, TOPK)], top[:, :, :],
                                                    top[:, :, 0:1].to_broadcast([P, TILES, TOPK]), ALU.subtract))

                def select(it, ch):
                    for s, dst in enumerate((first, second)):
                        dve.wait_ge(picked.sem, it * 2 * TILES + TILES * (s + 1))
                        ch.done(nc.vector.tensor_reduce(dst[:, :, bass.ds(it * TOPK, TOPK)],
                                                        onehot[:, s].rearrange("p (t k) j -> p t k j", t=TILES), AX.X, ALU.add))
                    ch.wait()

                for n in range(RING):
                    st.low(dve, 0, n)
                steps = 5 * 6 + 1 + TILES + 5 * TILES + 3 + 1 + 2
                with dve.Fori(0, PKH - 1) as it:
                    ch = Chain(dve, dve_chain, it, steps)
                    for n in range(RING):
                        st.low(dve, it, n + RING)
                    choose(it, ch)
                    select(it, ch)
                ch.close(PKH - 1)
                ch = Chain(dve, dve_chain)
                choose(PKH - 1, ch)
                select(PKH - 1, ch)
                dve.sem_inc(dve_to_act.sem, 1)
                ch.close()
            st.close(2 * PKH)
            dve_to_act.v += 1
        w_scope.close()
        with nc.Block() as block:
            @block.scalar
            def _(act):
                nc.scalar.activation(gates[:, :, :], gates[:, :, :], ACT.Exp).then_inc(act_to_dve.sem, 1)

            @block.vector
            def _(dve):
                ch = Chain(dve, dve_chain)
                dve.wait_ge(act_to_dve.sem, act_to_dve.v + 1)
                g16 = gates[:, :, :].rearrange("p t (h k) -> p (t h) k", k=TOPK)
                total = rstd[:, 0:TILES * PKH]
                ch.link(nc.vector.tensor_reduce(total, g16, AX.X, ALU.add))
                ch.link(nc.vector.reciprocal(total, total))
                ch.link(nc.vector.tensor_tensor(g16, g16, total.rearrange("p (n o) -> p n o", o=1
                                                                          ).to_broadcast([P, TILES * PKH, TOPK]), ALU.mult))
                ch.close()
            act_to_dve.v += 1

        GT = 64
        NG = T // GT
        gate_table = nc.dram_tensor("gate_table", [NG, P, NK, GT], F32, kind="Internal").ap()
        with ExitStack() as t_scope, nc.Block() as block:
            slot = sb(t_scope, "slot", [P, 3, T])
            fa = sb(t_scope, "fa", [P, 8, NK])
            fb = sb(t_scope, "fb", [P, 8, NK])
            stage = sb(t_scope, "stage", [P, 2, NK, GT])
            slots_turned, slots_here = sem("slots_turned"), sem("slots_here")
            fa_ready, fb_ready, table_done, staged = sem("fa_ready"), sem("fb_ready"), sem("table_done", 8), sem("staged", 4)
            stage_out = [sem("stage_out0", 16), sem("stage_out1", 16)]
            IN = 4

            @block.tensor
            def _(pe):
                pe.sem_inc(table_done.sem, 8)
                for n, src in enumerate((gates, first, second)):
                    for tile in range(TILES):
                        last = pe.transpose(ps[:, 4 + n, tile * P:(tile + 1) * P], src[:, tile, :], table("ident"))
                last.then_inc(slots_turned.sem, 1)
                with pe.Fori(0, NG * IN) as it:
                    for n in range(16):
                        u, bank = n % 8, n // 4
                        pe.wait_ge(fa_ready.sem, it * 16 + n + 1)
                        pe.wait_ge(fb_ready.sem, it * 4 + n // 4 + 1)
                        if n % 4 == 0:
                            pe.wait_ge(staged.sem, it * 4 + bank + 1)
                        pe.matmul(ps[:, bank, (n % 4) * NK:(n % 4 + 1) * NK], fa[:, u, :], fb[:, u, :],
                                  start=True, stop=True).then_inc(table_done.sem, 1)

            @block.vector
            def _(dve):
                dve.wait_ge(slots_here.sem, 1)
                with dve.Fori(0, NG * IN) as it:
                    for n in range(16):
                        dve.wait_ge(table_done.sem, it * 16 + (n | 3) + 1)
                        if n % 4 == 0:
                            nc.vector.tensor_tensor(
                                fb[:, n % 8:n % 8 + 4, :], tab[:, TABLE_NAMES.index("iota"):TABLE_NAMES.index("iota") + 1, :].to_broadcast([P, 4, NK]),
                                slot[:, 2, bass.ds(it * 16 + n, 4)].rearrange("p (t o) -> p t o", o=1).to_broadcast([P, 4, NK]),
                                ALU.is_equal).then_inc(fb_ready.sem, 1)
                        tok = bass.ds(it * 16 + n, 1)
                        nc.vector.tensor_scalar(fa[:, n % 8, :], table("iota"), slot[:, 1, tok], slot[:, 0, tok],
                                                ALU.is_equal, ALU.mult).then_inc(fa_ready.sem, 1)

            @block.scalar
            def _(act):
                act.sem_inc(staged.sem, 4)
                for s in stage_out:
                    act.sem_inc(s.sem, 16)
                act.wait_ge(slots_turned.sem, 1)
                nc.scalar.activation(slot[:, :, :], ps[:, 4:7, 0:T], ACT.Copy).then_inc(slots_here.sem, 1)
                with act.Fori(0, NG // 2) as pair:
                    for s in range(2):
                        act.wait_ge(stage_out[s].sem, pair * 16 + 16)
                        with act.Fori(0, IN) as q:
                            for n in range(4):
                                act.wait_ge(table_done.sem, pair * (2 * IN * 16) + q * 16 + (s * IN * 16 + 8 + 4 * n + 4))
                                nc.scalar.activation(stage[:, s, :, bass.ds(q * 16 + 4 * n, 4)],
                                                     ps[:, n, :].rearrange("p (t i) -> p i t", t=4),
                                                     ACT.Copy).then_inc(staged.sem, 1)

            @block.sync
            def _(sp):
                with sp.Fori(0, NG // 2) as pair:
                    for s in range(2):
                        sp.wait_ge(staged.sem, pair * 2 * 4 * IN + (s + 1) * 4 * IN + 4)
                        sp.dma_start(gate_table[bass.ds(pair * 2 + s, 1)].rearrange("o p i t -> (o p) i t"),
                                     stage[:, s]).then_inc(stage_out[s].sem, 16)
                for s in range(2):
                    sp.wait_ge(stage_out[s].sem, 16 + 16 * (NG // 2))
        p_scope.close()

        EG = 2
        STEPS = NK // EG
        LAG = 4
        acc_scope = ExitStack()
        acc = sb(acc_scope, "acc", [P, KD, T])
        e_scope = ExitStack()
        u_raw = sb(e_scope, "u_raw", [P, EG, KD, P])
        v_raw = sb(e_scope, "v_raw", [P, EG, D])
        u_hi = sb(e_scope, "u_hi", [P, EG, KD, P], F32R)
        u_lo = sb(e_scope, "u_lo", [P, EG, KD, P], F32R)
        v_hi = sb(e_scope, "v_hi", [P, EG, D], F32R)
        v_lo = sb(e_scope, "v_lo", [P, EG, D], F32R)
        gate = sb(e_scope, "gate", [P, NG, EG, GT])
        act_f = sb(e_scope, "act_f", [P, EG, T])
        act_hi = sb(e_scope, "act_hi", [P, EG, T], F32R)
        act_lo = sb(e_scope, "act_lo", [P, EG, T], F32R)
        with nc.Block() as block:
            u_landed = [sem(f"u_landed{e}") for e in range(EG)]
            v_landed = [sem(f"v_landed{e}") for e in range(EG)]
            gate_landed = sem("gate_landed")
            u_high, u_split, v_high, v_split = sem("u_high"), sem("u_split"), sem("v_high"), sem("v_split")
            act_high, act_split, gelu_done, gated_ = sem("act_high"), sem("act_split"), sem("gelu_done"), sem("act_gated")
            u_done, sum_done, added = sem("u_done"), sem("sum_done"), sem("added")

            @block.sync
            def _(sp):
                def load_u(g, e):
                    sp.dma_start(u_raw[:, e], expert_u[bass.ds(g * EG + e, 1)].rearrange("o p k c -> (o p) k c")
                                 ).then_inc(u_landed[e].sem, 16)

                def load_v(g, e):
                    sp.dma_start(v_raw[:, e], expert_v[bass.ds(g * EG + e, 1)].rearrange("o p c -> (o p) c")
                                 ).then_inc(v_landed[e].sem, 16)

                def load_gate(g):
                    sp.dma_start(gate[:, :, :, :].rearrange("p b e t -> p b (e t)"),
                                 gate_table[:, :, bass.ds(g * EG, EG), :].rearrange("b p e t -> p b (e t)")
                                 ).then_inc(gate_landed.sem, 16)

                for e in range(EG):
                    load_u(0, e)
                for e in range(EG):
                    load_v(0, e)
                load_gate(0)
                for e in range(EG):
                    sp.wait_ge(u_split.sem, e + 1)
                    load_u(1, e)

                def step(g, more_u=True):
                    if more_u:
                        for e in range(EG):
                            sp.wait_ge(u_split.sem, g * EG + (EG + e + 1))
                            load_u(g + 2, e)
                    for e in range(EG):
                        sp.wait_ge(v_split.sem, g * EG + (e + 1))
                        load_v(g + 1, e)
                    sp.wait_ge(gated_.sem, g + 1)
                    load_gate(g + 1)

                with sp.Fori(0, STEPS - 2) as it:
                    step(it)
                step(STEPS - 2, more_u=False)

            @block.scalar
            def _(act):
                def split_u(g, e, first=False):
                    act.wait_ge(u_landed[e].sem, g * 16 + 16)
                    if not first:
                        act.wait_ge(u_done.sem, g * EG + (e + 1 - EG))
                    nc.scalar.activation(u_hi[:, e], u_raw[:, e], ACT.Copy).then_inc(u_high.sem, 1)

                def gelu(g, e):
                    act.wait_ge(u_done.sem, g * EG + (e + 1))
                    nc.scalar.activation(act_f[:, e, :], ps[:, e, 0:T], ACT.Gelu_apprx_tanh).then_inc(gelu_done.sem, 1)

                for e in range(EG):
                    split_u(0, e, first=True)
                for e in range(EG):
                    split_u(1, e)
                for e in range(EG):
                    gelu(0, e)

                def step(g, more_u=2):
                    for e in range(EG):
                        act.wait_ge(v_landed[e].sem, g * 16 + 16)
                        if e == 0:
                            act.wait_ge(sum_done.sem, g * KD + KD)
                        nc.scalar.activation(v_hi[:, e], v_raw[:, e], ACT.Copy).then_inc(v_high.sem, 1)
                    act.wait_ge(gated_.sem, g + 1)
                    nc.scalar.activation(act_hi[:, :, :], act_f[:, :, :], ACT.Copy).then_inc(act_high.sem, 1)
                    if more_u == 2:
                        for e in range(EG):
                            split_u(g + 2, e)
                    if more_u:
                        act.wait_ge(act_split.sem, g + 1)
                        for e in range(EG):
                            gelu(g + 1, e)

                with act.Fori(0, STEPS - 2) as it:
                    step(it)
                step(STEPS - 2, more_u=1)
                step(STEPS - 1, more_u=0)

            @block.vector
            def _(dve):
                nc.vector.memset(acc[:, :, :], 0.0)
                dve.sem_inc(added.sem, KD)

                def split_u(g, e):
                    dve.wait_ge(u_high.sem, g * EG + (e + 1))
                    nc.vector.tensor_tensor(u_lo[:, e], u_raw[:, e], u_hi[:, e].bitcast(F32), ALU.subtract
                                            ).then_inc(u_split.sem, 1)

                for g in range(2):
                    for e in range(EG):
                        split_u(g, e)

                def step(g, more_u=True):
                    for e in range(EG):
                        dve.wait_ge(v_high.sem, g * EG + (e + 1))
                        nc.vector.tensor_tensor(v_lo[:, e], v_raw[:, e], v_hi[:, e].bitcast(F32), ALU.subtract
                                                ).then_inc(v_split.sem, 1)
                    dve.wait_ge(gate_landed.sem, g * 16 + 16)
                    dve.wait_ge(gelu_done.sem, g * EG + EG)
                    for e in range(EG):
                        a = act_f[:, e, :].rearrange("p (b t) -> p b t", b=NG)
                        last = nc.vector.tensor_tensor(a, a, gate[:, :, e, :], ALU.mult)
                    last.then_inc(gated_.sem, 1)
                    dve.wait_ge(act_high.sem, g + 1)
                    nc.vector.tensor_tensor(act_lo[:, :, :], act_f[:, :, :], act_hi[:, :, :].bitcast(F32), ALU.subtract
                                            ).then_inc(act_split.sem, 1)
                    for d in range(KD):
                        dve.wait_ge(sum_done.sem, g * KD + (KD + d + 1))
                        dve.wait_ge(added.sem, g * KD + (d + 1))
                        nc.vector.tensor_tensor(acc[:, d, :], acc[:, d, :], ps[:, 2 + d % LAG, 0:T], ALU.add
                                                ).then_inc(added.sem, 1)
                        if more_u and d in (5, 11):
                            split_u(g + 2, d // 6)

                with dve.Fori(0, STEPS - 2) as it:
                    step(it)
                step(STEPS - 2, more_u=False)
                step(STEPS - 1, more_u=False)

            @block.tensor
            def _(pe):
                def up(g, first=False):
                    for e in range(EG):
                        pe.wait_ge(u_split.sem, g * EG + (e + 1))
                        if e == 0 and not first:
                            pe.wait_ge(gelu_done.sem, g * EG)
                        for k in range(KD):
                            pe.matmul(ps[:, e, 0:T], u_hi[:, e, k, :], hhi[:, k, :], start=(k == 0), stop=False)
                            pe.matmul(ps[:, e, 0:T], u_hi[:, e, k, :], hlo[:, k, :], start=False, stop=False)
                            last = pe.matmul(ps[:, e, 0:T], u_lo[:, e, k, :], hhi[:, k, :], start=False, stop=(k == KD - 1))
                        last.then_inc(u_done.sem, 1)

                def down(g):
                    pe.wait_ge(v_split.sem, g * EG + EG)
                    pe.wait_ge(act_split.sem, g + 1)
                    for d in range(KD):
                        pe.wait_ge(added.sem, g * KD + (KD + d + 1 - LAG))
                        bank, cols_ = ps[:, 2 + d % LAG, 0:T], slice(d * P, (d + 1) * P)
                        for e in range(EG):
                            pe.matmul(bank, v_hi[:, e, cols_], act_hi[:, e, :], start=(e == 0), stop=False)
                            pe.matmul(bank, v_hi[:, e, cols_], act_lo[:, e, :], start=False, stop=False)
                            last = pe.matmul(bank, v_lo[:, e, cols_], act_hi[:, e, :], start=False, stop=(e == EG - 1))
                        last.then_inc(sum_done.sem, 1)

                pe.sem_inc(sum_done.sem, KD)
                up(0, first=True)
                with pe.Fori(0, STEPS - 1) as it:
                    up(it + 1)
                    down(it)
                down(STEPS - 1)

        e_scope.close()
        with ExitStack() as n_scope:
            sq = sb(n_scope, "sq", [P, KD, T])
            if debug is not None and "peer" in debug:
                dump("peer", (0, 16, acc[:, :, :]))
            square_root_of_mean(acc, sq)
            add_to_residual(acc, 80, out=y_out)
        acc_scope.close()
        h_scope.close()


def lay_out(i):
    def chan(a):
        return np.ascontiguousarray(np.asarray(a).reshape(-1, P).T)

    def blocks(w):
        w = np.asarray(w)
        return np.ascontiguousarray(w.reshape(KD, P, -1, P).transpose(2, 1, 0, 3))

    g = {k: np.asarray(v) for k, v in i.items()}
    xs = np.concatenate([g["x_prompt"][0], g["x_sample"][0]], 0)
    cc = np.stack([g["c_ctx"], g["c"][0]], 0)
    tables = constant_tables()
    out = {
        "x_t": xs.reshape(T, KD, P).transpose(2, 1, 0),
        "c_t": cc.reshape(2, KD, P).transpose(2, 1, 0),
        "cols_in": np.concatenate([chan(g["b_ada"]), chan(g["g_pre1"]), chan(g["g_post1"]), chan(g["g_pre2"]),
                                   chan(g["g_post2"]), chan(g["mu_shift"]), chan(g["w0"]), chan(g["a0"]),
                                   chan(g["k_k"]), chan(g["k_a"]), chan(g["r_k"]), chan(g["ln_x_w"]),
                                   chan(g["ln_x_b"]), chan(g["ln_v_w"]), chan(g["ln_v_b"])], 1),
        "tables_in": np.stack([tables[n] for n in TABLE_NAMES], 1),
        "w_ada": g["w_ada"][0].reshape(4, 4, P, 24, 512).transpose(3, 0, 2, 1, 4).reshape(96, P, KD, P),
        "w_in": blocks(g["w_in"][0]),
        "w2a2": np.stack([g["w2"][0].reshape(2 * 64, PAIRS, P), g["a2"][0].reshape(2 * 64, PAIRS, P)], 0).transpose(2, 1, 0, 3),
        "w_s": g["w_s"][0].transpose(2, 0, 1),
        "b_s": g["b_s"][0].reshape(1, HB, P),
        "state_t": np.stack([g["state_fwd"][0, 0], g["state_bwd"][0, 0]], 0)
                     .reshape(2, PAIRS, 2, HEAD, HEAD).transpose(1, 2, 4, 0, 3).reshape(PAIRS, P, 2, HEAD),
        "w_out": blocks(g["w_out"][0]),
        "w_query": blocks(g["w_query"][0]),
        "keys_t": g["sub_keys"][0].transpose(3, 1, 0, 2),
        "expert_u": g["expert_u"][0].reshape(NK, NK, KD, P).transpose(1, 3, 2, 0),
        "expert_v": g["expert_v"][0].reshape(NK, NK, D).transpose(1, 0, 2),
    }
    return {k: np.ascontiguousarray(v) for k, v in out.items()}


OUTS = {"y_out": ((P, KD, T), "float32"), "state_out": ((PAIRS, P, 2, HEAD), "float32")}


def kernel(**inputs):
    import concourse.bacc as bacc
    from concourse.bass_utils import run_bass_kernel_spmd

    nc = bacc.Bacc("TRN2", target_bir_lowering=False, num_devices=1, dynamic_dma_scratch_size=2048)
    arrays = lay_out(inputs)
    args = {n: nc.dram_tensor(n, a.shape, mybir.dt.from_np(a.dtype), kind="ExternalInput").ap()
            for n, a in arrays.items()}
    args |= {n: nc.dram_tensor(n, s, mybir.dt.from_np(np.dtype(d)), kind="ExternalOutput").ap()
             for n, (s, d) in OUTS.items()}
    build_program(nc, **args)
    got = run_bass_kernel_spmd(nc, [arrays], core_ids=[0]).results[0]
    y = np.asarray(got["y_out"]).transpose(2, 1, 0).reshape(T, D)
    st = np.asarray(got["state_out"]).reshape(PAIRS, 2, HEAD, 2, HEAD).transpose(3, 0, 1, 4, 2)
    st = st.reshape(2, 1, 1, 2 * PAIRS, HEAD, HEAD)
    return (np.ascontiguousarray(y[None, :CTX]), np.ascontiguousarray(y[None, CTX:]),
            np.ascontiguousarray(st[0]), np.ascontiguousarray(st[1]))
```

```python
from contextlib import ExitStack

import numpy as np

import concourse.bass as bass
from concourse import mybir

F32 = mybir.dt.float32
F32R = mybir.dt.float32r
U32 = mybir.dt.uint32
I32 = mybir.dt.int32
ALU = mybir.AluOpType
ACT = mybir.ActivationFunctionType
AX = mybir.AxisListType

P = 128
D = 2048
KD = D // P
CTX, LAT = 128, 256
T = CTX + LAT
TILES = T // P
GRID_W = 64
GRID_H = LAT // GRID_W
DA = 1024
DB = D - DA
HEAD = 64
PAIRS = DA // P
NSHIFT = (4 * DA + 256) // P
NIN = NSHIFT + 2 * DB // P
HB = DB // P
PKH = 8
TOPK = 16
NK = 128
SLOTS = PKH * TOPK
EXP_HALF = float(np.exp(-0.5))
EPS = 1e-6
GN_EPS = 64e-5
RING = 2
CREDIT = 8
NEG = -3.0e38

Z_R, Z_K, Z_V, Z_G, Z_LW, Z_LA, Z_U, Z_VG = 0, 8, 16, 24, 32, 33, 34, 42


def _mask(f):
    p, q = np.meshgrid(np.arange(P), np.arange(P), indexing="ij")
    return f(p, q).astype(np.float32)


def constant_tables():
    t = {"ident": _mask(lambda p, q: p == q),
         "mean_d": np.full((P, P), 1.0 / D, np.float32),
         "mean_db": np.full((P, P), 1.0 / DB, np.float32),
         "head_sum": _mask(lambda p, q: p // HEAD == q // HEAD),
         "head_mean": _mask(lambda p, q: p // HEAD == q // HEAD) / HEAD,
         "iota": _mask(lambda p, q: q),
         "ones": np.ones((P, P), np.float32),
         "pick": _mask(lambda p, q: (p < 4) & (p % 2 == q))}
    for d, (lt, le) in enumerate(((lambda i, t: i < t, lambda i, t: i <= t),
                                  (lambda i, t: i > t, lambda i, t: i >= t))):
        t[f"ab{d}"] = _mask(lt)
        t[f"rb{d}"] = _mask(le)
        t[f"ak{d}"] = _mask(lt)
        t[f"rk{d}"] = _mask(le)
    for d, sign in ((0, 1), (1, -1)):
        t[f"two{d}"] = _mask(lambda i, t: (t - i == sign) & (i // 2 == t // 2))
        for b in (2, 4, 8, 16, 32, 64):
            t[f"half{d}_{b}"] = _mask(lambda t, i: (t // b - i // b == sign) & (i // (2 * b) == t // (2 * b)))
    return t


TABLE_NAMES = list(constant_tables())
NTAB = TABLE_NAMES.index("ab0")
COLS = {}
_n = 0
for _name, _w in (("b_ada", 96), ("g_pre1", 16), ("g_post1", 16), ("g_pre2", 16), ("g_post2", 16),
                  ("mu", NSHIFT), ("w0", 16), ("a0", 16), ("k_k", 8), ("k_a", 8), ("r_k", 8),
                  ("ln_x_w", 8), ("ln_x_b", 8), ("ln_v_w", 8), ("ln_v_b", 8)):
    COLS[_name] = (_n, _w)
    _n += _w
NCOLS = _n


class Tally:

    def __init__(self, sem, start=0):
        self.sem, self.v = sem, start


class Chain:

    def __init__(self, eng, tally, it=None, per=0):
        self.eng, self.t, self.it, self.per, self.n = eng, tally, it, per, 0

    def at(self, n):
        v = self.t.v + n
        return v if self.it is None else self.it * self.per + v

    def done(self, ins):
        ins.then_inc(self.t.sem, 1)
        self.n += 1
        return self.n

    def wait(self, n=None):
        self.eng.wait_ge(self.t.sem, self.at(self.n if n is None else n))

    def link(self, ins):
        self.done(ins)
        self.wait()

    def close(self, passes=1):
        assert self.it is None or self.n == self.per, (self.n, self.per)
        self.t.v += self.n * passes
        self.n = 0


class Signal:

    def __init__(self, tally, per):
        self.t, self.per, self.n = tally, per, 0

    def inc(self, ins):
        ins.then_inc(self.t.sem, 1)
        self.n += 1
        return self.n

    def wait(self, eng, it, n):
        assert 1 <= n <= self.per, (n, self.per)
        eng.wait_ge(self.t.sem, it * self.per + self.t.v + n)

    def close(self, passes):
        assert self.n % self.per == 0, (self.n, self.per)
        self.t.v += self.per * passes
        self.n = 0


def build_program(nc, x_t, c_t, cols_in, tables_in, w_ada, w_in, w2a2, w_s, b_s, state_t, w_out, w_query,
                  keys_t, expert_u, expert_v, y_out, state_out, debug=None):
    ctx = ExitStack()

    def sem(name, start=0):
        return Tally(ctx.enter_context(nc.semaphore(name)), start)

    def sb(stack, name, shape, dt=F32):
        return stack.enter_context(nc.sbuf_tensor(name, shape, dt))

    with ctx:
        ps = ctx.enter_context(nc.psum_tensor("ps", [P, 8, 512], F32))
        x = sb(ctx, "x", [P, KD, T])
        cols = sb(ctx, "cols", [P, NCOLS])
        tab = sb(ctx, "tab", [P, NTAB, P])
        mod = sb(ctx, "mod", [P, 96, 2])
        rstd = sb(ctx, "rstd", [P, T])
        eps = sb(ctx, "eps", [P, 2])

        def table(name):
            n = TABLE_NAMES.index(name)
            return tab[:, n, :] if n < NTAB else scan_tab[:, n - NTAB, :]

        def scan_tables(name, n=1):
            a = TABLE_NAMES.index(name) - NTAB
            return scan_tab[:, a:a + n, :]

        def col(name, i=0, n=1):
            a, w = COLS[name]
            return cols[:, a + i:a + i + n]

        loads = sem("loads")
        raw_landed = [sem(f"raw_landed{i}") for i in range(8)]
        hi_ready = sem("hi_ready")
        lo_ready = sem("lo_ready", CREDIT)
        lo_of = [sem("lo_of_even", CREDIT), sem("lo_of_odd", CREDIT)]
        product_ready = sem("product_ready", CREDIT)
        bank_free = sem("bank_free", RING)
        act_chain = sem("act_chain")
        dve_chain = sem("dve_chain")
        pool_chain = sem("pool_chain")
        act_to_pe = sem("act_to_pe")
        dve_to_pe = sem("dve_to_pe")
        pe_to_act = sem("pe_to_act")
        pe_to_dve = sem("pe_to_dve")
        act_to_dve = sem("act_to_dve")
        dve_to_act = sem("dve_to_act")
        stores = sem("stores")

        z_scope = ExitStack()
        scan_tab = sb(z_scope, "scan_tab", [P, len(TABLE_NAMES) - NTAB, P])

        with nc.Block() as block:
            @block.sync
            def _(sp):
                for dst, src in ((x[:, :, :], x_t), (cols[:, :], cols_in), (tab[:, :, :], tables_in[:, 0:NTAB]),
                                 (scan_tab[:, :, :], tables_in[:, NTAB:])):
                    sp.dma_start(dst, src).then_inc(loads.sem, 16)
                sp.wait_ge(loads.sem, 64)

            @block.tensor
            def _(pe):
                pe.sem_inc(product_ready.sem, CREDIT)

            @block.vector
            def _(dve):
                for t in [lo_ready] + lo_of:
                    dve.sem_inc(t.sem, CREDIT)
                nc.vector.memset(eps[:, 0:1], EPS)
                nc.vector.memset(eps[:, 1:2], GN_EPS)
                dve.sem_inc(bank_free.sem, RING)
        loads.v = 64

        class Stream:
            def __init__(self, per, raw, parts, shared=False):
                assert per % len(raw) == 0 and per % len(parts) == 0
                self.per, self.raw, self.parts = per, raw, parts
                self.lows = lo_of if shared else [lo_ready]

            def split(self, it, n, before=0):
                m = len(self.lows)
                t = self.lows[n % m]
                return t.sem, it * (self.per // m) + (t.v + n // m + 1 - before // m)

            def load(self, sp, blocks, weights):
                with sp.Fori(0, blocks // self.per) as it:
                    for n in range(self.per):
                        u = n % len(self.raw)
                        sp.wait_ge(*self.split(it, n, len(self.raw)))
                        sp.dma_start(self.raw[u], weights[bass.ds(it * self.per + n, 1)].rearrange("o p k c -> (o p) k c")
                                     ).then_inc(raw_landed[u].sem, 16)

            def high(self, act, it, n):
                u, turn = n % len(self.raw), n // len(self.raw)
                turns = self.per // len(self.raw)
                act.wait_ge(raw_landed[u].sem, it * (16 * turns) + raw_landed[u].v + 16 * (turn + 1))
                act.wait_ge(product_ready.sem,
                            it * self.per + product_ready.v + n + 1 - len(self.parts))
                nc.scalar.activation(self.parts[n % len(self.parts)][0], self.raw[u], ACT.Copy).then_inc(hi_ready.sem, 1)

            def low(self, eng, it, n, ops=nc.vector):
                hi, lo = self.parts[n % len(self.parts)]
                eng.wait_ge(hi_ready.sem, it * self.per + hi_ready.v + n + 1)
                ops.tensor_tensor(lo, self.raw[n % len(self.raw)], hi.bitcast(F32), ALU.subtract
                                  ).then_inc(self.lows[n % len(self.lows)].sem, 1)

            def product(self, pe, it, n, bank, input_block=None):
                hi, lo = self.parts[n % len(self.parts)]
                pe.wait_ge(*self.split(it, n))
                pe.wait_ge(bank_free.sem, it * self.per + bank_free.v + n + 1 - RING)
                for k in range(KD):
                    if input_block is not None:
                        pe.wait_ge(input_block.sem, input_block.v + k + 1)
                    pe.matmul(bank, hi[:, k, :], hhi[:, k, :], start=(k == 0), stop=False)
                    pe.matmul(bank, hi[:, k, :], hlo[:, k, :], start=False, stop=False)
                    last = pe.matmul(bank, lo[:, k, :], hhi[:, k, :], start=False, stop=(k == KD - 1))
                last.then_inc(product_ready.sem, 1)

            def ahead(self, eng, blocks, split, drain, started=False):
                for n in range(0 if started else RING):
                    split(0, n)
                eng_loop = eng.Fori(0, blocks // RING - 1)
                with eng_loop as it:
                    for n in range(RING):
                        drain(it, n)
                        split(it, n + RING)
                for n in range(RING):
                    drain(blocks // RING - 1, n)

            def close(self, blocks, banks=True):
                for u in range(len(self.raw)):
                    raw_landed[u].v += 16 * (blocks // len(self.raw))
                for t in (hi_ready, product_ready) + ((bank_free,) if banks else ()):
                    t.v += blocks
                for t in self.lows:
                    t.v += blocks // len(self.lows)

        z = sb(z_scope, "z", [P, NIN, T])
        hf = z[:, Z_U:NIN, :]
        b_scope = ExitStack()
        hhi = sb(b_scope, "hhi", [P, KD, T], F32R)
        hlo = sb(b_scope, "hlo", [P, KD, T], F32R)
        raw = sb(b_scope, "raw", [P, RING, KD, P])
        whi = sb(b_scope, "whi", [P, RING, KD, P], F32R)
        wlo = sb(b_scope, "wlo", [P, RING, KD, P], F32R)
        st = Stream(RING, [raw[:, u] for u in range(RING)], [(whi[:, u], wlo[:, u]) for u in range(RING)])

        with ExitStack() as a_scope, nc.Block() as block:
            csig = sb(a_scope, "csig", [P, KD, 2])
            csil = sb(a_scope, "csil", [P, KD, 2])
            cparts = sb(a_scope, "cparts", [P, KD, 4], F32R)
            rows = sb(a_scope, "rows", [4, 2, 512])
            NCH, KQ = 24, 4
            rows_ready = sem("rows_ready")
            turned = sem("turned", 2)
            kq = KD // KQ
            more = z[:, 0:32, :].rearrange("p b t -> p (b t)").rearrange("p (s k c) -> p s k c", s=6, k=KD)
            hs = [h[:, :, :].rearrange("p k t -> p (k t)").rearrange("p (s k c) -> p s k c", s=3, k=KD) for h in (hhi, hlo)]
            sa = Stream(2 * KQ, [raw[:, 0], raw[:, 1]] + [more[:, u] for u in range(6)],
                        [(whi[:, u], wlo[:, u]) for u in range(2)] + [(hs[0][:, u], hs[1][:, u]) for u in range(2)])

            def w4(t):
                return t.rearrange("p k c -> p (k c)").rearrange("p (k c) -> p k c", k=kq)

            @block.sync
            def _(sp):
                sp.dma_start(csig[:, :, :], c_t).then_inc(loads.sem, 16)
                sa.load(sp, NCH * KQ, w_ada)

            @block.scalar
            def _(act):
                act.wait_ge(loads.sem, loads.v + 16)
                act.sem_inc(turned.sem, 2)
                nc.scalar.activation(csil[:, :, :], csig[:, :, :], ACT.Silu).then_inc(act_chain.sem, 1)
                act.wait_ge(act_chain.sem, act_chain.v + 1)
                nc.scalar.activation(cparts[:, :, 0:2], csil[:, :, :], ACT.Copy).then_inc(act_to_dve.sem, 1)
                for k in range(KD):
                    nc.scalar.activation(hf[:, k, :], x[:, k, :], ACT.Square).then_inc(act_to_pe.sem, 1)
                act.wait_ge(pe_to_act.sem, pe_to_act.v + 1)
                nc.scalar.activation(rstd[:, :], ps[:, 7, 0:T], ACT.Sqrt, bias=eps[:, 0:1]).then_inc(act_to_dve.sem, 1)
                def chunks(it, last=False):
                    for c in range(2):
                        for n in range(2, KQ + 2):
                            if not (last and c == 1 and n >= KQ):
                                sa.high(act, it, c * KQ + n)
                        act.wait_ge(product_ready.sem, it * 2 * KQ + product_ready.v + (c + 1) * KQ)
                        act.wait_ge(turned.sem, it * 2 + c + 1)
                        nc.scalar.activation(rows[:, c, :], ps[0:4, c, :], ACT.Copy).then_inc(rows_ready.sem, 1)

                for n in range(2):
                    sa.high(act, 0, n)
                with act.Fori(0, NCH // 2 - 1) as it:
                    chunks(it)
                chunks(NCH // 2 - 1, last=True)

            @block.tensor
            def _(pe):
                for k in range(KD):
                    pe.wait_ge(act_to_pe.sem, act_to_pe.v + 1 + k)
                    last = pe.matmul(ps[:, 7, 0:T], table("mean_d"), hf[:, k, :], start=(k == 0), stop=(k == KD - 1))
                last.then_inc(pe_to_act.sem, 1)
                pe.wait_ge(dve_to_pe.sem, dve_to_pe.v + 1)

                def quarter(it, n, first=False):
                    c, q = (n // KQ) % 2, n % KQ
                    pe.wait_ge(lo_ready.sem, it * 2 * KQ + lo_ready.v + n + 1)
                    if q == 0 and not first:
                        pe.wait_ge(rows_ready.sem, it * 2 + n // KQ - 1)
                    for k in range(kq):
                        pe.matmul(ps[0:4, c, :], cparts[:, q * kq + k, :], w4(sa.parts[n % 4][0])[:, k, :],
                                  start=(q == 0 and k == 0), stop=False)
                        last = pe.matmul(ps[0:4, c, :], cparts[:, q * kq + k, :], w4(sa.parts[n % 4][1])[:, k, :],
                                         start=False, stop=(q == KQ - 1 and k == kq - 1))
                    last.then_inc(product_ready.sem, 1)

                def chunks(it, last=False, first=False):
                    for c in range(2):
                        for n in range(2, KQ + 2):
                            if not (last and c == 1 and n >= KQ):
                                quarter(it, c * KQ + n, first=first and c == 0)
                        pe.wait_ge(rows_ready.sem, it * 2 + c + 1)
                        for j in range(4):
                            last_ = pe.matmul(ps[:, 6, bass.ds(it * 16 + c * 8 + 2 * j, 2)], rows[:, c, j * P:(j + 1) * P],
                                              tab[0:4, TABLE_NAMES.index("pick"), 0:2], start=True, stop=True)
                        last_.then_inc(turned.sem, 1)

                for n in range(2):
                    quarter(0, n, first=True)
                chunks(0, first=True)
                with pe.Fori(1, NCH // 2 - 1) as it:
                    chunks(it)
                chunks(NCH // 2 - 1, last=True)

            @block.vector
            def _(dve):
                ch = Chain(dve, dve_chain)
                dve.wait_ge(act_to_dve.sem, act_to_dve.v + 1)
                nc.vector.tensor_tensor(cparts[:, :, 2:4], csil[:, :, :], cparts[:, :, 0:2].bitcast(F32), ALU.subtract
                                        ).then_inc(dve_to_pe.sem, 1)
                dve.wait_ge(act_to_dve.sem, act_to_dve.v + 2)
                ch.done(nc.vector.reciprocal(rstd[:, :], rstd[:, :]))
                with dve.Fori(0, NCH // 2) as it:
                    for n in range(2 * KQ):
                        sa.low(dve, it, n)
                dve.wait_ge(turned.sem, 2 + NCH)
                ch.link(nc.vector.tensor_tensor(
                    mod[:, :, :], ps[:, 6, 0:2 * 96].rearrange("p (j s) -> p j s", s=2),
                    col("b_ada", 0, 96).rearrange("p (j o) -> p j o", o=1).to_broadcast([P, 96, 2]), ALU.add))
                for first, gain in ((16, "g_pre1"), (64, "g_pre2")):
                    m = mod[:, first:first + 16, :]
                    g = col(gain, 0, 16).rearrange("p (j o) -> p j o", o=1).to_broadcast([P, 16, 2])
                    ch.link(nc.vector.tensor_scalar(m, m, 1.0, None, ALU.add))
                    ch.link(nc.vector.tensor_tensor(m, m, g, ALU.mult))
                for first, gain in ((32, "g_post1"), (80, "g_post2")):
                    m = mod[:, first:first + 16, :]
                    g = col(gain, 0, 16).rearrange("p (j o) -> p j o", o=1).to_broadcast([P, 16, 2])
                    ch.link(nc.vector.tensor_tensor(m, m, g, ALU.mult))
                ch.close()
            loads.v += 16
            sa.close(NCH * KQ, banks=False)
            act_chain.v += 1
            act_to_pe.v += KD
            dve_to_pe.v += 1
            pe_to_act.v += 1
            act_to_dve.v += 2

        SPLIT_AT = (3, 9)

        class Modulate:

            def __init__(self, dst, shift_at, scale_at):
                self.dst, self.shift_at, self.scale_at = dst, shift_at, scale_at

            def vector(self, dve, split):
                dst = self.dst

                def low(k):
                    dve.wait_ge(act_to_dve.sem, act_to_dve.v + k + 1)
                    nc.vector.tensor_tensor(hlo[:, k, :], dst[:, k, :], hhi[:, k, :].bitcast(F32),
                                            ALU.subtract).then_inc(dve_to_pe.sem, 1)

                for k in range(KD):
                    nc.vector.tensor_tensor(dst[:, k, :], x[:, k, :], rstd[:, :], ALU.mult).then_inc(dve_to_act.sem, 1)
                    if k >= 2:
                        low(k - 2)
                    if k in SPLIT_AT:
                        split(0, SPLIT_AT.index(k))
                low(KD - 2)
                low(KD - 1)

            def scalar(self, act, split):
                dst = self.dst
                ch = Chain(act, act_chain)
                for k in range(KD):
                    act.wait_ge(dve_to_act.sem, dve_to_act.v + k + 1)
                    for s, (a, b) in enumerate(((0, CTX), (CTX, T))):
                        n = ch.done(nc.scalar.activation(dst[:, k, a:b], dst[:, k, a:b], ACT.Identity,
                                                         bias=mod[:, self.shift_at + k, s:s + 1],
                                                         scale=mod[:, self.scale_at + k, s:s + 1]))
                    ch.wait(n)
                    nc.scalar.activation(hhi[:, k, :], dst[:, k, :], ACT.Copy).then_inc(act_to_dve.sem, 1)
                    if k in SPLIT_AT:
                        split(0, SPLIT_AT.index(k))
                ch.n = 0

            def close(self):
                act_chain.v += 2 * KD
                for t in (dve_to_pe, dve_to_act, act_to_dve):
                    t.v += KD

        with ExitStack() as s_scope, nc.Block() as block:
            row = sb(s_scope, "row", [P, RING, CTX + 2])
            grid = sb(s_scope, "grid", [P, RING, GRID_H + 2, GRID_W + 2])
            near = sb(s_scope, "near", [P, T])
            near2 = sb(s_scope, "near2", [P, LAT])
            mu1 = sb(s_scope, "mu1", [P, 3, NSHIFT])
            z_padded = sem("z_padded")
            borders = sem("borders")
            shifted = sem("shifted", RING)
            g3 = near2[:, :].rearrange("p (h w) -> p h w", w=GRID_W)
            n3 = near[:, CTX:T].rearrange("p (h w) -> p h w", w=GRID_W)

            m1 = Modulate(hf, 0, 16)

            @block.sync
            def _(sp):
                st.load(sp, NSHIFT, w_in)

            @block.tensor
            def _(pe):
                for u in range(RING):
                    st.product(pe, 0, u, ps[:, u, 0:T], None if u else dve_to_pe)
                with pe.Fori(1, NSHIFT // RING) as it:
                    for u in range(RING):
                        st.product(pe, it, u, ps[:, u, 0:T])

            @block.gpsimd
            def _(pool):
                nc.gpsimd.memset(row[:, :, :], 0.0).then_inc(borders.sem, 1)
                nc.gpsimd.memset(grid[:, :, :, :], 0.0).then_inc(borders.sem, 1)

            @block.scalar
            def _(act):
                act.sem_inc(shifted.sem, RING)
                m1.scalar(act, lambda it, n: st.high(act, it, n))
                act.wait_ge(borders.sem, 3)

                def drain(it, u):
                    j = it * RING + u
                    act.wait_ge(product_ready.sem, it * RING + product_ready.v + u + 1)
                    act.wait_ge(shifted.sem, it * RING + u + 1)
                    nc.scalar.activation(z[:, bass.ds(j, 1), :].rearrange("p o t -> p (o t)"), ps[:, u, 0:T],
                                         ACT.Copy, scale=mu1[:, 0, bass.ds(j, 1)])
                    nc.scalar.activation(row[:, u, 1:CTX + 1], ps[:, u, 0:CTX], ACT.Copy)
                    nc.scalar.activation(grid[:, u, 1:GRID_H + 1, 1:GRID_W + 1],
                                         ps[:, u, CTX:T].rearrange("p (h w) -> p h w", w=GRID_W),
                                         ACT.Copy).then_inc(bank_free.sem, 1)

                st.ahead(act, NSHIFT, lambda it, n: st.high(act, it, n), drain, started=True)

            @block.vector
            def _(dve):
                ch = Chain(dve, dve_chain)
                nc.vector.tensor_scalar(mu1[:, 1, :], col("mu", 0, NSHIFT), 0.5, None, ALU.mult)
                nc.vector.tensor_scalar(mu1[:, 2, :], col("mu", 0, NSHIFT), 0.25, None, ALU.mult)
                ch.link(nc.vector.tensor_scalar(mu1[:, 0, :], col("mu", 0, NSHIFT), -1.0, 1.0, ALU.mult, ALU.add))
                dve.sem_inc(borders.sem, 1)
                ch.close()
                m1.vector(dve, lambda it, n: st.low(dve, it, n))

                def drain(it, u):
                    ch = Chain(dve, dve_chain, it, 4 * RING)
                    ch.n = 4 * u
                    j = it * RING + u
                    dve.wait_ge(bank_free.sem, it * RING + bank_free.v + u + 1)
                    dve.wait_ge(shifted.sem, it * RING + u + RING)
                    gr = grid[:, u]
                    ch.done(nc.vector.tensor_tensor(near[:, 0:CTX], row[:, u, 0:CTX], row[:, u, 2:CTX + 2], ALU.add))
                    ch.done(nc.vector.tensor_tensor(n3, gr[:, 0:GRID_H, 1:GRID_W + 1], gr[:, 2:GRID_H + 2, 1:GRID_W + 1], ALU.add))
                    b = ch.done(nc.vector.tensor_tensor(g3, gr[:, 1:GRID_H + 1, 0:GRID_W], gr[:, 1:GRID_H + 1, 2:GRID_W + 2], ALU.add))
                    ch.wait(b)
                    ch.done(nc.vector.tensor_tensor(near[:, CTX:T], near[:, CTX:T], near2[:, :], ALU.add))
                    zc = z[:, bass.ds(j, 1), 0:CTX].rearrange("p o t -> p (o t)")
                    zl = z[:, bass.ds(j, 1), CTX:T].rearrange("p o t -> p (o t)")
                    nc.vector.scalar_tensor_tensor(out=zc, in0=near[:, 0:CTX], scalar=mu1[:, 1, bass.ds(j, 1)], in1=zc,
                                                   op0=ALU.mult, op1=ALU.add)
                    ch.wait()
                    nc.vector.scalar_tensor_tensor(out=zl, in0=near[:, CTX:T], scalar=mu1[:, 2, bass.ds(j, 1)], in1=zl,
                                                   op0=ALU.mult, op1=ALU.add).then_inc(shifted.sem, 1)

                st.ahead(dve, NSHIFT, lambda it, n: st.low(dve, it, n), drain, started=True)
            m1.close()
            dve_chain.v += 4 * NSHIFT
            st.close(NSHIFT)

        with nc.Block() as block:
            NB = NIN - NSHIFT

            @block.sync
            def _(sp):
                st.load(sp, NB, w_in[NSHIFT:NIN])

            @block.tensor
            def _(pe):
                with pe.Fori(0, NB // RING) as it:
                    for u in range(RING):
                        st.product(pe, it, u, ps[:, u, 0:T])

            @block.scalar
            def _(act):
                def drain(it, u):
                    act.wait_ge(product_ready.sem, it * RING + product_ready.v + u + 1)
                    nc.scalar.activation(z[:, bass.ds(it * RING + u + Z_U, 1), :].rearrange("p o t -> p (o t)"),
                                         ps[:, u, 0:T], ACT.Gelu_apprx_tanh).then_inc(bank_free.sem, 1)

                st.ahead(act, NB, lambda it, n: st.high(act, it, n), drain)

            @block.vector
            def _(dve):
                st.ahead(dve, NB, lambda it, n: st.low(dve, it, n), lambda it, n: None)
            st.close(NB)
        b_scope.close()

        g_scope = ExitStack()
        wide = sb(g_scope, "wide", [P, HB, T])
        kk = sb(g_scope, "kk", [P, PAIRS, T])
        ka1 = sb(g_scope, "ka1", [P, PAIRS])
        with ExitStack() as c_scope, nc.Block() as block:
            wsp = sb(c_scope, "wsp", [P, HB, P])
            bsp = sb(c_scope, "bsp", [P, HB, P])
            mean = sb(c_scope, "mean", [P, T])
            vn = sb(c_scope, "vn", [P, RING, T])
            vt = sb(c_scope, "vt", [P, RING, T])
            spb = sb(c_scope, "spb", [P, RING, T])
            norm = sb(c_scope, "norm", [P, PAIRS, T])
            over = sb(c_scope, "over", [P, RING, T])
            kk_raw, kk_sq, kk_sum, kk_norm = sem("kk_raw"), sem("kk_sq"), sem("kk_sum"), sem("kk_norm", 2)
            vz = z[:, Z_VG:Z_VG + HB, :]
            vn_ready, vn_turned, vt_ready = sem("vn_ready"), sem("vn_turned", RING), sem("vt_ready")
            mixed, gated = sem("mixed", RING), sem("gated", RING)

            def over_heads(t):
                return t.rearrange("p (o t) -> p o t", o=1).to_broadcast([P, HB, T])

            @block.sync
            def _(sp):
                sp.dma_start(wsp[:, :, :], w_s).then_inc(loads.sem, 16)
                sp.dma_start(bsp[:, :, :], b_s.to_broadcast([P, HB, P])).then_inc(loads.sem, 16)

            @block.tensor
            def _(pe):
                pe.sem_inc(vn_turned.sem, RING)
                pe.sem_inc(mixed.sem, RING)
                for j in range(HB):
                    last = pe.matmul(ps[:, 0, 0:T], table("mean_db"), vz[:, j, :], start=(j == 0), stop=(j == HB - 1))
                last.then_inc(pe_to_dve.sem, 1)
                with pe.Fori(0, PAIRS // 2) as it:
                    for u in range(2):
                        pe.wait_ge(kk_sq.sem, it * 2 + u + 1)
                        pe.wait_ge(kk_norm.sem, it * 2 + u + 1)
                        pe.matmul(ps[:, 6 + u, 0:T], table("head_sum"), norm[:, bass.ds(it * 2 + u, 1), :].rearrange("p o t -> p (o t)"),
                                  start=True, stop=True).then_inc(kk_sum.sem, 1)
                pe.wait_ge(act_to_pe.sem, act_to_pe.v + 1)
                for j in range(HB):
                    last = pe.matmul(ps[:, 1, 0:T], table("mean_db"), wide[:, j, :], start=(j == 0), stop=(j == HB - 1))
                last.then_inc(pe_to_act.sem, 1)
                pe.wait_ge(loads.sem, loads.v + 32)
                with pe.Fori(0, HB // RING) as it:
                    for u in range(RING):
                        pe.wait_ge(vn_ready.sem, it * RING + u + 1)
                        pe.wait_ge(vt_ready.sem, it * RING + u + 1)
                        for c in range(TILES):
                            last = pe.transpose(ps[:, 2 + u, c * P:(c + 1) * P], vn[:, u, c * P:(c + 1) * P], table("ident"))
                        last.then_inc(vn_turned.sem, 1)
                    for u in range(RING):
                        pe.wait_ge(vt_ready.sem, it * RING + RING + u + 1)
                        pe.wait_ge(gated.sem, it * RING + u + 1)
                        for c in range(TILES):
                            last = pe.matmul(ps[:, 4 + u, c * P:(c + 1) * P], vt[:, u, c * P:(c + 1) * P],
                                             wsp[:, bass.ds(it * RING + u, 1), :].rearrange("p o q -> p (o q)"),
                                             start=True, stop=True)
                        last.then_inc(mixed.sem, 1)

            @block.scalar
            def _(act):
                act.sem_inc(vt_ready.sem, RING)
                act.sem_inc(kk_norm.sem, 2)
                with act.Fori(0, PAIRS) as it:
                    act.wait_ge(kk_raw.sem, it + 1)
                    nc.scalar.activation(norm[:, bass.ds(it, 1), :], kk[:, bass.ds(it, 1), :], ACT.Square).then_inc(kk_sq.sem, 1)
                with act.Fori(0, PAIRS // 2) as it:
                    for u in range(2):
                        act.wait_ge(kk_sum.sem, it * 2 + u + 1)
                        nc.scalar.activation(norm[:, bass.ds(it * 2 + u, 1), :].rearrange("p o t -> p (o t)"), ps[:, 6 + u, 0:T], ACT.Sqrt
                                             ).then_inc(kk_norm.sem, 1)
                act.wait_ge(dve_to_act.sem, dve_to_act.v + 1)
                nc.scalar.activation(wide[:, :, :], vz, ACT.Square).then_inc(act_to_pe.sem, 1)
                act.wait_ge(pe_to_act.sem, pe_to_act.v + 1)
                nc.scalar.activation(rstd[:, :], ps[:, 1, 0:T], ACT.Sqrt, bias=eps[:, 0:1]).then_inc(act_to_dve.sem, 1)
                with act.Fori(0, HB // RING) as it:
                    for u in range(RING):
                        act.wait_ge(vn_turned.sem, it * RING + RING + u + 1)
                        act.wait_ge(mixed.sem, it * RING + u + 1)
                        nc.scalar.activation(vt[:, u, :], ps[:, 2 + u, 0:T], ACT.Copy).then_inc(vt_ready.sem, 1)
                nc.scalar.activation(z[:, Z_LW, :], z[:, Z_LW, :], ACT.Tanh)
                gz = z[:, Z_G:Z_G + PAIRS, :]
                nc.scalar.activation(gz, gz, ACT.Sigmoid)

            @block.vector
            def _(dve):
                ch = Chain(dve, dve_chain)
                dve.sem_inc(gated.sem, RING)
                ch.done(nc.vector.tensor_scalar(ka1[:, :], col("k_a", 0, PAIRS), -1.0, 1.0, ALU.mult, ALU.add))
                with dve.Fori(0, PAIRS) as it:
                    nc.vector.tensor_scalar(kk[:, bass.ds(it, 1), :], z[:, bass.ds(it + Z_K, 1), :],
                                            cols[:, bass.ds(it + COLS["k_k"][0], 1)], None, ALU.mult
                                            ).then_inc(kk_raw.sem, 1)
                dve.wait_ge(pe_to_dve.sem, pe_to_dve.v + 1)
                ch.link(nc.vector.tensor_copy(mean[:, :], ps[:, 0, 0:T]))
                nc.vector.tensor_tensor(vz, vz, over_heads(mean[:, :]), ALU.subtract).then_inc(dve_to_act.sem, 1)
                dve.wait_ge(act_to_dve.sem, act_to_dve.v + 1)
                ch.link(nc.vector.reciprocal(rstd[:, :], rstd[:, :]))
                ch.link(nc.vector.tensor_tensor(vz, vz, over_heads(rstd[:, :]), ALU.mult))
                ch.close()
                dve.wait_ge(loads.sem, loads.v + 32)
                with dve.Fori(0, HB // RING) as it:
                    ch = Chain(dve, dve_chain, it, RING + 3)
                    for u in range(RING):
                        j = it * RING + u
                        dve.wait_ge(vn_turned.sem, it * RING + u + 1)
                        nc.vector.tensor_scalar(vn[:, u, :], z[:, bass.ds(j + Z_VG, 1), :].rearrange("p o t -> p (o t)"),
                                                cols[:, bass.ds(j + COLS["ln_v_w"][0], 1)],
                                                cols[:, bass.ds(j + COLS["ln_v_b"][0], 1)],
                                                ALU.mult, ALU.add).then_inc(vn_ready.sem, 1)
                    dve.wait_ge(kk_norm.sem, it * RING + 2 + RING)
                    nm, kn = norm[:, bass.ds(it * RING, RING), :], kk[:, bass.ds(it * RING, RING), :]
                    ch.link(nc.vector.tensor_scalar(over[:, :, :], nm, 1e-12, None, ALU.max))
                    ch.link(nc.vector.reciprocal(over[:, :, :], over[:, :, :]))
                    ch.link(nc.vector.tensor_tensor(kn, kn, over[:, :, :], ALU.mult))
                    for u in range(RING):
                        j = it * RING + u
                        dve.wait_ge(mixed.sem, it * RING + RING + u + 1)
                        dve.wait_ge(gated.sem, it * RING + RING + u)
                        ch.link(nc.vector.tensor_tensor(
                            spb[:, u, :].rearrange("p (c q) -> p c q", c=TILES),
                            ps[:, 4 + u, 0:T].rearrange("p (c q) -> p c q", c=TILES),
                            bsp[:, bass.ds(j, 1), :].to_broadcast([P, TILES, P]), ALU.add))
                        uz = z[:, bass.ds(j + Z_U, 1), :].rearrange("p o t -> p (o t)")
                        nc.vector.tensor_tensor(uz, uz, spb[:, u, :], ALU.mult).then_inc(gated.sem, 1)
                ch.close(HB // RING)
            loads.v += 32
            pe_to_dve.v += 1
            act_to_pe.v += 1
            pe_to_act.v += 1
            dve_to_act.v += 1
            act_to_dve.v += 1

        with nc.Block() as block:
            @block.gpsimd
            def _(pool):
                nc.gpsimd.memset(z[:, Z_VG:Z_VG + HB, :], 0.0)

        with ExitStack() as d_scope, nc.Block() as block:
            def buf(name, shape):
                return sb(d_scope, name, shape)

            GR = 4
            lora = buf("lora", [P, 2, P])
            s_in = buf("s_in", [P, 2, HEAD])
            s_new = buf("s_new", [P, 2, HEAD])
            vs = buf("vs", [P, T])
            sg = [buf(f"sg{d}", [P, T]) for d in range(2)]
            aa = [buf(f"aa{d}", [P, T]) for d in range(2)]
            cum = buf("cum", [P, T])
            bon = buf("bon", [P, T])
            cen = [buf(f"cen{d}", [P, T]) for d in range(2)]
            cex = [buf(f"cex{d}", [P, T]) for d in range(2)]
            fac = [[sg[0], cex[0], buf("fac0", [P, T])], [sg[1], cen[1], buf("fac1", [P, T])]]
            tot = [buf(f"tot{d}", [P, TILES]) for d in range(2)]
            half_next = [buf(f"halfnext{d}", [P, TILES]) for d in range(2)]
            half = [buf(f"half{d}", [P, TILES]) for d in range(2)]
            half2 = [buf(f"halftwo{d}", [P, 1]) for d in range(2)]
            kd = [buf(f"kd{d}", [P, T]) for d in range(2)]
            bq = aa
            kq = [fac[0][2], fac[1][2]]
            alone = z[:, Z_VG:Z_VG + 8, :].rearrange("p (b d h) t -> p b d h t", b=2, d=2)
            kr = [buf(f"kr{d}", [P, TILES, 2, P]) for d in range(2)]
            G = buf("G", [P, GR, TILES, 4, P])
            free = wide[:, :, :].rearrange("p b t -> p (b t)").rearrange("p (n g a t) -> p n g a t", n=2, g=GR, a=TILES)
            tn = free[:, 0]
            xl = free[:, 1].rearrange("p g a t -> p (g a t)")[:, 0:GR * TILES * HEAD].rearrange(
                "p (g a t) -> p g a t", g=GR, a=TILES)
            tt = buf("tt", [P, GR, TILES, P])
            vtok = buf("vtok", [P, T])
            btok = [buf(f"btok{d}", [P, 2, 2, P]) for d in range(2)]
            rs = [buf(f"rs{d}", [P, 2, 2, HEAD]) for d in range(2)]
            stm = [buf(f"stm{d}", [P, P]) for d in range(2)]
            sa_ = [buf(f"sa{d}", [P, TILES, 2, HEAD]) for d in range(2)]
            s0 = [buf(f"s0_{d}", [P, 2, P]) for d in range(2)]
            TURN = [(0, 1, 2), (0, 2, 1)]
            heads = [slice(0, HEAD), slice(HEAD, P)]
            LEVELS = (2, 4, 8, 16, 32, 64)
            NL = len(LEVELS)

            def signal(name, per):
                return Signal(sem(name), per)

            pass_done = sem("pass_done", 1)
            lora_landed, state_landed = sem("lora_landed"), sem("state_landed")
            v_copied, gates_in, gates = signal("v_copied", 1), signal("gates_in", 4), signal("gates", 4)
            centred, factors = signal("centred", 2), signal("factors", 2)
            multiplied, alone_ready = signal("multiplied", 4), signal("alone_ready", 2)
            halves, operands = signal("halves", 2), signal("operands", 2)
            bonus_in, bonus_sum, bonus_used = signal("bonus_in", 1), signal("bonus_sum", 1), signal("bonus_used", 1)
            scores, scores_masked = signal("scores", 12), signal("scores_masked", 12)
            init_ready = signal("init_ready", GR)
            turned, tn_ready = signal("tn_turned", GR), signal("tn_ready", GR)
            xs_, xm = signal("x_products", NL * GR), signal("x_masked", NL * GR)
            tps, tadds = signal("t_products", NL * GR), signal("t_added", NL * GR)
            tt_turned, tt_ready = signal("tt_turned", NL * GR), signal("tt_ready", NL * GR)
            toks, toks_ready = signal("tokens_turned", 3), signal("tokens_ready", 3)
            starts = signal("starts", 4)
            rhs_in, rhs_ready = signal("rhs_in", 4), signal("rhs_ready", 4)
            solved, solved_ready = signal("solved", 4), signal("solved_ready", 4)
            state_sum = signal("state_sum", 2)
            state_out_ready = signal("state_out_ready", 4)
            y_sum = signal("y_sum", 1)
            every = [v_copied, gates_in, gates, centred, factors, multiplied, alone_ready, halves, operands, bonus_in,
                     bonus_sum, bonus_used, scores, scores_masked, init_ready, turned, tn_ready, xs_, xm, tps, tadds, tt_turned,
                     tt_ready, toks, toks_ready, starts, rhs_in, rhs_ready, solved, solved_ready, state_sum,
                     state_out_ready, y_sum]
            front_chain = sem("front_chain")

            def zb(first, it):
                return z[:, bass.ds(it + first, 1), :].rearrange("p o t -> p (o t)")

            def colr(name, it, more=0):
                return cols[:, bass.ds(it + (COLS[name][0] + more), 1)]

            def tiled(t):
                return t.rearrange("p (a t) -> p a t", a=TILES)

            def early(t, g, b):
                return t.rearrange("p (a n s b) -> p a n s b", n=HEAD // b, s=2, b=b)[:, :, :, g // 2, :]

            def dense(t, b):
                return t.rearrange("p (a n b) -> p a n b", n=HEAD // b, b=b)

            ENGINES = 5

            def begin(eng, it):
                eng.wait_ge(pass_done.sem, it * ENGINES + 1)

            def end(eng):
                eng.drain().then_inc(pass_done.sem, 1)

            @block.sync
            def _(sp):
                def load_lora(it):
                    sp.dma_start(lora[:, :, :], w2a2[bass.ds(it, 1)].rearrange("o p a c -> (o p) a c")
                                 ).then_inc(lora_landed.sem, 16)

                def one(it, front):
                    begin(sp, it)
                    sp.dma_start(s_in[:, :, :], state_t[bass.ds(it, 1)].rearrange("o p a c -> (o p) a c")
                                 ).then_inc(state_landed.sem, 16)
                    if front:
                        gates_in.wait(sp, it, 4)
                        load_lora(it + 1)
                    state_out_ready.wait(sp, it, 4)
                    sp.dma_start(state_out[bass.ds(it, 1)].rearrange("o p a c -> (o p) a c"), s_new[:, :, :]
                                 ).then_inc(stores.sem, 16)
                    sp.wait_ge(stores.sem, it * 16 + stores.v + 16)
                    sp.sem_inc(pass_done.sem, 1)

                load_lora(0)
                sp.sem_inc(pass_done.sem, 1)
                with sp.Fori(0, PAIRS - 1) as it:
                    one(it, True)
                one(PAIRS - 1, False)

            @block.gpsimd
            def _(pool):
                with pool.Fori(0, PAIRS) as it:
                    begin(pool, it)
                    v_copied.inc(nc.gpsimd.tensor_copy(vs[:, :], zb(Z_V, it)))
                    ch = Chain(pool, pool_chain, it, GR)
                    for g in range(GR):
                        d = g // 2
                        scores_masked.wait(pool, it, TILES * (g + 1))
                        m = scan_tables(f"two{d}").to_broadcast([P, TILES, P])
                        e = tab[:, TABLE_NAMES.index("ident"):TABLE_NAMES.index("ident") + 1, :].to_broadcast([P, TILES, P])
                        ch.link(nc.gpsimd.tensor_tensor(tt[:, g], G[:, g, :, 0, :], m, ALU.mult))
                        init_ready.inc(nc.gpsimd.tensor_tensor(tt[:, g], tt[:, g], e, ALU.add))
                    ch.close(PAIRS)
                    end(pool)

            @block.scalar
            def _(act):
                K = EXP_HALF

                def front_gates(it, d):
                    gates_in.wait(act, it, 2 * d + 1)
                    gates.inc(nc.scalar.activation(sg[d][:, :], ps[:, 6, 0:T], ACT.Sigmoid, bias=colr("w0", it, PAIRS * d)))
                    gates_in.wait(act, it, 2 * d + 2)
                    gates.inc(nc.scalar.activation(aa[d][:, :], ps[:, 7, 0:T], ACT.Sigmoid, bias=colr("a0", it, PAIRS * d)))

                def front_factors(it, d):
                    centred.wait(act, it, d + 1)
                    srcs = ((cen[d], -K), (cex[d], -K), (cen[d], K)) if d == 0 else ((cex[d], K), (cen[d], K), (cex[d], -K))
                    for i, (src, sc) in enumerate(srcs):
                        nc.scalar.activation(fac[d][i][:, :], src[:, :], ACT.Exp, scale=sc)
                    factors.inc(nc.scalar.activation(half_next[d][:, :], tot[d][:, :], ACT.Exp, scale=-K))

                def front_alone(it, d):
                    for b, src in enumerate((bq[d], kq[d])):
                        multiplied.wait(act, it, 2 * d + b + 1)
                        for hh in range(2):
                            last = nc.scalar.activation(alone[heads[hh], b, d, hh, :], src[heads[hh], :], ACT.Copy)
                    alone_ready.inc(last)

                def one(it, more):
                    begin(act, it)
                    for d in range(2):
                        toks.wait(act, it, 1 + d)
                        toks_ready.inc(nc.scalar.activation(btok[d][:, :, :, :].rearrange("p a b c -> p (a b c)"),
                                                            ps[:, 1 + d, :], ACT.Copy))
                    toks.wait(act, it, 3)
                    toks_ready.inc(nc.scalar.activation(vtok[:, :], ps[:, 0, 0:T], ACT.Copy))
                    for g in range(GR):
                        turned.wait(act, it, g + 1)
                        tn_ready.inc(nc.scalar.activation(tn[:, g], tiled(ps[:, 4 + g % 2, 0:T]), ACT.Copy))
                    if more:
                        operands.wait(act, it, 2)
                        halves.wait(act, it, 2)
                        front_gates(it + 1, 0)
                    for n in range(NL * GR):
                        g = n % GR
                        tt_turned.wait(act, it, n + 1)
                        tt_ready.inc(nc.scalar.activation(tt[:, g], tiled(ps[:, 4 + g % 2, 0:T]), ACT.Copy))
                        if more:
                            if n == 0:
                                front_gates(it + 1, 1)
                            elif n in (7, 11):
                                front_factors(it + 1, n // 4 - 1)
                            elif n in (16, 21):
                                front_alone(it + 1, (n - 16) // 5)
                    for turn, w in ((0, 2), (2, 1)):
                        n = 0 if turn == 0 else 1
                        for d in range(2):
                            rhs_in.wait(act, it, 2 * n + d + 1)
                            rhs_ready.inc(nc.scalar.activation(rs[d][:, 0:w], ps[:, 0 + d, 0:P * w].rearrange("p (a h v) -> p a h v", a=w, h=2), ACT.Copy))
                        for d in range(2):
                            solved.wait(act, it, 2 * n + d + 1)
                            solved_ready.inc(nc.scalar.activation(sa_[d][:, turn:turn + w],
                                                                  ps[:, 2 + d, 0:P * w].rearrange("p (a h v) -> p a h v", a=w, h=2), ACT.Copy))
                    y_sum.wait(act, it, 1)
                    nc.scalar.activation(zb(Z_R, it), ps[:, 5, 0:T], ACT.Copy)
                    end(act)

                for step in (front_gates, front_factors, front_alone):
                    for d in range(2):
                        step(0, d)
                with act.Fori(0, PAIRS - 1) as it:
                    one(it, True)
                one(PAIRS - 1, False)

            @block.vector
            def _(dve):
                FRONT = 20

                def front_step(it, n):
                    d = n // 4 if n < 8 else (n - 8) // 5
                    fc = Chain(dve, front_chain, it, FRONT)
                    if n < 8:
                        k = n % 4
                        fc.n = 7 * d + (0, 3, 4, 7)[k]
                        if k == 0:
                            gates.wait(dve, it, 2 * d + 1)
                            if d:
                                fc.wait(7)
                            for i in range(TILES):
                                c = slice(i * P, (i + 1) * P)
                                fc.done(nc.vector.tensor_tensor_scan(cum[:, c], table("ones"), sg[d][:, c], 0.0, ALU.mult, ALU.add))
                        elif k == 1:
                            fc.wait()
                            fc.done(nc.vector.tensor_scalar(tot[d][:, :], cum[:, P - 1:T:P], 0.5, None, ALU.mult))
                        elif k == 2:
                            fc.wait()
                            for i in range(TILES):
                                c = slice(i * P, (i + 1) * P)
                                fc.done(nc.vector.tensor_scalar(cen[d][:, c], cum[:, c], tot[d][:, i:i + 1], None, ALU.subtract))
                        else:
                            fc.wait()
                            centred.inc(nc.vector.tensor_tensor(cex[d][:, :], cen[d][:, :], sg[d][:, :], ALU.subtract))
                    else:
                        k = (n - 8) % 5
                        fc.n = 14 + 3 * d + k
                        if k == 0:
                            gates.wait(dve, it, 2 * d + 2)
                            fc.done(nc.vector.tensor_scalar(kd[d][:, :], aa[d][:, :], colr("k_a", it), ka1[:, bass.ds(it, 1)], ALU.mult, ALU.add))
                        elif k == 1:
                            fc.wait()
                            fc.done(nc.vector.tensor_tensor(kd[d][:, :], kd[d][:, :], zb(Z_K, it), ALU.mult))
                        elif k == 2:
                            fc.done(nc.vector.tensor_tensor(aa[d][:, :], kk[:, bass.ds(it, 1), :].rearrange("p o t -> p (o t)"),
                                                            aa[d][:, :], ALU.mult))
                        elif k == 3:
                            factors.wait(dve, it, d + 1)
                            fc.wait()
                            multiplied.inc(nc.vector.tensor_tensor(bq[d][:, :], aa[d][:, :], fac[d][2][:, :], ALU.mult))
                        else:
                            multiplied.wait(dve, it, 2 * d + 1)
                            multiplied.inc(nc.vector.tensor_tensor(kq[d][:, :], kd[d][:, :], fac[d][2][:, :], ALU.mult))

                def one(it, more):
                    begin(dve, it)
                    ch = Chain(dve, dve_chain, it, 7)
                    factors.wait(dve, it, 2)
                    for d in range(2):
                        halves.inc(nc.vector.tensor_copy(half[d][:, :], half_next[d][:, :]))
                    for d in range(2):
                        ch.done(nc.vector.scalar_tensor_tensor(
                            out=kr[d][:, :, 0, :], in0=kk[:, bass.ds(it, 1), :].rearrange("p o (a t) -> p (o a) t", a=TILES),
                            scalar=-1.0, in1=tiled(fac[d][1][:, :]), op0=ALU.mult, op1=ALU.mult))
                        ch.wait()
                        operands.inc(nc.vector.tensor_tensor(
                            kr[d][:, :, 1, :], z[:, bass.ds(it, 1), :].rearrange("p o (a t) -> p (o a) t", a=TILES),
                            tiled(fac[d][0][:, :]), ALU.mult))
                    ch.link(nc.vector.tensor_tensor(kd[0][:, :], kd[0][:, :], kd[1][:, :], ALU.add))
                    bonus_in.inc(nc.vector.scalar_tensor_tensor(out=bon[:, :], in0=kd[0][:, :], scalar=colr("r_k", it), in1=zb(Z_R, it),
                                                                op0=ALU.mult, op1=ALU.mult))
                    for n in range(12):
                        g, tile = n // TILES, n % TILES
                        scores.wait(dve, it, n + 1)
                        scores_masked.inc(nc.vector.tensor_tensor(G[:, g, tile], ps[:, 6 + n % 2, :].rearrange("p (a t) -> p a t", a=4),
                                                                  scan_tables(f"ab{g // 2}", 4), ALU.mult))
                    dve.wait_ge(state_landed.sem, it * 16 + 16)
                    halves.wait(dve, it, 2)
                    for d in range(2):
                        f, l = TURN[d][1], TURN[d][2]
                        starts.inc(nc.vector.scalar_tensor_tensor(
                            out=s0[d][:, 0, :].rearrange("p (h v) -> p h v", h=2), in0=s_in[:, d:d + 1, :].to_broadcast([P, 2, HEAD]),
                            scalar=half[d][:, f:f + 1], in1=table("head_sum").rearrange("p (h v) -> p h v", h=2),
                            op0=ALU.mult, op1=ALU.mult))
                        ch.done(nc.vector.tensor_tensor(half2[d][:, :], half[d][:, f:f + 1], half[d][:, l:l + 1], ALU.mult))
                    bonus_sum.wait(dve, it, 1)
                    v_copied.wait(dve, it, 1)
                    bonus_used.inc(nc.vector.tensor_tensor(zb(Z_K, it), ps[:, 3, 0:T], vs[:, :], ALU.mult))
                    if more:
                        operands.wait(dve, it, 2)
                        bonus_in.wait(dve, it, 1)
                    for lv, b in enumerate(LEVELS):
                        for g in range(GR):
                            xs_.wait(dve, it, lv * GR + g + 1)
                            mask = scan_tables(f"half{g // 2}_{b}")[:, 0, :]
                            xm.inc(nc.vector.tensor_tensor(
                                dense(xl[:, g].rearrange("p a t -> p (a t)"), b), dense(ps[:, g % 2, 0:TILES * HEAD], b),
                                early(mask, g, b).to_broadcast([P, TILES, HEAD // b, b]), ALU.mult))
                        for g in range(GR):
                            tps.wait(dve, it, lv * GR + g + 1)
                            t = early(tn[:, g].rearrange("p a t -> p (a t)"), g, b)
                            tadds.inc(nc.vector.tensor_tensor(t, dense(ps[:, 2 + g % 2, 0:TILES * HEAD], b), t, ALU.add))
                            if more and 2 <= lv * GR + g < 20:
                                front_step(it + 1, lv * GR + g - 2)
                    for d in range(2):
                        state_sum.wait(dve, it, d + 1)
                        for hh in range(2):
                            state_out_ready.inc(nc.vector.tensor_scalar(
                                s_new[heads[hh], d, :], ps[heads[hh], 6 + d, hh * HEAD:(hh + 1) * HEAD],
                                half[d][heads[hh], 0:1], None, ALU.mult))
                        starts.wait(dve, it, 2)
                        ch.link(nc.vector.tensor_tensor(stm[d][:, :], ps[:, 6 + d, P:2 * P], s0[d][:, 0, :], ALU.add))
                        starts.inc(nc.vector.scalar_tensor_tensor(out=s0[d][:, 1, :], in0=stm[d][:, :], scalar=half2[d][:, 0:1],
                                                                  in1=table("head_sum"), op0=ALU.mult, op1=ALU.mult))
                    end(dve)

                for n in range(18):
                    front_step(0, n)
                with dve.Fori(0, PAIRS - 1) as it:
                    one(it, True)
                one(PAIRS - 1, False)
                dve_chain.v += 7 * PAIRS

            @block.tensor
            def _(pe):
                def front(it, n):
                    if n == 0:
                        pe.wait_ge(lora_landed.sem, it * 16 + 16)
                    if n >= 2:
                        gates.wait(pe, it, n - 1)
                    r = slice(64 * (n // 2), 64 * (n // 2) + 64)
                    gates_in.inc(pe.matmul(ps[:, 6 + n % 2, 0:T], lora[r, n % 2, :], z[r, (Z_LW, Z_LA)[n % 2], :], start=True, stop=True))

                def one(it, more):
                    begin(pe, it)
                    for d in range(2):
                        multiplied.wait(pe, it, 2 * d + 2)
                        for j in range(2):
                            c = slice(TURN[d][j] * P, (TURN[d][j] + 1) * P)
                            pe.transpose(ps[:, 1 + d, 2 * j * P:(2 * j + 1) * P], bq[d][:, c], table("ident"))
                            last = pe.transpose(ps[:, 1 + d, (2 * j + 1) * P:(2 * j + 2) * P], kq[d][:, c], table("ident"))
                        toks.inc(last)
                    v_copied.wait(pe, it, 1)
                    for i in range(TILES):
                        last = pe.transpose(ps[:, 0, i * P:(i + 1) * P], vs[:, i * P:(i + 1) * P], table("ident"))
                    toks.inc(last)
                    gates.wait(pe, it, 4)
                    for n in range(12):
                        g, tile = n // TILES, n % TILES
                        d, hh = g // 2, g % 2
                        c = slice(tile * P, (tile + 1) * P)
                        if n % 6 == 0:
                            operands.wait(pe, it, d + 1)
                            alone_ready.wait(pe, it, d + 1)
                        if n >= 2:
                            scores_masked.wait(pe, it, n - 1)
                        m = kr[d][:, tile, :, :].rearrange("p a t -> p (a t)")
                        pe.matmul(ps[:, 6 + n % 2, 0:2 * P], alone[:, 0, d, hh, c], m, start=True, stop=True)
                        scores.inc(pe.matmul(ps[:, 6 + n % 2, 2 * P:4 * P], alone[:, 1, d, hh, c], m, start=True, stop=True))
                    bonus_in.wait(pe, it, 1)
                    bonus_sum.inc(pe.matmul(ps[:, 3, 0:T], table("head_sum"), bon[:, :], start=True, stop=True))
                    scores_masked.wait(pe, it, 12)
                    for g in range(GR):
                        init_ready.wait(pe, it, g + 1)
                        if g >= 2:
                            tn_ready.wait(pe, it, g - 1)
                        for i in range(TILES):
                            last = pe.transpose(ps[:, 4 + g % 2, i * P:(i + 1) * P], tt[:, g, i], table("ident"))
                        turned.inc(last)
                        if more and g >= 2:
                            front(it + 1, g - 2)
                    toks_ready.wait(pe, it, 3)
                    tn_ready.wait(pe, it, GR)
                    last_y = [None]

                    def y_of(tile):
                        if tile:
                            for d in range(2):
                                pe.matmul(ps[:, 5, tile * P:(tile + 1) * P], s0[d][:, TURN[d].index(tile) - 1, :], kr[d][:, tile, 1, :],
                                          start=(d == 0), stop=False)
                        for hh in range(2):
                            out = ps[heads[hh], 5, tile * P:(tile + 1) * P]
                            for d in range(2):
                                g, turn = 2 * d + hh, TURN[d].index(tile)
                                pe.matmul(out, sa_[d][:, turn, hh, :], G[:, g, tile, 1, :], start=(d == 0 and tile == 0), stop=False)
                                last_y[0] = pe.matmul(out, vtok[:, tile * P + hh * HEAD:tile * P + (hh + 1) * HEAD], G[:, g, tile, 3, :],
                                                      start=False, stop=(d == 1))

                    def x_product(lv, g):
                        b = LEVELS[lv]
                        if lv * GR + g >= 2:
                            xm.wait(pe, it, lv * GR + g - 1)
                        for i in range(TILES):
                            last = pe.matmul(ps[:, g % 2, i * HEAD:(i + 1) * HEAD].rearrange("p (n b) -> p n b", b=b),
                                             G[:, g, i, 0, :], early(tn[:, g, i], g, b)[:, 0], start=True, stop=True)
                        xs_.inc(last)

                    for g in range(GR):
                        x_product(0, g)
                    if more:
                        front(it + 1, 2)
                        front(it + 1, 3)
                    bonus_used.wait(pe, it, 1)
                    for lv in range(NL):
                        for g in range(GR):
                            m = lv * GR + g
                            xm.wait(pe, it, m + 1)
                            if lv > 0:
                                tt_ready.wait(pe, it, m - GR + 1)
                            if m >= 2:
                                tadds.wait(pe, it, m - 1)
                            for i in range(TILES):
                                last = pe.matmul(ps[:, 2 + g % 2, i * HEAD:(i + 1) * HEAD], tt[:, g, i], xl[:, g, i], start=True, stop=True)
                            tps.inc(last)
                        for g in range(GR):
                            m = lv * GR + g
                            tadds.wait(pe, it, m + 1)
                            if m >= 2:
                                tt_ready.wait(pe, it, m - 1)
                            for i in range(TILES):
                                last = pe.transpose(ps[:, 4 + g % 2, i * P:(i + 1) * P], tn[:, g, i], table("ident"))
                            tt_turned.inc(last)
                            if lv < NL - 1:
                                x_product(lv + 1, g)
                    if more:
                        gates.wait(pe, it + 1, 4)
                    for turn, w in ((0, 2), (2, 1)):
                        n = 0 if turn == 0 else 1
                        for d in range(2):
                            starts.wait(pe, it, 2 * n + d + 1)
                            for j in range(w):
                                tile = TURN[d][turn + j]
                                if tile:
                                    pe.matmul(ps[:, d, j * P:(j + 1) * P], kr[d][:, tile, 0, :], s0[d][:, turn + j - 1, :],
                                              start=True, stop=False)
                                for hh in range(2):
                                    last = pe.matmul(ps[:, d, (2 * j + hh) * HEAD:(2 * j + hh + 1) * HEAD], G[:, 2 * d + hh, tile, 2, :],
                                                     vtok[:, tile * P + hh * HEAD:tile * P + (hh + 1) * HEAD],
                                                     start=(tile == 0), stop=(tile == 0 or hh == 1))
                            rhs_in.inc(last)
                        tt_ready.wait(pe, it, NL * GR)
                        for d in range(2):
                            rhs_ready.wait(pe, it, 2 * n + d + 1)
                            for j in range(w):
                                for hh in range(2):
                                    last = pe.matmul(ps[:, 2 + d, (2 * j + hh) * HEAD:(2 * j + hh + 1) * HEAD],
                                                     tt[:, 2 * d + hh, TURN[d][turn + j]], rs[d][:, j, hh, :], start=True, stop=True)
                            solved.inc(last)
                        if turn == 0:
                            for d in range(2):
                                solved_ready.wait(pe, it, d + 1)
                                for j in range(2):
                                    tile = TURN[d][j]
                                    out = ps[:, 6 + d, j * P:(j + 1) * P]
                                    pe.matmul(out, btok[d][:, j, 0, :], sa_[d][:, j, :, :].rearrange("p h v -> p (h v)"), start=True, stop=False)
                                    last = pe.matmul(out, btok[d][:, j, 1, :], vtok[:, tile * P:(tile + 1) * P], start=False, stop=True)
                                state_sum.inc(last)
                            y_of(0)
                    solved_ready.wait(pe, it, 4)
                    state_out_ready.wait(pe, it, 4)
                    for tile in range(1, TILES):
                        y_of(tile)
                    y_sum.inc(last_y[0])
                    end(pe)

                for n in range(4):
                    front(0, n)
                with pe.Fori(0, PAIRS - 1) as it:
                    one(it, True)
                one(PAIRS - 1, False)
            for sg_ in every:
                sg_.close(PAIRS)
            stores.v += 16 * PAIRS

        g_scope.close()

        def dump(name, *parts):
            with nc.Block() as block:
                @block.sync
                def _(sp):
                    for a, b, src in parts:
                        sp.dma_start(debug[name][:, a:b, :], src).then_inc(stores.sem, 16)
                        sp.wait_ge(stores.sem, stores.v + 16)
                        stores.v += 16

        if debug is not None and "z" in debug:
            dump("z", (0, NIN, z[:, :, :]))
            z_scope.close()
            return

        def stack_right(stack, name, shape, dt=F32):
            return stack.enter_context(nc.sbuf_tensor(name, shape, dt, side="right"))

        def square_root_of_mean(src, sq):
            with nc.Block() as block:
                @block.scalar
                def _(act):
                    for k in range(KD):
                        nc.scalar.activation(sq[:, k, :], src[:, k, :], ACT.Square).then_inc(act_to_pe.sem, 1)
                    act.wait_ge(pe_to_act.sem, pe_to_act.v + 1)
                    nc.scalar.activation(rstd[:, :], ps[:, 7, 0:T], ACT.Sqrt, bias=eps[:, 0:1]).then_inc(act_to_dve.sem, 1)

                @block.tensor
                def _(pe):
                    for k in range(KD):
                        pe.wait_ge(act_to_pe.sem, act_to_pe.v + 1 + k)
                        last = pe.matmul(ps[:, 7, 0:T], table("mean_d"), sq[:, k, :], start=(k == 0), stop=(k == KD - 1))
                    last.then_inc(pe_to_act.sem, 1)

                @block.vector
                def _(dve):
                    dve.wait_ge(act_to_dve.sem, act_to_dve.v + 1)
                    nc.vector.reciprocal(rstd[:, :], rstd[:, :])
            act_to_pe.v += KD
            pe_to_act.v += 1
            act_to_dve.v += 1

        def add_to_residual(branch, gate_at, squares=None, out=None):
            base = dve_chain.v
            SCALED = 2

            def summed(k):
                return base + min(k + 1 + SCALED, KD) + 2 * (k + 1)

            with nc.Block() as block:
                @block.vector
                def _(dve):
                    ch = Chain(dve, dve_chain)
                    scaled = {}

                    def scale(k):
                        scaled[k] = ch.done(nc.vector.tensor_tensor(branch[:, k, :], branch[:, k, :], rstd[:, :], ALU.mult))

                    for k in range(SCALED):
                        scale(k)
                    for k in range(KD):
                        if k + SCALED < KD:
                            scale(k + SCALED)
                        ch.wait(scaled[k])
                        for s_, (a, b) in enumerate(((0, CTX), (CTX, T))):
                            ch.done(nc.vector.scalar_tensor_tensor(out=x[:, k, a:b], in0=branch[:, k, a:b],
                                                                   scalar=mod[:, gate_at + k, s_:s_ + 1], in1=x[:, k, a:b],
                                                                   op0=ALU.mult, op1=ALU.add))
                    if squares is not None:
                        dve.wait_ge(act_to_dve.sem, act_to_dve.v + 1)
                        ch.done(nc.vector.reciprocal(rstd[:, :], rstd[:, :]))
                    ch.close()

                if squares is not None:
                    @block.scalar
                    def _(act):
                        for k in range(KD):
                            act.wait_ge(dve_chain.sem, summed(k))
                            nc.scalar.activation(squares[:, k, :], x[:, k, :], ACT.Square).then_inc(act_to_pe.sem, 1)
                        act.wait_ge(pe_to_act.sem, pe_to_act.v + 1)
                        nc.scalar.activation(rstd[:, :], ps[:, 7, 0:T], ACT.Sqrt, bias=eps[:, 0:1]).then_inc(act_to_dve.sem, 1)

                    @block.tensor
                    def _(pe):
                        for k in range(KD):
                            pe.wait_ge(act_to_pe.sem, act_to_pe.v + 1 + k)
                            last = pe.matmul(ps[:, 7, 0:T], table("mean_d"), squares[:, k, :], start=(k == 0), stop=(k == KD - 1))
                        last.then_inc(pe_to_act.sem, 1)
                    act_to_pe.v += KD
                    pe_to_act.v += 1
                    act_to_dve.v += 1

                if out is not None:
                    @block.sync
                    def _(sp):
                        for k in range(0, KD, 4):
                            sp.wait_ge(dve_chain.sem, summed(k + 3))
                            sp.dma_start(out[:, k:k + 4, :], x[:, k:k + 4, :]).then_inc(stores.sem, 16)
                        sp.wait_ge(stores.sem, stores.v + 16 * (KD // 4))
                    stores.v += 16 * (KD // 4)

        h_scope = ExitStack()
        hhi = stack_right(h_scope, "hhi2", [P, KD, T], F32R)
        hlo = stack_right(h_scope, "hlo2", [P, KD, T], F32R)
        w_scope = ExitStack()
        raw = stack_right(w_scope, "raw2", [P, RING, KD, P])
        whi = stack_right(w_scope, "whi2", [P, RING, KD, P], F32R)
        wlo = stack_right(w_scope, "wlo2", [P, RING, KD, P], F32R)
        st = Stream(RING, [raw[:, u] for u in range(RING)], [(whi[:, u], wlo[:, u]) for u in range(RING)])

        OUT_AT = Z_K
        mixed_out = z[:, OUT_AT:OUT_AT + KD, :]
        with nc.Block() as block:
            dev = z[:, Z_V:Z_V + PAIRS, :]
            gn_mean, gn_dev, gn_sq, gn_var = sem("gn_mean"), sem("gn_dev"), sem("gn_sq"), sem("gn_var")
            gn_root, gn_done, y_high = sem("gn_root"), sem("gn_done"), sem("y_high")
            y_ready, y_split, sq_added = sem("y_ready"), sem("y_split"), sem("sq_added")
            square_sum = z[:, Z_G, :]

            def flat(t):
                return t.rearrange("p o t -> p (o t)")

            @block.sync
            def _(sp):
                st.load(sp, KD, w_out)

            @block.tensor
            def _(pe):
                with pe.Fori(0, PAIRS) as it:
                    pe.matmul(flat(ps[:, bass.ds(it, 1), 0:T]), table("head_mean"), flat(z[:, bass.ds(it, 1), :]),
                              start=True, stop=True).then_inc(gn_mean.sem, 1)
                with pe.Fori(0, PAIRS) as it:
                    pe.wait_ge(gn_sq.sem, it + 1)
                    pe.matmul(flat(ps[:, bass.ds(it, 1), 0:T]), table("head_mean"), flat(z[:, bass.ds(it + Z_V, 1), :]),
                              start=True, stop=True).then_inc(gn_var.sem, 1)
                pe.wait_ge(y_split.sem, PAIRS + 1)
                with pe.Fori(0, KD // RING) as it:
                    for u in range(RING):
                        st.product(pe, it, u, ps[:, u, 0:T])
                pe.wait_ge(sq_added.sem, KD + 1)
                pe.matmul(ps[:, 7, 0:T], table("mean_d"), square_sum, start=True, stop=True).then_inc(pe_to_act.sem, 1)

            @block.gpsimd
            def _(pool):
                with pool.Fori(0, PAIRS) as it:
                    pool.wait_ge(gn_done.sem, it * 3 + 3)
                    y = z[:, bass.ds(it, 1), :]
                    nc.gpsimd.tensor_tensor(y, y, z[:, bass.ds(it + Z_K, 1), :], ALU.add).then_inc(pool_chain.sem, 1)
                    pool.wait_ge(pool_chain.sem, it + (pool_chain.v + 1))
                    nc.gpsimd.tensor_tensor(y, y, z[:, bass.ds(it + Z_G, 1), :], ALU.mult).then_inc(y_ready.sem, 1)

            @block.scalar
            def _(act):
                with act.Fori(0, PAIRS) as it:
                    act.wait_ge(gn_dev.sem, it + 1)
                    nc.scalar.activation(z[:, bass.ds(it + Z_V, 1), :], z[:, bass.ds(it, 1), :], ACT.Square).then_inc(gn_sq.sem, 1)
                with act.Fori(0, PAIRS) as it:
                    act.wait_ge(gn_var.sem, it + 1)
                    nc.scalar.activation(z[:, bass.ds(it + Z_V, 1), :], ps[:, bass.ds(it, 1), 0:T], ACT.Sqrt, bias=eps[:, 1:2]
                                         ).then_inc(gn_root.sem, 1)
                nc.scalar.activation(hhi[:, PAIRS:KD, :], z[:, Z_U:Z_U + HB, :], ACT.Copy).then_inc(y_high.sem, 1)
                for n in range(RING):
                    st.high(act, 0, n)
                with act.Fori(0, PAIRS) as it:
                    act.wait_ge(y_ready.sem, it + 1)
                    nc.scalar.activation(hhi[:, bass.ds(it, 1), :], z[:, bass.ds(it, 1), :], ACT.Copy).then_inc(y_high.sem, 1)
                act.wait_ge(y_split.sem, PAIRS + 1)

                def drain(it, u):
                    act.wait_ge(product_ready.sem, it * RING + product_ready.v + u + 1)
                    nc.scalar.activation(flat(z[:, bass.ds(it * RING + u + OUT_AT, 1), :]),
                                         ps[:, u, 0:T], ACT.Copy)
                    nc.scalar.activation(flat(z[:, bass.ds(it * RING + u + Z_U, 1), :]),
                                         ps[:, u, 0:T], ACT.Square).then_inc(bank_free.sem, 1)

                st.ahead(act, KD, lambda it, n: st.high(act, it, n), drain, started=True)
                act.wait_ge(pe_to_act.sem, pe_to_act.v + 1)
                nc.scalar.activation(rstd[:, :], ps[:, 7, 0:T], ACT.Sqrt, bias=eps[:, 0:1]).then_inc(act_to_dve.sem, 1)

            @block.vector
            def _(dve):
                with dve.Fori(0, PAIRS) as it:
                    dve.wait_ge(gn_mean.sem, it + 1)
                    y = z[:, bass.ds(it, 1), :]
                    nc.vector.tensor_tensor(y, y, ps[:, bass.ds(it, 1), 0:T], ALU.subtract).then_inc(gn_dev.sem, 1)
                with dve.Fori(0, PAIRS) as it:
                    dve.wait_ge(gn_root.sem, it + 1)
                    y, dev_ = z[:, bass.ds(it, 1), :], z[:, bass.ds(it + Z_V, 1), :]
                    nc.vector.reciprocal(dev_, dev_).then_inc(gn_done.sem, 1)
                    dve.wait_ge(gn_done.sem, it * 3 + 1)
                    nc.vector.tensor_tensor(y, y, dev_, ALU.mult).then_inc(gn_done.sem, 1)
                    dve.wait_ge(gn_done.sem, it * 3 + 2)
                    nc.vector.tensor_scalar(y, y, cols[:, bass.ds(it + COLS["ln_x_w"][0], 1)],
                                            cols[:, bass.ds(it + COLS["ln_x_b"][0], 1)], ALU.mult, ALU.add).then_inc(gn_done.sem, 1)
                dve.wait_ge(y_high.sem, 1)
                nc.vector.tensor_tensor(hlo[:, PAIRS:KD, :], z[:, Z_U:Z_U + HB, :], hhi[:, PAIRS:KD, :].bitcast(F32),
                                        ALU.subtract).then_inc(y_split.sem, 1)
                for n in range(RING):
                    st.low(dve, 0, n)
                with dve.Fori(0, PAIRS) as it:
                    dve.wait_ge(y_high.sem, it + 2)
                    nc.vector.tensor_tensor(hlo[:, bass.ds(it, 1), :], z[:, bass.ds(it, 1), :], hhi[:, bass.ds(it, 1), :].bitcast(F32),
                                            ALU.subtract).then_inc(y_split.sem, 1)
                dve.wait_ge(y_split.sem, PAIRS + 1)
                nc.vector.memset(square_sum, 0.0).then_inc(sq_added.sem, 1)

                def add_square(it, u):
                    dve.wait_ge(bank_free.sem, it * RING + bank_free.v + u + 1)
                    dve.wait_ge(sq_added.sem, it * RING + u + 1)
                    nc.vector.tensor_tensor(square_sum, square_sum, flat(z[:, bass.ds(it * RING + u + Z_U, 1), :]), ALU.add
                                            ).then_inc(sq_added.sem, 1)

                st.ahead(dve, KD, lambda it, n: st.low(dve, it, n), add_square, started=True)
                dve.wait_ge(act_to_dve.sem, act_to_dve.v + 1)
                nc.vector.reciprocal(rstd[:, :], rstd[:, :])
            st.close(KD)
            pool_chain.v += PAIRS
            pe_to_act.v += 1
            act_to_dve.v += 1
        if debug is not None and "y" in debug:
            dump("y", (0, 8, z[:, 0:8, :]), (8, 16, z[:, Z_U:Z_U + 8, :]))
        if debug is not None and "o" in debug:
            dump("o", (0, 16, mixed_out))
        add_to_residual(mixed_out, 32, squares=hf)
        if debug is not None and "x2" in debug:
            dump("x2", (0, 16, x[:, :, :]))
        z_scope.close()

        p_scope = ExitStack()
        gates = sb(p_scope, "gates", [P, TILES, SLOTS])
        first = sb(p_scope, "first", [P, TILES, SLOTS])
        second = sb(p_scope, "second", [P, TILES, SLOTS])
        with ExitStack() as q_scope, nc.Block() as block:
            st = Stream(RING, st.raw, st.parts, shared=True)
            h2 = sb(q_scope, "h2", [P, KD, T])
            m2 = Modulate(h2, 48, 64)
            keys = sb(q_scope, "keys", [P, 2 * PKH, NK])
            qs = sb(q_scope, "qs", [P, RING, T])
            score = sb(q_scope, "score", [P, RING, TILES, NK])
            score2 = sb(q_scope, "score2", [P, RING, TILES, NK])
            best = sb(q_scope, "best", [P, 2, TILES, TOPK])
            which = sb(q_scope, "which", [P, 2, TILES, TOPK], U32)
            whichf = sb(q_scope, "whichf", [P, 2, TILES, TOPK])
            cand = sb(q_scope, "cand", [P, TILES, TOPK, TOPK])
            cand2 = sb(q_scope, "cand2", [P, TILES, TOPK * TOPK])
            top = sb(q_scope, "top", [P, TILES, TOPK])
            pos = sb(q_scope, "pos", [P, TILES, TOPK], U32)
            half_pos = sb(q_scope, "half_pos", [P, 2, TILES, TOPK], U32)
            half_posf = sb(q_scope, "half_posf", [P, 2, TILES, TOPK])
            onehot = sb(q_scope, "onehot", [P, 2, TILES * TOPK, TOPK])
            keys_sem = sem("keys_landed")
            scored, score_ready, score_used = sem("scored"), sem("score_ready"), sem("score_used")
            settled = sem("settled")
            positions, picked = sem("positions"), sem("picked")

            @block.sync
            def _(sp):
                sp.dma_start(keys[:, :, :].rearrange("p (h s) k -> p h s k", s=2), keys_t).then_inc(keys_sem.sem, 16)
                st.load(sp, 2 * PKH, w_query)

            @block.tensor
            def _(pe):
                pe.wait_ge(keys_sem.sem, 16)

                def head(it, first=False):
                    for u in range(RING):
                        st.product(pe, it, u, ps[:, u, 0:T], dve_to_pe if first and u == 0 else None)
                    for u in range(RING):
                        pe.wait_ge(bank_free.sem, it * RING + bank_free.v + u + 1)
                        pe.wait_ge(score_ready.sem, it * RING + u + 1)
                        for tile in range(TILES):
                            last = pe.matmul(ps[:, 4 + u, tile * P:(tile + 1) * P], qs[:, u, tile * P:(tile + 1) * P],
                                             keys[:, bass.ds(it * 2 + u, 1), :].rearrange("p o k -> p (o k)"),
                                             start=True, stop=True)
                        last.then_inc(scored.sem, 1)

                head(0, first=True)
                with pe.Fori(1, PKH) as it:
                    head(it)

            @block.scalar
            def _(act):
                act.sem_inc(score_ready.sem, RING)
                act.sem_inc(score_used.sem, 1)

                def drain(it, u):
                    act.wait_ge(product_ready.sem, it * RING + product_ready.v + u + 1)
                    nc.scalar.activation(qs[:, u, :], ps[:, u, 0:T], ACT.Copy).then_inc(bank_free.sem, 1)

                def scores(it):
                    for u in range(RING):
                        act.wait_ge(scored.sem, it * RING + u + 1)
                        act.wait_ge(score_used.sem, it + 1)
                        nc.scalar.activation(score[:, u, :, :].rearrange("p t k -> p (t k)"), ps[:, 4 + u, 0:T], ACT.Copy
                                             ).then_inc(score_ready.sem, 1)

                m2.scalar(act, lambda it, n: st.high(act, it, n))
                with act.Fori(0, PKH - 1) as it:
                    for n in range(RING):
                        drain(it, n)
                        st.high(act, it, n + RING)
                    scores(it)
                for n in range(RING):
                    drain(PKH - 1, n)
                scores(PKH - 1)

            @block.gpsimd
            def _(pool):
                def pick(it):
                    for s in range(2):
                        pool.wait_ge(positions.sem, it * 2 + s + 1)
                        for tile in range(TILES):
                            part = onehot[:, s, tile * TOPK:(tile + 1) * TOPK, :]
                            nc.gpsimd.tensor_tensor(
                                part, part, whichf[:, s, tile:tile + 1, :].to_broadcast([P, TOPK, TOPK]), ALU.mult
                                ).then_inc(picked.sem, 1)

                st.low(pool, 0, 1, nc.gpsimd)
                st.low(pool, 0, 3, nc.gpsimd)
                with pool.Fori(0, PKH - 2) as it:
                    pick(it)
                    st.low(pool, it, 5, nc.gpsimd)
                pick(PKH - 2)
                pick(PKH - 1)

            @block.vector
            def _(dve):
                def best16(ch, srcs, spares, values, indices):
                    def settle():
                        ch.wait()
                        dve.sem_inc(settled.sem, 1)

                    n = len(srcs)
                    settle()
                    for i in range(n):
                        ch.done(nc.vector.max(values[i][:, 0:8], srcs[i]))
                    settle()
                    for i in range(n):
                        ch.done(nc.vector.max_index(indices[i][:, 0:8], values[i][:, 0:8], srcs[i]))
                    for i in range(n):
                        ch.done(nc.vector.match_replace(spares[i], values[i][:, 0:8], srcs[i], NEG))
                    settle()
                    for i in range(n):
                        ch.done(nc.vector.max(values[i][:, 8:16], spares[i]))
                    settle()
                    for i in range(n):
                        ch.done(nc.vector.max_index(indices[i][:, 8:16], values[i][:, 8:16], spares[i]))
                    ch.wait()

                def choose(it, ch):
                    dve.wait_ge(score_ready.sem, it * RING + 2 * RING)
                    dve.sem_inc(settled.sem, 1)
                    seg = [(u, tile) for u in range(2) for tile in range(TILES)]
                    best16(ch, [score[:, u, t_, :] for u, t_ in seg], [score2[:, u, t_, :] for u, t_ in seg],
                           [best[:, u, t_, :] for u, t_ in seg], [which[:, u, t_, :] for u, t_ in seg])
                    dve.sem_inc(score_used.sem, 1)
                    ch.done(nc.vector.tensor_copy(whichf[:, :, :, :], which[:, :, :, :]))
                    for tile in range(TILES):
                        ch.done(nc.vector.tensor_tensor(
                            cand[:, tile], best[:, 0, tile, :].rearrange("p (a o) -> p a o", o=1).to_broadcast([P, TOPK, TOPK]),
                            best[:, 1, tile:tile + 1, :].to_broadcast([P, TOPK, TOPK]), ALU.add))
                    ch.wait()
                    best16(ch, [cand[:, t_].rearrange("p a b -> p (a b)") for t_ in range(TILES)],
                           [cand2[:, t_, :] for t_ in range(TILES)], [top[:, t_, :] for t_ in range(TILES)],
                           [pos[:, t_, :] for t_ in range(TILES)])
                    ch.done(nc.vector.tensor_scalar(half_pos[:, 0], pos[:, :, :], 4, None, ALU.logical_shift_right))
                    ch.link(nc.vector.tensor_scalar(half_pos[:, 1], pos[:, :, :], 15, None, ALU.bitwise_and))
                    ch.link(nc.vector.tensor_copy(half_posf[:, :, :, :], half_pos[:, :, :, :]))
                    for s in range(2):
                        nc.vector.tensor_tensor(
                            onehot[:, s], half_posf[:, s].rearrange("p t (k o) -> p (t k) o", o=1).to_broadcast([P, TILES * TOPK, TOPK]),
                            table("iota")[:, 0:TOPK].rearrange("p (o k) -> p o k", o=1).to_broadcast([P, TILES * TOPK, TOPK]),
                            ALU.is_equal).then_inc(positions.sem, 1)
                    ch.done(nc.vector.tensor_tensor(gates[:, :, bass.ds(it * TOPK, TOPK)], top[:, :, :],
                                                    top[:, :, 0:1].to_broadcast([P, TILES, TOPK]), ALU.subtract))

                def select(it, ch):
                    for s, dst in enumerate((first, second)):
                        dve.wait_ge(picked.sem, it * 2 * TILES + TILES * (s + 1))
                        ch.done(nc.vector.tensor_reduce(dst[:, :, bass.ds(it * TOPK, TOPK)],
                                                        onehot[:, s].rearrange("p (t k) j -> p t k j", t=TILES), AX.X, ALU.add))
                    ch.wait()

                m2.vector(dve, lambda it, n: st.low(dve, it, n) if n == 0 else None)
                st.low(dve, 0, 2)
                ch = Chain(dve, dve_chain)
                choose(0, ch)
                ch.close()
                steps = 5 * 6 + 1 + TILES + 5 * TILES + 3 + 1 + 2
                with dve.Fori(0, PKH - 2) as it:
                    ch = Chain(dve, dve_chain, it, steps)
                    st.low(dve, it, 4)
                    select(it, ch)
                    choose(it + 1, ch)
                ch.close(PKH - 2)
                ch = Chain(dve, dve_chain)
                select(PKH - 2, ch)
                choose(PKH - 1, ch)
                select(PKH - 1, ch)
                dve.sem_inc(dve_to_act.sem, 1)
                ch.close()
            st.close(2 * PKH)
            m2.close()
            dve_to_act.v += 1
        EG = 2
        STEPS = NK // EG
        LAG = 4
        u_raw, u_hi, u_lo = raw, whi, wlo
        u_landed = [sem(f"u_landed{e}") for e in range(EG)]
        v_landed = [sem(f"v_landed{e}") for e in range(EG)]
        gate_landed = sem("gate_landed")
        u_high, u_split, v_high, v_split = sem("u_high"), sem("u_split"), sem("v_high"), sem("v_split")
        act_high, act_split, gelu_done, gated_ = sem("act_high"), sem("act_split"), sem("gelu_done"), sem("act_gated")
        acc_zero = sem("acc_zero")
        u_done, sum_done, added = sem("u_done"), sem("sum_done"), sem("added")
        assert EG == RING

        def load_u(sp, g, e):
            sp.dma_start(u_raw[:, e], expert_u[bass.ds(g * EG + e, 1)].rearrange("o p k c -> (o p) k c")
                         ).then_inc(u_landed[e].sem, 16)

        def u_high_part(act, g, e, first=False):
            act.wait_ge(u_landed[e].sem, g * 16 + 16)
            if not first:
                act.wait_ge(u_done.sem, g * EG + (e + 1 - EG))
            nc.scalar.activation(u_hi[:, e], u_raw[:, e], ACT.Copy).then_inc(u_high.sem, 1)

        def u_low_part(dve, g, e):
            dve.wait_ge(u_high.sem, g * EG + (e + 1))
            nc.vector.tensor_tensor(u_lo[:, e], u_raw[:, e], u_hi[:, e].bitcast(F32), ALU.subtract
                                    ).then_inc(u_split.sem, 1)

        def up(pe, g, first=False):
            for e in range(EG):
                pe.wait_ge(u_split.sem, g * EG + (e + 1))
                if e == 0 and not first:
                    pe.wait_ge(gelu_done.sem, g * EG)
                for k in range(KD):
                    pe.matmul(ps[:, e, 0:T], u_hi[:, e, k, :], hhi[:, k, :], start=(k == 0), stop=False)
                    pe.matmul(ps[:, e, 0:T], u_hi[:, e, k, :], hlo[:, k, :], start=False, stop=False)
                    last = pe.matmul(ps[:, e, 0:T], u_lo[:, e, k, :], hhi[:, k, :], start=False, stop=(k == KD - 1))
                last.then_inc(u_done.sem, 1)

        with nc.Block() as block:
            @block.scalar
            def _(act):
                nc.scalar.activation(gates[:, :, :], gates[:, :, :], ACT.Exp).then_inc(act_to_dve.sem, 1)

            @block.vector
            def _(dve):
                ch = Chain(dve, dve_chain)
                dve.wait_ge(act_to_dve.sem, act_to_dve.v + 1)
                g16 = gates[:, :, :].rearrange("p t (h k) -> p (t h) k", k=TOPK)
                total = rstd[:, 0:TILES * PKH]
                ch.link(nc.vector.tensor_reduce(total, g16, AX.X, ALU.add))
                ch.link(nc.vector.reciprocal(total, total))
                ch.link(nc.vector.tensor_tensor(g16, g16, total.rearrange("p (n o) -> p n o", o=1
                                                                          ).to_broadcast([P, TILES * PKH, TOPK]), ALU.mult))
                ch.close()
            act_to_dve.v += 1

        GT = 64
        NG = T // GT
        gate_table = nc.dram_tensor("gate_table", [NG, P, NK, GT], F32, kind="Internal").ap()
        with ExitStack() as t_scope, nc.Block() as block:
            slot = sb(t_scope, "slot", [P, 3, T])
            fa = sb(t_scope, "fa", [P, 8, NK])
            fb = sb(t_scope, "fb", [P, 8, NK])
            stage = sb(t_scope, "stage", [P, 2, NK, GT])
            slots_turned, slots_here = sem("slots_turned"), sem("slots_here")
            fa_mask, fa_act, fa_pool = sem("fa_mask"), sem("fa_act"), sem("fa_pool")
            fb_ready, table_done, staged = sem("fb_ready"), sem("table_done", 8), sem("staged", 4)
            stage_out = [sem("stage_out0", 16), sem("stage_out1", 16)]
            IN = 4

            @block.tensor
            def _(pe):
                pe.sem_inc(table_done.sem, 8)
                for n, src in enumerate((gates, first, second)):
                    for tile in range(TILES):
                        last = pe.transpose(ps[:, 4 + n, tile * P:(tile + 1) * P], src[:, tile, :], table("ident"))
                last.then_inc(slots_turned.sem, 1)
                with pe.Fori(0, NG * IN) as it:
                    for n in range(16):
                        u, bank = n % 8, n // 4
                        pe.wait_ge(fb_ready.sem, it * 4 + n // 4 + 1)
                        if n % 4 < 2:
                            pe.wait_ge(fa_act.sem, it * 8 + 2 * (n // 4) + n % 4 + 1)
                        else:
                            pe.wait_ge(fa_pool.sem, it * 4 + n // 4 + 1)
                        if n % 4 == 0:
                            pe.wait_ge(staged.sem, it * 4 + bank + 1)
                        pe.matmul(ps[:, bank, (n % 4) * NK:(n % 4 + 1) * NK], fa[:, u, :], fb[:, u, :],
                                  start=True, stop=True).then_inc(table_done.sem, 1)
                for bank in range(2):
                    pe.wait_ge(staged.sem, NG * IN * 4 + bank + 1)
                up(pe, 0, first=True)

            @block.vector
            def _(dve):
                for e in range(EG):
                    u_low_part(dve, 0, e)
                dve.wait_ge(slots_here.sem, 1)
                with dve.Fori(0, NG * IN) as it:
                    for n in range(0, 16, 4):
                        dve.wait_ge(table_done.sem, it * 16 + n + 4)
                        for key, f, ready in ((1, fa, fa_mask), (2, fb, fb_ready)):
                            nc.vector.tensor_tensor(
                                f[:, n % 8:n % 8 + 4, :], tab[:, TABLE_NAMES.index("iota"):TABLE_NAMES.index("iota") + 1, :].to_broadcast([P, 4, NK]),
                                slot[:, key, bass.ds(it * 16 + n, 4)].rearrange("p (t o) -> p t o", o=1).to_broadcast([P, 4, NK]),
                                ALU.is_equal).then_inc(ready.sem, 1)

            @block.gpsimd
            def _(pool):
                pool.wait_ge(slots_here.sem, 1)
                with pool.Fori(0, NG * IN) as it:
                    for n in range(0, 16, 4):
                        pool.wait_ge(fa_mask.sem, it * 4 + n // 4 + 1)
                        f = fa[:, n % 8 + 2:n % 8 + 4, :]
                        nc.gpsimd.tensor_tensor(
                            f, f, slot[:, 0, bass.ds(it * 16 + n + 2, 2)].rearrange("p (t o) -> p t o", o=1).to_broadcast([P, 2, NK]),
                            ALU.mult).then_inc(fa_pool.sem, 1)

            @block.scalar
            def _(act):
                act.sem_inc(staged.sem, 4)
                for s in stage_out:
                    act.sem_inc(s.sem, 16)
                for e in range(EG):
                    u_high_part(act, 0, e, first=True)
                act.wait_ge(slots_turned.sem, 1)
                nc.scalar.activation(slot[:, :, :], ps[:, 4:7, 0:T], ACT.Copy).then_inc(slots_here.sem, 1)

                def gate_two(quad):
                    reg, n = quad
                    act.wait_ge(fa_mask.sem, reg + (n + 1))
                    for t in range(2):
                        f = fa[:, (4 * n) % 8 + t, :]
                        nc.scalar.activation(f, f, ACT.Copy, scale=slot[:, 0, bass.ds(reg * 4 + (4 * n + t), 1)]
                                             ).then_inc(fa_act.sem, 1)

                def copies(pair, s, q, last=False):
                    reg = pair * (2 * IN * 4) + q * 4
                    for n in range(4):
                        if not (last and n == 3):
                            gate_two((reg, s * IN * 4 + n + 1))
                        act.wait_ge(table_done.sem, reg * 4 + (s * IN * 16 + 8 + 4 * n + 4))
                        nc.scalar.activation(stage[:, s, :, bass.ds(q * 16 + 4 * n, 4)],
                                             ps[:, n, :].rearrange("p (t i) -> p i t", t=4),
                                             ACT.Copy).then_inc(staged.sem, 1)

                def fill(pair, s, last=False):
                    act.wait_ge(stage_out[s].sem, pair * 16 + 16)
                    with act.Fori(0, IN - 1 if last else IN) as q:
                        copies(pair, s, q)
                    if last:
                        copies(pair, s, IN - 1, last=True)

                gate_two((0, 0))
                with act.Fori(0, NG // 2 - 1) as pair:
                    for s in range(2):
                        fill(pair, s)
                fill(NG // 2 - 1, 0)
                fill(NG // 2 - 1, 1, last=True)

            @block.sync
            def _(sp):
                for e in range(EG):
                    load_u(sp, 0, e)
                for e in range(EG):
                    sp.wait_ge(u_split.sem, e + 1)
                    load_u(sp, 1, e)
                with sp.Fori(0, NG // 2) as pair:
                    for s in range(2):
                        sp.wait_ge(staged.sem, pair * 2 * 4 * IN + (s + 1) * 4 * IN + 4)
                        sp.dma_start(gate_table[bass.ds(pair * 2 + s, 1)].rearrange("o p i t -> (o p) i t"),
                                     stage[:, s]).then_inc(stage_out[s].sem, 16)
                for s in range(2):
                    sp.wait_ge(stage_out[s].sem, 16 + 16 * (NG // 2))
        p_scope.close()

        acc_scope = ExitStack()
        acc = sb(acc_scope, "acc", [P, KD, T])
        e_scope = ExitStack()
        v_raw = sb(e_scope, "v_raw", [P, EG, D])
        v_hi = sb(e_scope, "v_hi", [P, EG, D], F32R)
        v_lo = sb(e_scope, "v_lo", [P, EG, D], F32R)
        gate = sb(e_scope, "gate", [P, NG, EG, GT])
        act_f = sb(e_scope, "act_f", [P, EG, T])
        act_hi = sb(e_scope, "act_hi", [P, EG, T], F32R)
        act_lo = sb(e_scope, "act_lo", [P, EG, T], F32R)
        with nc.Block() as block:
            @block.sync
            def _(sp):
                def load_v(g, e):
                    sp.dma_start(v_raw[:, e], expert_v[bass.ds(g * EG + e, 1)].rearrange("o p c -> (o p) c")
                                 ).then_inc(v_landed[e].sem, 16)

                def load_gate(g):
                    sp.dma_start(gate[:, :, :, :].rearrange("p b e t -> p b (e t)"),
                                 gate_table[:, :, bass.ds(g * EG, EG), :].rearrange("b p e t -> p b (e t)")
                                 ).then_inc(gate_landed.sem, 16)

                for e in range(EG):
                    load_v(0, e)
                load_gate(0)

                def step(g, more_u=True):
                    if more_u:
                        for e in range(EG):
                            sp.wait_ge(u_split.sem, g * EG + (EG + e + 1))
                            load_u(sp, g + 2, e)
                    for e in range(EG):
                        sp.wait_ge(v_split.sem, g * EG + (e + 1))
                        load_v(g + 1, e)
                    sp.wait_ge(gated_.sem, g + 1)
                    load_gate(g + 1)

                with sp.Fori(0, STEPS - 2) as it:
                    step(it)
                step(STEPS - 2, more_u=False)

            @block.scalar
            def _(act):
                def gelu(g, e):
                    act.wait_ge(u_done.sem, g * EG + (e + 1))
                    nc.scalar.activation(act_f[:, e, :], ps[:, e, 0:T], ACT.Gelu_apprx_tanh).then_inc(gelu_done.sem, 1)

                for e in range(EG):
                    u_high_part(act, 1, e)
                for e in range(EG):
                    gelu(0, e)

                def step(g, more_u=2):
                    for e in range(EG):
                        act.wait_ge(v_landed[e].sem, g * 16 + 16)
                        if e == 0:
                            act.wait_ge(sum_done.sem, g * KD + KD)
                        nc.scalar.activation(v_hi[:, e], v_raw[:, e], ACT.Copy).then_inc(v_high.sem, 1)
                    act.wait_ge(gated_.sem, g + 1)
                    nc.scalar.activation(act_hi[:, :, :], act_f[:, :, :], ACT.Copy).then_inc(act_high.sem, 1)
                    if more_u == 2:
                        for e in range(EG):
                            u_high_part(act, g + 2, e)
                    if more_u:
                        act.wait_ge(act_split.sem, g + 1)
                        for e in range(EG):
                            gelu(g + 1, e)

                with act.Fori(0, STEPS - 2) as it:
                    step(it)
                step(STEPS - 2, more_u=1)
                step(STEPS - 1, more_u=0)

            @block.gpsimd
            def _(pool):
                nc.gpsimd.memset(acc[:, :, :], 0.0).then_inc(acc_zero.sem, 1)

            @block.vector
            def _(dve):
                for e in range(EG):
                    u_low_part(dve, 1, e)
                dve.wait_ge(acc_zero.sem, 1)
                dve.sem_inc(added.sem, KD)

                def step(g, more_u=True):
                    for e in range(EG):
                        dve.wait_ge(v_high.sem, g * EG + (e + 1))
                        nc.vector.tensor_tensor(v_lo[:, e], v_raw[:, e], v_hi[:, e].bitcast(F32), ALU.subtract
                                                ).then_inc(v_split.sem, 1)
                    dve.wait_ge(gate_landed.sem, g * 16 + 16)
                    dve.wait_ge(gelu_done.sem, g * EG + EG)
                    for e in range(EG):
                        a = act_f[:, e, :].rearrange("p (b t) -> p b t", b=NG)
                        last = nc.vector.tensor_tensor(a, a, gate[:, :, e, :], ALU.mult)
                    last.then_inc(gated_.sem, 1)
                    dve.wait_ge(act_high.sem, g + 1)
                    nc.vector.tensor_tensor(act_lo[:, :, :], act_f[:, :, :], act_hi[:, :, :].bitcast(F32), ALU.subtract
                                            ).then_inc(act_split.sem, 1)
                    for d in range(KD):
                        dve.wait_ge(sum_done.sem, g * KD + (KD + d + 1))
                        dve.wait_ge(added.sem, g * KD + (d + 1))
                        nc.vector.tensor_tensor(acc[:, d, :], acc[:, d, :], ps[:, 2 + d % LAG, 0:T], ALU.add
                                                ).then_inc(added.sem, 1)
                        if more_u and d in (5, 11):
                            u_low_part(dve, g + 2, d // 6)

                with dve.Fori(0, STEPS - 2) as it:
                    step(it)
                step(STEPS - 2, more_u=False)
                step(STEPS - 1, more_u=False)

            @block.tensor
            def _(pe):
                def down(g):
                    pe.wait_ge(v_split.sem, g * EG + EG)
                    pe.wait_ge(act_split.sem, g + 1)
                    for d in range(KD):
                        pe.wait_ge(added.sem, g * KD + (KD + d + 1 - LAG))
                        bank, cols_ = ps[:, 2 + d % LAG, 0:T], slice(d * P, (d + 1) * P)
                        for e in range(EG):
                            pe.matmul(bank, v_hi[:, e, cols_], act_hi[:, e, :], start=(e == 0), stop=False)
                            pe.matmul(bank, v_hi[:, e, cols_], act_lo[:, e, :], start=False, stop=False)
                            last = pe.matmul(bank, v_lo[:, e, cols_], act_hi[:, e, :], start=False, stop=(e == EG - 1))
                        last.then_inc(sum_done.sem, 1)

                pe.sem_inc(sum_done.sem, KD)
                with pe.Fori(0, STEPS - 1) as it:
                    up(pe, it + 1)
                    down(it)
                down(STEPS - 1)

        e_scope.close()
        w_scope.close()
        with ExitStack() as n_scope:
            sq = sb(n_scope, "sq", [P, KD, T])
            if debug is not None and "peer" in debug:
                dump("peer", (0, 16, acc[:, :, :]))
            square_root_of_mean(acc, sq)
            add_to_residual(acc, 80, out=y_out)
        acc_scope.close()
        h_scope.close()


def lay_out(i):
    def chan(a):
        return np.ascontiguousarray(np.asarray(a).reshape(-1, P).T)

    def blocks(w):
        w = np.asarray(w)
        return np.ascontiguousarray(w.reshape(KD, P, -1, P).transpose(2, 1, 0, 3))

    g = {k: np.asarray(v) for k, v in i.items()}
    xs = np.concatenate([g["x_prompt"][0], g["x_sample"][0]], 0)
    cc = np.stack([g["c_ctx"], g["c"][0]], 0)
    tables = constant_tables()
    out = {
        "x_t": xs.reshape(T, KD, P).transpose(2, 1, 0),
        "c_t": cc.reshape(2, KD, P).transpose(2, 1, 0),
        "cols_in": np.concatenate([chan(g["b_ada"]), chan(g["g_pre1"]), chan(g["g_post1"]), chan(g["g_pre2"]),
                                   chan(g["g_post2"]), chan(g["mu_shift"]), chan(g["w0"]), chan(g["a0"]),
                                   chan(g["k_k"]), chan(g["k_a"]), chan(g["r_k"]), chan(g["ln_x_w"]),
                                   chan(g["ln_x_b"]), chan(g["ln_v_w"]), chan(g["ln_v_b"])], 1),
        "tables_in": np.stack([tables[n] for n in TABLE_NAMES], 1),
        "w_ada": g["w_ada"][0].reshape(4, 4, P, 24, 512).transpose(3, 0, 2, 1, 4).reshape(96, P, KD, P),
        "w_in": blocks(g["w_in"][0]),
        "w2a2": np.stack([g["w2"][0].reshape(2 * 64, PAIRS, P), g["a2"][0].reshape(2 * 64, PAIRS, P)], 0).transpose(2, 1, 0, 3),
        "w_s": g["w_s"][0].transpose(2, 0, 1),
        "b_s": g["b_s"][0].reshape(1, HB, P),
        "state_t": np.stack([g["state_fwd"][0, 0], g["state_bwd"][0, 0]], 0)
                     .reshape(2, PAIRS, 2, HEAD, HEAD).transpose(1, 2, 4, 0, 3).reshape(PAIRS, P, 2, HEAD),
        "w_out": blocks(g["w_out"][0]),
        "w_query": blocks(g["w_query"][0]),
        "keys_t": g["sub_keys"][0].transpose(3, 1, 0, 2),
        "expert_u": g["expert_u"][0].reshape(NK, NK, KD, P).transpose(1, 3, 2, 0),
        "expert_v": g["expert_v"][0].reshape(NK, NK, D).transpose(1, 0, 2),
    }
    return {k: np.ascontiguousarray(v) for k, v in out.items()}


OUTS = {"y_out": ((P, KD, T), "float32"), "state_out": ((PAIRS, P, 2, HEAD), "float32")}


def kernel(**inputs):
    import concourse.bacc as bacc
    from concourse.bass_utils import run_bass_kernel_spmd

    nc = bacc.Bacc("TRN2", target_bir_lowering=False, num_devices=1, dynamic_dma_scratch_size=2048)
    arrays = lay_out(inputs)
    args = {n: nc.dram_tensor(n, a.shape, mybir.dt.from_np(a.dtype), kind="ExternalInput").ap()
            for n, a in arrays.items()}
    args |= {n: nc.dram_tensor(n, s, mybir.dt.from_np(np.dtype(d)), kind="ExternalOutput").ap()
             for n, (s, d) in OUTS.items()}
    build_program(nc, **args)
    got = run_bass_kernel_spmd(nc, [arrays], core_ids=[0]).results[0]
    y = np.asarray(got["y_out"]).transpose(2, 1, 0).reshape(T, D)
    st = np.asarray(got["state_out"]).reshape(PAIRS, 2, HEAD, 2, HEAD).transpose(3, 0, 1, 4, 2)
    st = st.reshape(2, 1, 1, 2 * PAIRS, HEAD, HEAD)
    return (np.ascontiguousarray(y[None, :CTX]), np.ascontiguousarray(y[None, CTX:]),
            np.ascontiguousarray(st[0]), np.ascontiguousarray(st[1]))
```
